# Optimizing a Trainium2 kernel written in Bass

```python
import math, functools
import jax, jax.numpy as jnp
from jax import lax
import numpy as np

D_MODEL = 1024
BATCH = 1
SEQ = 1024
DEPTH = 2
DEC_BATCH = 8
DEC_SEQ = 16
PAST_LEN = 1024

CHUNK = 64
Q_BLOCK = 128
N_A = DEPTH // 2
N_B = DEPTH - N_A
A_HEADS = D_MODEL // 128
A_HEAD_DIM = 64
A_V_DIM = 2 * A_HEAD_DIM
A_QK = A_HEADS * 2 * A_HEAD_DIM
A_V = A_HEADS * A_V_DIM
B_HEADS = D_MODEL // 64
B_HEAD_DIM = 64
B_QK = B_HEADS * B_HEAD_DIM
D_FF = 4 * D_MODEL
ROPE_THETA = 10000.0
EPS = 1e-6
NEG = -1e30

kernel_name = 'yoco_diffattn_fox_stream_step'

def rmsnorm(x, g):
    xf = x.astype(jnp.float32)
    y = xf * lax.rsqrt(jnp.mean(xf * xf, axis=-1, keepdims=True) + EPS)
    return (y * g.astype(jnp.float32)).astype(x.dtype)

def rope(x, pos):
    half = x.shape[-1] // 2
    inv = jnp.power(ROPE_THETA, -jnp.arange(half, dtype=jnp.float32) / half)
    ang = pos.astype(jnp.float32)[:, None] * inv[None, :]
    cos = jnp.cos(ang)[None, :, None, :]
    sin = jnp.sin(ang)[None, :, None, :]
    xf = x.astype(jnp.float32)
    x1, x2 = xf[..., :half], xf[..., half:]
    return jnp.concatenate([x1 * cos - x2 * sin, x2 * cos + x1 * sin], axis=-1).astype(x.dtype)

def to_blocks(a):
    b, s = a.shape[:2]
    return jnp.moveaxis(a.reshape(b, s // Q_BLOCK, Q_BLOCK, *a.shape[2:]), 1, 0)

def from_blocks(a):
    nb, b, qb = a.shape[:3]
    return jnp.moveaxis(a, 0, 1).reshape(b, nb * qb, *a.shape[3:])

def sweep(attend, q_args, q_pos, blocked):
    if not blocked:
        return attend(*q_args, q_pos)
    qb = tuple(to_blocks(a) for a in q_args)
    pb = q_pos.reshape(-1, Q_BLOCK)
    out = lax.map(lambda t: attend(*t[0], t[1]), (qb, pb))
    return from_blocks(out)

def diff_attend(q, q_pos, k, v, k_pos, lam):
    s = jnp.einsum('bqhmd,bkhmd->bhmqk', q, k, preferred_element_type=jnp.float32)
    s = s * (A_HEAD_DIM ** -0.5)
    mask = (k_pos[None, :] // CHUNK) <= (q_pos[:, None] // CHUNK)
    p = jax.nn.softmax(jnp.where(mask, s, NEG), axis=-1)
    w = p[:, :, 0] - lam * p[:, :, 1]
    return jnp.einsum('bhqk,bkhe->bqhe', w.astype(v.dtype), v)

def fox_attend(q, cq, q_pos, k, v, ck, k_pos):
    s = jnp.einsum('bqhd,bkhd->bhqk', q, k, preferred_element_type=jnp.float32)
    s = s * (B_HEAD_DIM ** -0.5)
    bias = jnp.transpose(cq, (0, 2, 1))[..., :, None] - jnp.transpose(ck, (0, 2, 1))[..., None, :]
    mask = k_pos[None, :] <= q_pos[:, None]
    p = jax.nn.softmax(jnp.where(mask, s + bias, NEG), axis=-1)
    return jnp.einsum('bhqk,bkhd->bqhd', p.astype(v.dtype), v)

def sq_relu_mlp(x, w_up, w_down):
    return jnp.square(jax.nn.relu(x @ w_up)) @ w_down

def _trunk(x, past_len, c_ak, c_av, c_bk, c_bv, c_bf, weights, blocked):
    (norm_attn, norm_mlp, w_qkv_a, lambda_q1, lambda_k1, lambda_q2, lambda_k2, subln_a, w_o_a,
     norm_kv, w_kvf, b_f, w_q_b, w_o_b, w_up, w_down, norm_final) = weights
    b, t, _ = x.shape
    q_pos = past_len + jnp.arange(t, dtype=jnp.int32)
    k_pos = jnp.arange(past_len + t, dtype=jnp.int32)
    h = x
    a_k_rows, a_v_rows = [], []
    shared = None
    for l in range(DEPTH):
        hn = rmsnorm(h, norm_attn[l])
        if l < N_A:
            i = l
            qkv = hn @ w_qkv_a[i]
            q, k, v = jnp.split(qkv, [A_QK, 2 * A_QK], axis=-1)
            q = rope(q.reshape(b, t, 2 * A_HEADS, A_HEAD_DIM), q_pos).reshape(b, t, A_HEADS, 2, A_HEAD_DIM)
            k = rope(k.reshape(b, t, 2 * A_HEADS, A_HEAD_DIM), q_pos)
            v = v.reshape(b, t, A_HEADS, A_V_DIM)
            a_k_rows.append(k)
            a_v_rows.append(v)
            k_all = k if c_ak is None else jnp.concatenate([c_ak[i], k], axis=1)
            v_all = v if c_av is None else jnp.concatenate([c_av[i], v], axis=1)
            k_all = k_all.reshape(b, -1, A_HEADS, 2, A_HEAD_DIM)
            lam_init = 0.8 - 0.6 * math.exp(-0.3 * i)
            lam = (jnp.exp(jnp.sum(lambda_q1[i].astype(jnp.float32) * lambda_k1[i].astype(jnp.float32)))
                   - jnp.exp(jnp.sum(lambda_q2[i].astype(jnp.float32) * lambda_k2[i].astype(jnp.float32)))
                   + lam_init)
            attend = functools.partial(diff_attend, k=k_all, v=v_all, k_pos=k_pos, lam=lam)
            o = sweep(lambda qq, pp: attend(qq, pp), (q,), q_pos, blocked)
            o = rmsnorm(o, subln_a[i]) * (1.0 - lam_init)
            mix = o.reshape(b, t, A_V) @ w_o_a[i]
        else:
            j = l - N_A
            if shared is None:
                kvf = rmsnorm(h, norm_kv) @ w_kvf
                bk, bv, fl = jnp.split(kvf, [B_QK, 2 * B_QK], axis=-1)
                bk = bk.reshape(b, t, B_HEADS, B_HEAD_DIM)
                bv = bv.reshape(b, t, B_HEADS, B_HEAD_DIM)
                blogf = jax.nn.log_sigmoid(fl.astype(jnp.float32) + b_f.astype(jnp.float32)).astype(x.dtype)
                kb_all = bk if c_bk is None else jnp.concatenate([c_bk, bk], axis=1)
                vb_all = bv if c_bv is None else jnp.concatenate([c_bv, bv], axis=1)
                f_all = blogf if c_bf is None else jnp.concatenate([c_bf, blogf], axis=1)
                c_all = jnp.cumsum(f_all.astype(jnp.float32), axis=1)
                shared = (bk, bv, blogf, kb_all, vb_all, c_all)
            bk, bv, blogf, kb_all, vb_all, c_all = shared
            qb = (hn @ w_q_b[j]).reshape(b, t, B_HEADS, B_HEAD_DIM)
            cq = c_all[:, past_len:]
            attend = functools.partial(fox_attend, k=kb_all, v=vb_all, ck=c_all, k_pos=k_pos)
            o = sweep(lambda qq, cc, pp: attend(qq, cc, pp), (qb, cq), q_pos, blocked)
            mix = o.reshape(b, t, B_QK) @ w_o_b[j]
        h = h + mix
        h = h + sq_relu_mlp(rmsnorm(h, norm_mlp[l]), w_up[l], w_down[l])
    bk, bv, blogf = shared[0], shared[1], shared[2]
    return rmsnorm(h, norm_final), jnp.stack(a_k_rows), jnp.stack(a_v_rows), bk, bv, blogf

def setup_inputs(seed: int = 0) -> dict:
    key = jax.random.key(seed)
    ks = jax.random.split(key, 32)
    f32 = jnp.float32
    D = D_MODEL

    def nrm(k, shape, scale):
        return jax.random.normal(k, shape, f32) * scale

    x_prompt = nrm(ks[0], (BATCH, SEQ, D), 1.0)
    x_sample = nrm(ks[1], (DEC_BATCH, DEC_SEQ, D), 1.0)
    cache_a_k = nrm(ks[2], (N_A, DEC_BATCH, PAST_LEN, 2 * A_HEADS, A_HEAD_DIM), 1.0)
    cache_a_v = nrm(ks[3], (N_A, DEC_BATCH, PAST_LEN, A_HEADS, A_V_DIM), 1.0)
    cache_b_k = nrm(ks[4], (DEC_BATCH, PAST_LEN, B_HEADS, B_HEAD_DIM), 1.0)
    cache_b_v = nrm(ks[5], (DEC_BATCH, PAST_LEN, B_HEADS, B_HEAD_DIM), 1.0)
    cache_b_logf = jax.nn.log_sigmoid(
        jax.random.uniform(ks[6], (DEC_BATCH, PAST_LEN, B_HEADS), f32, 1.0, 5.0)
        + nrm(ks[7], (DEC_BATCH, PAST_LEN, B_HEADS), 1.0))
    norm_attn = 1.0 + nrm(ks[8], (DEPTH, D), 0.02)
    norm_mlp = 1.0 + nrm(ks[9], (DEPTH, D), 0.02)
    w_qkv_a = nrm(ks[10], (N_A, D, 2 * A_QK + A_V), D ** -0.5)
    lambda_q1 = nrm(ks[11], (N_A, A_HEAD_DIM), 0.1)
    lambda_k1 = nrm(ks[12], (N_A, A_HEAD_DIM), 0.1)
    lambda_q2 = nrm(ks[13], (N_A, A_HEAD_DIM), 0.1)
    lambda_k2 = nrm(ks[14], (N_A, A_HEAD_DIM), 0.1)
    subln_a = 1.0 + nrm(ks[15], (N_A, A_V_DIM), 0.02)
    w_o_a = nrm(ks[16], (N_A, A_V, D), A_V ** -0.5)
    norm_kv = 1.0 + nrm(ks[17], (D,), 0.02)
    w_kvf = nrm(ks[18], (D, 2 * B_QK + B_HEADS), D ** -0.5)
    b_f = jax.random.uniform(ks[19], (B_HEADS,), f32, 1.0, 5.0)
    w_q_b = nrm(ks[20], (N_B, D, B_QK), D ** -0.5)
    w_o_b = nrm(ks[21], (N_B, B_QK, D), B_QK ** -0.5)
    w_up = nrm(ks[22], (DEPTH, D, D_FF), D ** -0.5)
    w_down = nrm(ks[23], (DEPTH, D_FF, D), D_FF ** -0.5)
    norm_final = 1.0 + nrm(ks[24], (D,), 0.02)
    return {'x_prompt': x_prompt, 'x_sample': x_sample,
            'cache_a_k': cache_a_k, 'cache_a_v': cache_a_v,
            'cache_b_k': cache_b_k, 'cache_b_v': cache_b_v, 'cache_b_logf': cache_b_logf,
            'norm_attn': norm_attn, 'norm_mlp': norm_mlp, 'w_qkv_a': w_qkv_a,
            'lambda_q1': lambda_q1, 'lambda_k1': lambda_k1, 'lambda_q2': lambda_q2, 'lambda_k2': lambda_k2,
            'subln_a': subln_a, 'w_o_a': w_o_a, 'norm_kv': norm_kv, 'w_kvf': w_kvf, 'b_f': b_f,
            'w_q_b': w_q_b, 'w_o_b': w_o_b, 'w_up': w_up, 'w_down': w_down, 'norm_final': norm_final}

def reference(x_prompt, x_sample, cache_a_k, cache_a_v, cache_b_k, cache_b_v, cache_b_logf,
              norm_attn, norm_mlp, w_qkv_a, lambda_q1, lambda_k1, lambda_q2, lambda_k2, subln_a, w_o_a,
              norm_kv, w_kvf, b_f, w_q_b, w_o_b, w_up, w_down, norm_final):
    weights = (norm_attn, norm_mlp, w_qkv_a, lambda_q1, lambda_k1, lambda_q2, lambda_k2, subln_a, w_o_a,
               norm_kv, w_kvf, b_f, w_q_b, w_o_b, w_up, w_down, norm_final)
    y_prompt, pak, pav, pbk, pbv, pbf = _trunk(x_prompt, 0, None, None, None, None, None, weights, True)
    past_len = cache_b_k.shape[1]
    y_sample, sak, sav, sbk, sbv, sbf = _trunk(x_sample, past_len, cache_a_k, cache_a_v,
                                              cache_b_k, cache_b_v, cache_b_logf, weights, False)
    return (y_prompt, y_sample, pak, pav, pbk, pbv, pbf, sak, sav, sbk, sbv, sbf)


_drawn_inputs = setup_inputs


def setup_inputs(seed=0):
    import zlib

    import numpy as np

    out = dict(_drawn_inputs(seed))
    spreads = {}
    factors = {'subln_a': 3.915,
     'norm_kv': 22.489,
     'norm_final': 23.312,
     'norm_mlp': 4.727,
     'cache_b_k': 8.0,
     'cache_b_v': 8.0,
     'cache_b_logf': 8.0}
    for name, (base, spread) in spreads.items():
        noise = np.random.default_rng([zlib.crc32(name.encode()), seed]).standard_normal(out[name].shape)
        drawn = base * np.exp(spread * noise) if base else spread * noise
        out[name] = __import__('jax').numpy.asarray(drawn.astype(out[name].dtype))
    for name, factor in factors.items():
        out[name] = (out[name] * factor).astype(out[name].dtype)
    return out
```

```python
from contextlib import ExitStack

import numpy as np

import concourse.bass as bass
from concourse import mybir

F32 = mybir.dt.float32
F32R = mybir.dt.float32r
ALU = mybir.AluOpType
ACT = mybir.ActivationFunctionType
AX = mybir.AxisListType.X

P = 128
D = 1024
KT = D // P
SEQ = 1024
RT = SEQ // P + 1
ROWS = RT * P
NB, NQ = 8, 16
PAST = 1024
CT = PAST // P
NKEY = PAST + P
DFF = 4096
FC = 256
EPS = 1e-6
NEG = -1e30
QS = 64.0 ** -0.5
HALF = 512

C_IDENT, C_BLK, C_TRI = 0, 128, 256
C_WIN = (384, 384 + 240)
C_SELA = 864
C_SELB = C_SELA + 64
C_STREAM = C_SELB + 128
C_FRAME = C_STREAM + 8
C_LAM = C_FRAME + 16
C_ROPE = C_LAM + 2
C_AUX = C_ROPE + RT * 64
NCONST = C_AUX + 2
NHSEL = 16 * 128 + 2 * 128


def constant_tables():
    p = np.arange(P)
    t = np.zeros((P, NCONST), np.float32)
    t[:, C_IDENT:C_IDENT + P] = np.eye(P)
    t[:, C_BLK:C_BLK + P] = np.where(p[None] // 64 <= p[:, None] // 64, 0, NEG)
    t[:, C_TRI:C_TRI + P] = np.where(p[None] <= p[:, None], 0, NEG)
    j, m, q = p // 32, p // 16 % 2, p % 16
    c = np.arange(240)[None] - 112
    t[:, C_WIN[0]:C_WIN[0] + 240] = np.where((c >= 0) & (c < NQ), 0, NEG)
    t[:, C_WIN[1]:C_WIN[1] + 240] = np.where((c >= 0) & (c <= q[:, None]), 0, NEG)
    for a in range(4):
        for f in range(NQ):
            t[:, C_SELA + a * 16 + f] = (j == a) & (q == f)
            for s in range(2):
                t[:, C_SELB + (a * 2 + s) * 16 + f] = (j == a) & (q == f) & (m == s)
    for b in range(8):
        t[:, C_STREAM + b] = p // 16 == b
    for f in range(NQ):
        t[:, C_FRAME + f] = q == f
    t[:, C_LAM] = m == 0
    t[:, C_LAM + 1] = -(m == 1).astype(np.float32)
    t[66:68, C_AUX] = 1
    t[64:66, C_AUX + 1] = 1
    inv = np.power(np.float32(10000.0), -np.arange(32, dtype=np.float32) / np.float32(32))
    for r in range(RT):
        pos = (r * P + p if r < RT - 1 else PAST + q).astype(np.float32)
        ang = (pos[:, None] * inv[None]).astype(np.float32)
        t[:, C_ROPE + r * 64:C_ROPE + r * 64 + 32] = np.cos(ang)
        t[:, C_ROPE + r * 64 + 32:C_ROPE + r * 64 + 64] = np.sin(ang)
    h = np.zeros((16, NHSEL), np.float32)
    for a in range(16):
        h[a, a * 128:(a + 1) * 128] = 1
        for g in range(2):
            h[a, 2048 + g * 128:2048 + (g + 1) * 128] = 2 * (4 * g + j) + m == a
    return t, h


class Core:

    def __init__(self, nc, ctx, hsel):
        self.nc, self.hsel, self.sems = nc, hsel, []
        self.h = ctx.enter_context(nc.sbuf_tensor("h_rows", [P, RT, D], F32))
        self.const = ctx.enter_context(nc.sbuf_tensor("const_sb", [P, NCONST], F32))
        self.ident = self.const[:, C_IDENT:C_IDENT + P]
        self.neglam = ctx.enter_context(nc.sbuf_tensor("neglam", [P, 1], F32))
        self.lamcol = ctx.enter_context(nc.sbuf_tensor("lamcol", [P, 1], F32))

    def clear_semaphores(self):
        self.nc.clear_and_free_semaphores(self.sems)
        self.nc.all_engine_barrier()
        self.sems = []

    def cos_sin(self, r):
        v = self.const[:, C_ROPE + r * 64:C_ROPE + (r + 1) * 64]
        return v[:, 0:32], v[:, 32:64]


def rows_of(prompt, sample, r):
    return prompt[r * P:(r + 1) * P, :] if r < RT - 1 else sample


def scope(core, ctx, tag):
    nc = core.nc

    def sb(name, shape, dt=F32):
        return ctx.enter_context(nc.sbuf_tensor(f"{tag}_{name}", shape, dt))

    def ps(name, shape):
        return ctx.enter_context(nc.psum_tensor(f"{tag}_{name}", shape, F32))

    def sem(name):
        s = nc.alloc_semaphore(name=f"{tag}_{name}")
        core.sems.append(s)
        return s

    return sb, ps, sem




def start_phase(nc, core, x_prompt, x_sample, table, lams):
    with ExitStack() as ctx:
        sb, ps, sem = scope(core, ctx, "st")
        lv = sb("lam_vectors", [P, 4, 64])
        prod = sb("lam_products", [P, 64])
        dots = sb("lam_dots", [P, 2])
        ex = sb("lam_exps", [P, 2])
        s_load, s_dot, s_exp, s_v = sem("load"), sem("dot"), sem("exp"), sem("v")
        block = ctx.enter_context(nc.Block())

        @block.sync
        def _(sp):
            for i, v in enumerate(lams):
                sp.dma_start(lv[:, i, :], v.rearrange("a d -> (a d)").partition_broadcast(P)).then_inc(s_load, 16)
            sp.dma_start(core.const[:], table).then_inc(s_load, 16)
            for r in range(RT):
                sp.dma_start(core.h[:, r, :], rows_of(x_prompt, x_sample, r)).then_inc(s_load, 16)
            sp.wait_ge(s_load, 16 * (5 + RT))

        @block.scalar
        def _(act):
            act.wait_ge(s_dot, 2)
            act.activation(ex[:], dots[:], ACT.Exp).then_inc(s_exp, 1)

        @block.vector
        def _(dve):
            dve.wait_ge(s_load, 16 * (5 + RT))
            for i in range(2):
                if i:
                    dve.wait_ge(s_dot, 1)
                dve.tensor_tensor_reduce(prod[:], lv[:, 2 * i, :], lv[:, 2 * i + 1, :], 1.0, 0.0,
                                         ALU.mult, ALU.add, dots[:, i:i + 1]).then_inc(s_dot, 1)
            dve.wait_ge(s_exp, 1)
            dve.tensor_tensor(core.neglam[:], ex[:, 1:2], ex[:, 0:1], ALU.subtract).then_inc(s_v, 1)
            dve.wait_ge(s_v, 1)
            dve.tensor_scalar(core.neglam[:], core.neglam[:], -0.2, None, ALU.add).then_inc(s_v, 1)
            dve.wait_ge(s_v, 2)
            dve.tensor_scalar(core.lamcol[:], core.const[:, C_LAM + 1:C_LAM + 2], core.neglam[:, 0:1], -1.0,
                              ALU.mult, ALU.mult).then_inc(s_v, 1)
            dve.wait_ge(s_v, 3)
            dve.tensor_tensor(core.lamcol[:], core.lamcol[:], core.const[:, C_LAM:C_LAM + 1],
                              ALU.add).then_inc(s_v, 1)




class Norm:

    def __init__(self, core, sb, ps, sem, kind, gain, src):
        self.core, self.kind, self.gain_src, self.src = core, kind, gain, src
        self.hi = sb("xt_hi", [P, KT, ROWS], F32R)
        self.lo = sb("xt_lo", [P, KT, ROWS], F32R)
        self.xn = sb("xn", [P, 2, D])
        self.stat = sb("stat", [P, RT, 8])
        self.rstd = sb("rstd", [P, RT, 8])
        if kind != "plain":
            self.sq = self.xn
            self.gain = sb("gain", [P, D if kind == "rms" else P])
        self.bank = [ps(f"nt{i}", [P, 4, P]) for i in range(2)]
        self.s_pre, self.s_root = sem("pre"), sem("root")
        self.s_gain, self.s_sq, self.s_rs = sem("gain"), sem("sumsq"), sem("rstd")
        self.s_x = [sem("x0"), sem("x1")]
        self.s_xn, self.s_tp, self.s_hi, self.s_lo = sem("xn"), sem("xT"), sem("xhi"), sem("xlo")

    def sync(self, sp):
        k = self.kind
        if k == "rms":
            sp.dma_start(self.gain[:], self.gain_src.partition_broadcast(P)).then_inc(self.s_gain, 16)
        elif k == "head":
            sp.dma_start(self.gain[:], self.gain_src.partition_broadcast(P)).then_inc(self.s_gain, 16)
        if k != "rms":
            for r in range(RT):
                if r >= 2:
                    sp.wait_ge(self.s_tp, 2 * (r - 1))
                sp.dma_start(self.xn[:, r % 2, :], self.src[r * P:(r + 1) * P, :]).then_inc(self.s_x[r % 2], 16)

    def scalar(self, act):
        core = self.core
        w = 1 if self.kind == "rms" else 8

        def squares(r):
            if r >= 2:
                act.wait_ge(self.s_tp, 2 * (r - 1))
            act.activation(self.xn[:, r % 2, :], core.h[:, r, :], ACT.Square,
                           accum_out=self.stat[:, r, 0:1]).then_inc(self.s_sq, 1)

        def root(r):
            act.wait_ge(self.s_pre, r + 1)
            act.activation(self.rstd[:, r, 0:w], self.rstd[:, r, 0:w], ACT.Sqrt).then_inc(self.s_root, 1)

        def highs(r):
            for g in range(2):
                act.wait_ge(self.s_tp, 2 * r + g + 1)
                act.activation(self.hi[:, 4 * g:4 * g + 4, r * P:(r + 1) * P], self.bank[g][:],
                               ACT.Copy).then_inc(self.s_hi, 1)

        if self.kind == "rms":
            squares(0)
        for r in range(RT):
            if self.kind == "rms" and r >= 1:
                squares(r)
            if self.kind != "plain":
                root(r)
            if r >= 1:
                highs(r - 1)
        highs(RT - 1)

    def vector(self, dve):
        core, k = self.core, self.kind
        w, width = (1, D) if k == "rms" else (8, P)
        n = [0]

        def own(ins):
            n[0] += 1
            ins.then_inc(self.s_rs, 1)
            dve.wait_ge(self.s_rs, n[0])

        def lows(r):
            for g in range(2):
                dve.wait_ge(self.s_hi, 2 * r + g + 1)
                hi = self.hi[:, 4 * g:4 * g + 4, r * P:(r + 1) * P]
                dve.tensor_tensor(self.lo[:, 4 * g:4 * g + 4, r * P:(r + 1) * P], self.bank[g][:],
                                  hi.bitcast(F32), ALU.subtract).then_inc(self.s_lo, 1)

        if k != "plain":
            dve.wait_ge(self.s_gain, 16)
        if k == "head":
            own(dve.tensor_scalar(self.gain[:], self.gain[:], 0.8, None, ALU.mult))
        for r in range(RT):
            if k != "plain":
                x = self.xn[:, r % 2, :]
                xh = x.rearrange("p (h e) -> p h e", e=P)
                if k == "rms":
                    dve.wait_ge(self.s_sq, r + 1)
                else:
                    dve.wait_ge(self.s_x[r % 2], 16 * (r // 2 + 1))
                    own(dve.tensor_tensor(self.sqh[:], x, x, ALU.mult))
                    own(dve.tensor_reduce(self.stat[:, r, :], self.sqh[:].rearrange("p (h e) -> p h e", e=P),
                                          AX, ALU.add))
                own(dve.tensor_scalar(self.stat[:, r, 0:w], self.stat[:, r, 0:w], 1.0 / width, EPS,
                                      ALU.mult, ALU.add))
                dve.reciprocal(self.rstd[:, r, 0:w], self.stat[:, r, 0:w]).then_inc(self.s_pre, 1)
                if r >= 1:
                    lows(r - 1)
                dve.wait_ge(self.s_root, r + 1)
                if k == "rms":
                    dve.scalar_tensor_tensor(x, core.h[:, r, :], self.rstd[:, r, 0:1],
                                             self.gain[:], ALU.mult, ALU.mult).then_inc(self.s_xn, 1)
                else:
                    own(dve.tensor_tensor(xh, xh, self.rstd[:, r, :].unsqueeze(2).to_broadcast([P, 8, P]), ALU.mult))
                    dve.tensor_tensor(xh, xh, self.gain[:].unsqueeze(1).to_broadcast([P, 8, P]),
                                      ALU.mult).then_inc(self.s_xn, 1)
            elif r >= 1:
                lows(r - 1)
        lows(RT - 1)

    def tensor(self, pe):
        for r in range(RT):
            if self.kind == "plain":
                pe.wait_ge(self.s_x[r % 2], 16 * (r // 2 + 1))
            else:
                pe.wait_ge(self.s_xn, r + 1)
            for g in range(2):
                if r:
                    pe.wait_ge(self.s_lo, 2 * r + g - 1)
                for c in range(4):
                    ins = pe.transpose(self.bank[g][:, c, :], self.xn[:, r % 2, (4 * g + c) * P:(4 * g + c + 1) * P],
                                       self.core.ident)
                ins.then_inc(self.s_tp, 1)


def product(pe, out, lhs, rhs, start, stop):
    (lh, ll), (rh, rl) = lhs, rhs
    pe.matmul(out, lh, rh, start=start, stop=False)
    pe.matmul(out, lh, rl, start=False, stop=False)
    return pe.matmul(out, ll, rh, start=False, stop=stop)




def dense_phase(nc, core, tag, kind, gain, src, pieces, forget=None):
    with ExitStack() as ctx:
        sb, ps, sem = scope(core, ctx, tag)
        norm = Norm(core, sb, ps, sem, kind, gain, src)
        if kind == "head":
            norm.sqh = sb("sqh", [P, D])
        raw = sb("w_raw", [P, 4, HALF])
        whi = sb("w_hi", [P, 2, KT, HALF], F32R)
        wlo = sb("w_lo", [P, 2, KT, HALF], F32R)
        stores = any(do != "add" for _, _, do, _ in pieces)
        if stores:
            ob = sb("out_rows", [P, 2, HALF])
        if any(do == "rope" for _, _, do, _ in pieces):
            tc, tsn = sb("times_cos", [P, HALF]), sb("times_sin", [P, HALF])
        NPS = 4
        acc = [ps(f"acc{i}", [P, HALF]) for i in range(NPS)]
        s_raw, s_whi, s_wlo, s_mm, s_ev = sem("raw"), sem("whi"), sem("wlo"), sem("mm"), sem("ev")
        s_rot = sem("rot")
        s_st = [sem("store0"), sem("store1")]
        if forget:
            w_f, b_f, f_prompt, f_sample = forget
            fraw = sb("f_raw", [P, KT, 16])
            fhi, flo = sb("f_hi", [P, KT, 16], F32R), sb("f_lo", [P, KT, 16], F32R)
            fb = sb("f_bias", [P, 16])
            z, e, u, t, m = (sb(f"f_{x}", [P, RT, 16]) for x in "zeutm")
            facc = ps("f_acc", [P, RT, 16])
            s_fl, s_fw, s_fm, s_fv, s_fa, s_fo = sem("fl"), sem("fw"), sem("fm"), sem("fv"), sem("fa"), sem("fo")
        block = ctx.enter_context(nc.Block())
        NT = len(pieces) * RT

        @block.sync
        def _(sp):
            if forget:
                sp.dma_start(fraw[:], w_f.rearrange("(k p) n -> p k n", p=P)).then_inc(s_fl, 16)
                sp.dma_start(fb[:], b_f.partition_broadcast(P)).then_inc(s_fl, 16)
            norm.sync(sp)
            for i, (w, c0, _, _) in enumerate(pieces):
                wv = w[:, c0:c0 + HALF].rearrange("(k p) n -> p k n", p=P)
                for q in range(2):
                    if 2 * i + q >= 1:
                        sp.wait_ge(s_wlo, 2 * i + q)
                    sp.dma_start(raw[:], wv[:, 4 * q:4 * q + 4, :]).then_inc(s_raw, 16)

        @block.gpsimd
        def _(pool):
            if forget:
                pool.wait_ge(s_fl, 32)
                pool.tensor_copy(fhi[:], fraw[:]).then_inc(s_fw, 1)
                pool.wait_ge(s_fw, 1)
                pool.tensor_tensor(flo[:], fraw[:], fhi[:].bitcast(F32), ALU.subtract).then_inc(s_fw, 1)
            for i in range(len(pieces)):
                for q in range(2):
                    n = 2 * i + q
                    pool.wait_ge(s_raw, 16 * (n + 1))
                    if i >= 2 and q == 0:
                        pool.wait_ge(s_mm, RT * (i - 1))
                    hi = whi[:, i % 2, 4 * q:4 * q + 4, :]
                    pool.tensor_copy(hi, raw[:]).then_inc(s_whi, 1)
                    pool.wait_ge(s_whi, n + 1)
                    pool.tensor_tensor(wlo[:, i % 2, 4 * q:4 * q + 4, :], raw[:], hi.bitcast(F32),
                                       ALU.subtract).then_inc(s_wlo, 1)

        @block.tensor
        def _(pe):
            norm.tensor(pe)
            pe.wait_ge(norm.s_lo, 2 * RT)
            if forget:
                pe.wait_ge(s_fw, 2)
                for r in range(RT):
                    for k in range(KT):
                        x = [v[:, k, r * P:(r + 1) * P] for v in (norm.hi, norm.lo)]
                        ins = product(pe, facc[:, r, :], x, (fhi[:, k, :], flo[:, k, :]), k == 0, k == KT - 1)
                ins.then_inc(s_fm, 1)
            for i in range(len(pieces)):
                pe.wait_ge(s_wlo, 2 * i + 2)
                for r in range(RT):
                    n = i * RT + r
                    if n >= NPS:
                        pe.wait_ge(s_ev, n - NPS + 1)
                    for k in range(KT):
                        x = [v[:, k, r * P:(r + 1) * P] for v in (norm.hi, norm.lo)]
                        ins = product(pe, acc[n % NPS][:], x, (whi[:, i % 2, k, :], wlo[:, i % 2, k, :]),
                                      k == 0, k == KT - 1)
                    ins.then_inc(s_mm, 1)

        @block.vector
        def _(dve):
            norm.vector(dve)
            nrot = 0
            if forget:
                dve.wait_ge(s_fm, 1)
                dve.tensor_tensor(z[:], facc[:], fb[:].unsqueeze(1).to_broadcast([P, RT, 16]),
                                  ALU.add).then_inc(s_fv, 1)
                dve.wait_ge(s_fv, 1)
                dve.tensor_scalar(u[:], z[:], -1.0, None, ALU.mult).then_inc(s_fv, 1)
                dve.wait_ge(s_fv, 2)
                dve.tensor_tensor(t[:], z[:], u[:], ALU.min).then_inc(s_fv, 1)
                dve.wait_ge(s_fa, 1)
                dve.tensor_scalar(u[:], e[:], 1.0, None, ALU.add).then_inc(s_fv, 1)
                dve.wait_ge(s_fa, 2)
                dve.tensor_scalar(m[:], u[:], 1.0, None, ALU.is_equal).then_inc(s_fv, 1)
                dve.tensor_scalar(u[:], u[:], -1.0, None, ALU.add).then_inc(s_fv, 1)
                dve.wait_ge(s_fv, 6)
                dve.tensor_tensor(u[:], u[:], m[:], ALU.add).then_inc(s_fv, 1)
                dve.tensor_tensor(t[:], t[:], m[:], ALU.add).then_inc(s_fv, 1)
                dve.wait_ge(s_fv, 8)
                dve.tensor_tensor(t[:], t[:], e[:], ALU.mult).then_inc(s_fv, 1)
                dve.reciprocal(m[:], u[:]).then_inc(s_fv, 1)
                dve.wait_ge(s_fv, 10)
                dve.tensor_tensor(t[:], t[:], m[:], ALU.mult).then_inc(s_fv, 1)
                dve.tensor_scalar(z[:], z[:], 0.0, None, ALU.min).then_inc(s_fv, 1)
                dve.wait_ge(s_fv, 12)
                dve.tensor_tensor(z[:], z[:], t[:], ALU.subtract).then_inc(s_fv, 1)
            for i, (_, c0, do, dst) in enumerate(pieces):
                for r in range(RT):
                    n = i * RT + r
                    dve.wait_ge(s_mm, n + 1)
                    src_ = acc[n % NPS][:]
                    if do == "add":
                        hc = core.h[:, r, dst:dst + HALF]
                        dve.tensor_tensor(hc, hc, src_, ALU.add).then_inc(s_ev, 1)
                        continue
                    if n >= 2:
                        dve.wait_ge(s_st[n % 2], 16 * (n // 2))
                    o = ob[:, n % 2, :]
                    if do == "store":
                        dve.tensor_copy(o, src_).then_inc(s_ev, 1)
                        continue
                    v = src_.rearrange("p (h s e) -> p h s e", s=2, e=32)
                    cos, sin = (x.unsqueeze(1).unsqueeze(1).to_broadcast([P, 8, 2, 32]) for x in core.cos_sin(r))
                    if nrot:
                        dve.wait_ge(s_ev, n)
                    tcv = tc[:].rearrange("p (h s e) -> p h s e", s=2, e=32)
                    tsv = tsn[:].rearrange("p (h s e) -> p h s e", s=2, e=32)
                    dve.tensor_tensor(tcv, v, cos, ALU.mult).then_inc(s_rot, 1)
                    dve.tensor_tensor(tsv, v, sin, ALU.mult).then_inc(s_rot, 1)
                    nrot += 2
                    dve.wait_ge(s_rot, nrot)
                    ov = o.rearrange("p (h s e) -> p h s e", s=2, e=32)
                    dve.tensor_tensor(ov[:, :, 0, :], tcv[:, :, 0, :], tsv[:, :, 1, :], ALU.subtract).then_inc(s_rot, 1)
                    nrot += 1
                    dve.wait_ge(s_rot, nrot)
                    dve.tensor_tensor(ov[:, :, 1, :], tcv[:, :, 1, :], tsv[:, :, 0, :], ALU.add).then_inc(s_ev, 1)

        @block.scalar
        def _(act):
            norm.scalar(act)
            if forget:
                act.wait_ge(s_fv, 3)
                act.activation(e[:], t[:], ACT.Exp).then_inc(s_fa, 1)
                act.wait_ge(s_fv, 4)
                act.activation(t[:], u[:], ACT.Ln).then_inc(s_fa, 1)
                act.wait_ge(s_fv, 13)
                act.dma_start(f_prompt.rearrange("(r p) h -> p r h", p=P), z[:, 0:RT - 1, :]).then_inc(s_fo, 16)
                act.dma_start(f_sample, z[:, RT - 1, :]).then_inc(s_fo, 16)
            if stores:
                for i, (_, _, do, dst) in enumerate(pieces):
                    prompt, sample, d0 = dst
                    for r in range(RT):
                        n = i * RT + r
                        act.wait_ge(s_ev, n + 1)
                        act.dma_start(rows_of(prompt, sample, r)[:, d0:d0 + HALF],
                                      ob[:, n % 2, :]).then_inc(s_st[n % 2], 16)
                for k in range(2):
                    act.wait_ge(s_st[k], 16 * ((NT - k + 1) // 2))
            if forget:
                act.wait_ge(s_fo, 32)




def mlp_phase(nc, core, tag, gain, w_up, w_down):
    with ExitStack() as ctx:
        sb, ps, sem = scope(core, ctx, tag)
        norm = Norm(core, sb, ps, sem, "rms", gain, None)
        NF, RG = FC // P, 3
        GW = ROWS // RG
        up_raw, dn_raw = sb("up_raw", [P, KT, FC]), sb("dn_raw", [P, NF, D])
        up_hi, up_lo = sb("up_hi", [P, KT, FC], F32R), sb("up_lo", [P, KT, FC], F32R)
        dn_hi, dn_lo = sb("dn_hi", [P, NF, D], F32R), sb("dn_lo", [P, NF, D], F32R)
        hid_hi, hid_lo = sb("hid_hi", [P, NF, ROWS], F32R), sb("hid_lo", [P, NF, ROWS], F32R)
        rl, sq = sb("relu", [P, 2, GW]), sb("relu2", [P, 2, GW])
        ups = [ps(f"up{i}", [P, HALF]) for i in range(3)]
        dns = [ps(f"dn{i}", [P, HALF]) for i in range(3)]
        s_ur, s_dr, s_uh, s_ul, s_dh, s_dl = (sem(x) for x in ("ur", "dr", "uh", "ul", "dh", "dl"))
        s_um, s_ue, s_sq, s_hh, s_hl, s_dm, s_de = (sem(x) for x in ("um", "ue", "sq", "hh", "hl", "dm", "de"))
        block = ctx.enter_context(nc.Block())
        NU, ND = NF * RG, RT * 2
        STEPS = DFF // FC

        @block.sync
        def _(sp):
            norm.sync(sp)
            with sp.Fori(0, STEPS) as i:
                sp.wait_ge(s_ul, i + 1)
                sp.dma_start(up_raw[:], w_up[:, bass.ts(i, FC)].rearrange("(k p) n -> p k n", p=P)).then_inc(s_ur, 16)
                sp.wait_ge(s_dl, i + 1)
                sp.dma_start(dn_raw[:], w_down[bass.ts(i, FC), :].rearrange("(k p) n -> p k n", p=P)).then_inc(s_dr, 16)

        @block.gpsimd
        def _(pool):
            pool.sem_inc(s_ul, 1)
            pool.sem_inc(s_dl, 1)
            with pool.Fori(0, STEPS) as i:
                pool.wait_ge(s_uh, i + 1)
                pool.tensor_tensor(up_lo[:], up_raw[:], up_hi[:].bitcast(F32), ALU.subtract).then_inc(s_ul, 1)
                pool.wait_ge(s_dh, i + 1)
                pool.tensor_tensor(dn_lo[:], dn_raw[:], dn_hi[:].bitcast(F32), ALU.subtract).then_inc(s_dl, 1)

        @block.tensor
        def _(pe):
            norm.tensor(pe)
            pe.wait_ge(norm.s_lo, 2 * RT)
            pe.sem_inc(s_hl, 3)
            pe.sem_inc(s_de, 3)
            pe.sem_inc(s_um, 1)
            pe.sem_inc(s_dm, 1)
            with pe.Fori(0, STEPS) as i:
                pe.wait_ge(s_ul, i + 2)
                for g in range(RG):
                    for f in range(NF):
                        n = g * NF + f
                        pe.wait_ge(s_hl, i * NU + n + 1)
                        for k in range(KT):
                            w = [v[:, k, f * P:(f + 1) * P] for v in (up_hi, up_lo)]
                            x = [v[:, k, g * GW:(g + 1) * GW] for v in (norm.hi, norm.lo)]
                            ins = product(pe, ups[n % 3][:, 0:GW], w, x, k == 0, k == KT - 1)
                        ins.then_inc(s_um, 1)
                pe.wait_ge(s_dl, i + 2)
                for r in range(RT):
                    if r % 3 == 0:
                        pe.wait_ge(s_hl, i * NU + NF * (r // 3 + 1) + 3)
                    for c in range(2):
                        n = 2 * r + c
                        pe.wait_ge(s_de, i * ND + n + 1)
                        for f in range(NF):
                            x = [v[:, f, r * P:(r + 1) * P] for v in (hid_hi, hid_lo)]
                            w = [v[:, f, c * HALF:(c + 1) * HALF] for v in (dn_hi, dn_lo)]
                            ins = product(pe, dns[n % 3][:], x, w, f == 0, f == NF - 1)
                        ins.then_inc(s_dm, 1)

        @block.scalar
        def _(act):
            norm.scalar(act)
            act.sem_inc(s_sq, 2)

            def up_high(i):
                act.wait_ge(s_ur, i * 16 + 16)
                act.wait_ge(s_um, i * NU + 1)
                act.activation(up_hi[:], up_raw[:], ACT.Copy).then_inc(s_uh, 1)

            def step(i):
                act.wait_ge(s_dr, i * 16 + 16)
                act.wait_ge(s_dm, i * ND + 1)
                act.activation(dn_hi[:], dn_raw[:], ACT.Copy).then_inc(s_dh, 1)
                for n in range(NU):
                    g, f = n // NF, n % NF
                    act.wait_ge(s_um, i * NU + n + 2)
                    act.wait_ge(s_sq, i * NU + n + 1)
                    act.activation(rl[:, n % 2, :], ups[n % 3][:, 0:GW], ACT.Relu).then_inc(s_ue, 1)
                    act.wait_ge(s_sq, i * NU + n + 3)
                    act.activation(hid_hi[:, f, g * GW:(g + 1) * GW], sq[:, n % 2, :], ACT.Copy).then_inc(s_hh, 1)

            up_high(0)
            with act.Fori(0, STEPS - 1) as i:
                step(i)
                up_high(i + 1)
            step(STEPS - 1)

        @block.vector
        def _(dve):
            norm.vector(dve)
            with dve.Fori(0, STEPS) as i:
                def square(n):
                    dve.wait_ge(s_ue, i * NU + n + 1)
                    dve.tensor_tensor(sq[:, n % 2, :], rl[:, n % 2, :], rl[:, n % 2, :], ALU.mult).then_inc(s_sq, 1)

                def low(n):
                    g, f = n // NF, n % NF
                    dve.wait_ge(s_hh, i * NU + n + 1)
                    hi = hid_hi[:, f, g * GW:(g + 1) * GW].bitcast(F32)
                    dve.tensor_tensor(hid_lo[:, f, g * GW:(g + 1) * GW], sq[:, n % 2, :], hi,
                                      ALU.subtract).then_inc(s_hl, 1)

                for n in range(NU):
                    square(n)
                    low(n)
                for n in range(ND):
                    r, c = n // 2, n % 2
                    hc = core.h[:, r, c * HALF:(c + 1) * HALF]
                    dve.wait_ge(s_dm, i * ND + n + 2)
                    dve.tensor_tensor(hc, hc, dns[n % 3][:], ALU.add).then_inc(s_de, 1)




def prompt_attention(nc, core, tag, fox, q_rows, k_rows, v_rows, logf, cum, o_rows):
    with ExitStack() as ctx:
        sb, ps, sem = scope(core, ctx, tag)
        QT, PAIRS, TURNS = SEQ // P, 8, 4
        NM = 2 if fox else 1
        kd, qd = sb("k_dup", [P, QT, 2, 2, 64]), sb("q_dup", [P, QT, 2, 2, 64])
        vr = sb("v_rows", [P, 2, QT, P])
        khi, klo = sb("kT_hi", [P, 2, 2, SEQ], F32R), sb("kT_lo", [P, 2, 2, SEQ], F32R)
        q2 = sb("qT", [P, 2, 2, SEQ], F32R)
        pr = sb("probs", [P, 2, 2, SEQ])
        wT = sb("wT", [P, 2, NM, SEQ])
        ost = sb("o_rows", [P, 2, QT, P])
        nmx, dsum, rinv, fac = (sb(n, [P, 2 * QT]) for n in ("neg_max", "row_sum", "inv_sum", "factor"))
        ident_r, mask_r = sb("ident_r", [P, P], F32R), sb("mask_r", [P, P], F32R)
        S = [ps(f"s{m}", [P, 2, HALF]) for m in range(2)]
        T = [ps(f"t{b}", [P, HALF]) for b in range(2)]
        K = ps("kq", [P, HALF])
        O = ps("o", [P, P])
        s_kt, s_ke = sem("kt"), sem("ke")
        s_kd, s_qd, s_t, s_kh, s_s, s_nm, s_e, s_f, s_w, s_pv, s_oe, s_of, s_c = (
            sem(x) for x in ("kd", "qd", "t", "kh", "s", "nm", "exp", "fac", "w", "pv", "oe", "of", "c"))
        s_vd, s_te, s_od = ([sem(f"{n}{b}") for b in range(2)] for n in ("vd", "te", "od"))
        if fox:
            q2b = sb("qT_aux", [P, 2, 2, SEQ], F32R)
            lf, c = sb("logf", [P, QT, 16]), sb("cum", [16, SEQ])
            cp = sb("cum_parts", [16, 4, SEQ], F32R)
            s_lf, s_cv, s_cd, s_qb = sem("lf"), sem("cv"), sem("cd"), sem("qb")
            s_ax = [sem("ax0"), sem("ax1")]
        block = ctx.enter_context(nc.Block())

        tiles = [QT - 1 - s % QT for s in range(2 * QT)]
        groups = [[(k, min(4, t + 1 - k)) for k in range(0, t + 1, 4)] for t in tiles]

        kq_steps = [[8 * (s // QT) + j for j in ((6, 7) if s % QT == 6 else (s % QT,) if s % QT < 6 else ())]
                    for s in range(2 * QT)]

        w_units, NU = {}, 0
        for s in range(2 * QT):
            for m in range(NM):
                w_units[s, m] = NU
                NU += len(groups[s])

        class Turn:

            def __init__(self, it, last=False):
                self.it, self.last = it, last
                self.w = w_units

            def units(self, n):
                return self.it * NU + n

            def fills(self, n):
                return self.it * (NU // 2) + n // 2

            def kq_of(self, s, m):
                units = [] if self.last and s >= QT else kq_steps[s]
                return units[-1:] if m else units[:-1]

            def has_next(self, s):
                return not (self.last and s == 2 * QT - 1)

        def kq_parts(j):
            j %= 8
            return j < 4, j % 4 // 2, 4 * (j % 2)

        @block.sync
        def _(sp):
            def load_k(p):
                v = k_rows[0:SEQ, bass.ts(p, P)].rearrange("(t p) e -> p t e", p=P)
                for m in range(2):
                    for dup in range(2):
                        sp.dma_start(kd[:, :, m, dup, :], v[:, :, m * 64:m * 64 + 64]).then_inc(s_kd, 16)

            def load_q(p):
                v = q_rows[0:SEQ, bass.ts(p, P)].rearrange("(t p) e -> p t e", p=P)
                for m in range(2):
                    for dup in range(2):
                        sp.dma_start(qd[:, :, m, dup, :], v[:, :, m * 64:m * 64 + 64]).then_inc(s_qd, 16)

            def load_v(p, par):
                sp.dma_start(vr[:, par], v_rows[0:SEQ, bass.ts(p, P)].rearrange(
                    "(t p) e -> p t e", p=P)).then_inc(s_vd[par], 16)

            def load_c(p, par):
                v = cum[bass.ds(p * 2, 2)]
                sp.dma_start(klo[64:66, par].bitcast(F32), v[:, 0:2, :].rearrange("m r k -> r m k")).then_inc(s_ax[par], 16)
                sp.dma_start(q2b[66:68, par].bitcast(F32), v[:, 2:4, :].rearrange("m r k -> r m k")).then_inc(s_ax[par], 16)

            if fox:
                sp.dma_start(lf[:], logf.rearrange("(r p) h -> p r h", p=P)).then_inc(s_lf, 16)
            load_k(0)
            load_q(0)
            load_v(0, 0)
            load_v(1, 1)
            if fox:
                sp.wait_ge(s_cv, 11)
                sp.dma_start(cum[:], cp[:].bitcast(F32)).then_inc(s_cd, 16)
                sp.wait_ge(s_cd, 16)
                load_c(0, 0)
                load_c(1, 1)
            sp.wait_ge(s_kt, 4)
            load_k(1)
            sp.wait_ge(s_kt, 8)
            load_q(1)
            with sp.Fori(0, TURNS - 1) as it:
                for par in range(2):
                    p = it * 2 + (2 + par)
                    sp.wait_ge(s_kt, it * 16 + (8 * par + 12))
                    load_k(p)
                    sp.wait_ge(s_kt, it * 16 + (8 * par + 16))
                    load_q(p)
                    if fox:
                        sp.wait_ge(s_s, it * 32 + 16 * (par + 1))
                        load_c(p, par)
                    sp.wait_ge(s_pv, it * (2 * QT * NM) + QT * NM * (par + 1))
                    load_v(p, par)

        @block.gpsimd
        def _(pool):
            pool.tensor_copy(ident_r[:], core.ident).then_inc(s_c, 1)
            m0 = C_TRI if fox else C_BLK
            pool.tensor_copy(mask_r[:], core.const[:, m0:m0 + P]).then_inc(s_c, 1)

            def store(it, par):
                pool.wait_ge(s_oe, it * (2 * QT) + (QT * (par + 1) + 1))
                pool.dma_start(o_rows[0:SEQ, bass.ts(it * 2 + par, P)].rearrange("(t p) e -> p t e", p=P),
                               ost[:, par]).then_inc(s_od[par], 16)
                pool.wait_ge(s_od[par], it * 16 + 16)
                pool.sem_inc(s_of, 1)

            with pool.Fori(0, TURNS - 1) as it:
                store(it, 0)
                store(it, 1)
            store(TURNS - 1, 0)
            store(TURNS - 1, 1)

        @block.tensor
        def _(pe):
            for s, n in ((s_te[0], 1), (s_te[1], 1), (s_ke, 1), (s_e, 2), (s_oe, 1), (s_of, 2)):
                pe.sem_inc(s, n)
            if fox:
                pe.wait_ge(s_lf, 16)
                for t in range(QT):
                    ins = pe.transpose(S[0][0:16, t // 4, (t % 4) * P:(t % 4 + 1) * P], lf[:, t, :], core.ident)
                ins.then_inc(s_cv, 1)

            def kq_unit(j, done, loaded):
                keys, m, t0 = kq_parts(j)
                src = kd if keys else qd
                if j % 4 == 0:
                    pe.wait_ge(s_kd if keys else s_qd, loaded)
                pe.wait_ge(s_ke, done + 1)
                for x in range(4):
                    ins = pe.transpose(K[:, x * P:(x + 1) * P], src[:, t0 + x, m].rearrange("p a e -> p (a e)"),
                                       core.ident)
                ins.then_inc(s_kt, 1)

            def scores(turn, s, m):
                t, par = tiles[s % (2 * QT)], s // QT % 2
                it = turn.it
                if s % QT == 0 and m == 0:
                    pe.wait_ge(s_ke, it * 16 + (s // QT * 8 + 9))
                    if fox:
                        pe.wait_ge(s_qb, it * 8 + 4 * (s // QT + 1))
                        pe.wait_ge(s_ax[par], it * 32 + (64 if s == 2 * QT else 32))
                n = (t + 1) * P
                pe.wait_ge(s_e, it * 32 + (2 * s + m + 1))
                for k0 in range(0, n, HALF):
                    w = min(HALF, n - k0)
                    last = k0 + w == n
                    out = S[m][:, k0 // HALF, 0:w]
                    pe.matmul(out, q2[:, par, m, t * P:(t + 1) * P], khi[:, par, m, k0:k0 + w],
                              start=True, stop=False)
                    ins = pe.matmul(out, (q2b if fox else q2)[:, par, m, t * P:(t + 1) * P],
                                    klo[:, par, m, k0:k0 + w], start=False, stop=True)
                    if last:
                        ins = pe.matmul(out[:, w - P:w], ident_r[:], mask_r[:], start=False, stop=True,
                                        skip_group_check=True)
                ins.then_inc(s_s, 1)

            def weights(turn, s, m):
                n0, it = turn.w[s, m], turn.it
                if fox:
                    pe.wait_ge(s_e, it * 32 + (2 * s + m + 3))
                else:
                    pe.wait_ge(s_w, it * (2 * QT) + (s + 1))
                for x, (k0, cnt) in enumerate(groups[s]):
                    b = (n0 + x) % 2
                    pe.wait_ge(s_te[b], turn.fills(n0 + x) + 1)
                    for y in range(cnt):
                        ins = pe.transpose(T[b][:, y * P:(y + 1) * P], pr[:, s % 2, m, (k0 + y) * P:(k0 + y + 1) * P],
                                           core.ident)
                    ins.then_inc(s_t, 1)

            def values(turn, s, m):
                t, par, it = tiles[s], s // QT, turn.it
                if m == 0:
                    pe.wait_ge(s_oe, it * (2 * QT) + (s + 1))
                if s % QT == 0 and m == 0:
                    pe.wait_ge(s_vd[par], it * 16 + 16)
                n0 = turn.w[s, m]
                out = O[:, 64 * m:64 * m + 64] if fox else O[:]
                for x, (k0, cnt) in enumerate(groups[s]):
                    pe.wait_ge(s_te[(n0 + x) % 2], turn.fills(n0 + x) + 2)
                    for k in range(k0, k0 + cnt):
                        v = vr[:, par, k, 64 * m:64 * m + 64] if fox else vr[:, par, k, :]
                        ins = pe.matmul(out, wT[:, s % 2, m, k * P:(k + 1) * P], v, start=k == 0, stop=k == t)
                ins.then_inc(s_pv, 1)

            def run(turn):
                for s in range(2 * QT):
                    for m in range(2):
                        if turn.has_next(s):
                            scores(turn, s + 1, m)
                        for j in turn.kq_of(s, m):
                            kq_unit(j, turn.it * 16 + (8 + j), turn.it * 128 + (128 if j < 8 else 192))
                        if fox or m:
                            if s:
                                values(turn, s - 1, m if fox else 0)
                            weights(turn, s, m if fox else 0)
                for m in range(NM):
                    values(turn, 2 * QT - 1, m)

            for j in range(8):
                kq_unit(j, j, 64)
            pe.wait_ge(s_c, 2)
            if fox:
                pe.wait_ge(s_cv, 11)
                pe.wait_ge(s_qb, 4)
                pe.wait_ge(s_ax[0], 32)
            scores(Turn(0), 0, 0)
            scores(Turn(0), 0, 1)
            with pe.Fori(0, TURNS - 1) as it:
                run(Turn(it))
            run(Turn(TURNS - 1, last=True))

        def kq_high(eng, j, done, par):
            keys, m, t0 = kq_parts(j)
            eng.wait_ge(s_kt, done + 1)
            if fox and not keys:
                eng.activation(q2b[0:64, par, m, t0 * P:t0 * P + HALF], K[0:64, :], ACT.Copy,
                               scale=QS).then_inc(s_qb, 1)
            eng.activation((khi if keys else q2)[:, par, m, t0 * P:t0 * P + HALF], K[:], ACT.Copy,
                           scale=1.0 if keys else QS).then_inc(s_kh, 1)

        def kq_low(eng, j, done, par):
            keys, m, t0 = kq_parts(j)
            cols = slice(t0 * P, t0 * P + HALF)
            eng.wait_ge(s_kh, done + 1)
            if keys:
                rows = slice(0, 64) if fox else slice(0, P)
                ins = eng.tensor_tensor(klo[rows, par, m, cols], K[rows, :], khi[rows, par, m, cols].bitcast(F32),
                                        ALU.subtract)
            else:
                q = q2[64:P, par, m, cols]
                ins = eng.scalar_tensor_tensor(q, K[64:P, :], QS, q.bitcast(F32), ALU.mult, ALU.subtract)
            ins.then_inc(s_ke, 1)

        def weights_out(eng, copy, turn, s, m, mine):
            for x, (k0, cnt) in enumerate(groups[s]):
                n = turn.w[s, m] + x
                if mine(n):
                    eng.wait_ge(s_t, turn.units(n) + 1)
                    copy(wT[:, s % 2, m, k0 * P:(k0 + cnt) * P], T[n % 2][:, 0:cnt * P]).then_inc(s_te[n % 2], 1)

        @block.scalar
        def _(act):
            def exp(turn, s, m):
                n, col = (tiles[s % (2 * QT)] + 1) * P, 2 * (s % QT) + m
                act.wait_ge(s_nm, turn.it * 32 + (2 * s + m + 1))
                act.activation(pr[:, s % 2, m, 0:n], S[m][:].rearrange("p a b -> p (a b)")[:, 0:n], ACT.Exp,
                               bias=nmx[:, col:col + 1], accum_out=dsum[:, col:col + 1]).then_inc(s_e, 1)

            def copy(o, x):
                return act.activation(o, x, ACT.Copy)

            def run(turn):
                for s in range(2 * QT):
                    for m in range(2):
                        for j in turn.kq_of(s, m):
                            kq_high(act, j, turn.it * 16 + (8 + j), (j // 8 + 1) % 2)
                        if turn.has_next(s):
                            exp(turn, s + 1, m)
                        if fox or m:
                            weights_out(act, copy, turn, s, m if fox else 0, lambda n: not fox or n % 2 == 0)

            for j in range(8):
                kq_high(act, j, j, 0)
            exp(Turn(0), 0, 0)
            exp(Turn(0), 0, 1)
            with act.Fori(0, TURNS - 1) as it:
                run(Turn(it))
            run(Turn(TURNS - 1, last=True))

        @block.vector
        def _(dve):
            if fox:
                k_one, q_one = (core.const[64:P, C_AUX + x:C_AUX + x + 1].to_broadcast([64, 4 * SEQ]) for x in range(2))
                dve.tensor_copy(klo[64:P].rearrange("p a b c -> p (a b c)"), k_one).then_inc(s_c, 1)
                dve.tensor_copy(q2b[64:P].rearrange("p a b c -> p (a b c)"), q_one).then_inc(s_c, 1)

            def cumulate():
                zero = pr[0:16, 0, 0, :]
                dve.memset(zero, 0.0).then_inc(s_cv, 1)
                dve.wait_ge(s_cv, 2)
                dve.tensor_copy(c[:], S[0][0:16, :, :].rearrange("p a b -> p (a b)")).then_inc(s_cv, 1)
                dve.wait_ge(s_cv, 3)
                dve.tensor_tensor_scan(c[:], c[:], zero, 0.0, ALU.add, ALU.add).then_inc(s_cv, 1)
                dve.wait_ge(s_cv, 4)
                dve.tensor_copy(cp[:, 2, :], c[:]).then_inc(s_cv, 1)
                dve.wait_ge(s_cv, 5)
                dve.tensor_tensor(cp[:, 3, :], c[:], cp[:, 2, :].bitcast(F32), ALU.subtract).then_inc(s_cv, 1)
                dve.wait_ge(s_cv, 6)
                dve.tensor_scalar(cp[:, 0, :], cp[:, 2, :].bitcast(F32), -1.0, None, ALU.mult).then_inc(s_cv, 1)
                dve.tensor_scalar(cp[:, 1, :], cp[:, 3, :].bitcast(F32), -1.0, None, ALU.mult).then_inc(s_cv, 1)
                dve.wait_ge(s_cv, 8)
                dve.wait_ge(s_c, 4)
                dve.memset(zero, 0.0).then_inc(s_cv, 3)

            def maximum(turn, s, m):
                n, col = (tiles[s % (2 * QT)] + 1) * P, 2 * (s % QT) + m
                dve.wait_ge(s_s, turn.it * 32 + (2 * s + m + 1))
                dve.tensor_reduce(nmx[:, col:col + 1], S[m][:].rearrange("p a b -> p (a b)")[:, 0:n],
                                  AX, ALU.max, negate=True).then_inc(s_nm, 1)

            def combine(turn, s):
                d = s % QT
                dve.wait_ge(s_e, turn.it * 32 + (2 * s + 4))
                dve.reciprocal(rinv[:, 2 * d:2 * d + 2], dsum[:, 2 * d:2 * d + 2]).then_inc(s_f, 1)
                if fox:
                    return
                n = (tiles[s] + 1) * P
                dve.wait_ge(s_f, turn.it * (4 * QT) + (2 * s + 1))
                dve.tensor_scalar(fac[:, d:d + 1], dsum[:, 2 * d:2 * d + 1], rinv[:, 2 * d + 1:2 * d + 2],
                                  core.neglam[:, 0:1], ALU.mult, ALU.mult).then_inc(s_f, 1)
                dve.wait_ge(s_f, turn.it * (4 * QT) + (2 * s + 2))
                dve.scalar_tensor_tensor(pr[:, s % 2, 0, 0:n], pr[:, s % 2, 1, 0:n], fac[:, d:d + 1],
                                         pr[:, s % 2, 0, 0:n], ALU.mult, ALU.add).then_inc(s_w, 1)

            def outputs(turn, s):
                t, d, par, it = tiles[s], s % QT, s // QT, turn.it
                dve.wait_ge(s_pv, it * (2 * QT * NM) + (s + 1) * NM)
                if d == 0:
                    dve.wait_ge(s_of, it * 2 + (par + 1))
                if fox:
                    dve.wait_ge(s_f, it * (2 * QT) + (s + 1))
                    dve.tensor_tensor(ost[:, par, t, :].rearrange("p (s e) -> p s e", s=2),
                                      O[:].rearrange("p (s e) -> p s e", s=2),
                                      rinv[:, 2 * d:2 * d + 2].unsqueeze(2).to_broadcast([P, 2, 64]),
                                      ALU.mult).then_inc(s_oe, 1)
                else:
                    dve.tensor_scalar(ost[:, par, t, :], O[:], rinv[:, 2 * d:2 * d + 1], None,
                                      ALU.mult).then_inc(s_oe, 1)

            def run(turn):
                for s in range(2 * QT):
                    for m in range(2):
                        if turn.has_next(s):
                            maximum(turn, s + 1, m)
                        for j in turn.kq_of(s, m):
                            kq_low(dve, j, turn.it * 16 + (8 + j), (j // 8 + 1) % 2)
                        if fox:
                            weights_out(dve, dve.tensor_copy, turn, s, m, lambda n: n % 2 == 1)
                        if not m:
                            combine(turn, s)
                    if s:
                        outputs(turn, s - 1)
                outputs(turn, 2 * QT - 1)

            if fox:
                cumulate()
            for j in range(8):
                kq_low(dve, j, j, 0)
            maximum(Turn(0), 0, 0)
            maximum(Turn(0), 0, 1)
            with dve.Fori(0, TURNS - 1) as it:
                run(Turn(it))
            run(Turn(TURNS - 1, last=True))




def decode_attention(nc, core, tag, fox, q_rows, k_new, v_new, k_cache, v_cache, logf_new, logf_cache, cum, o_rows):
    with ExitStack() as ctx:
        sb, ps, sem = scope(core, ctx, tag)
        KR = VR = 4
        kr, vr = sb("k_tiles", [P, KR, D]), sb("v_tiles", [P, VR, D])
        nr, vn = sb("new_rows", [P, 2, D]), sb("v_new", [P, D])
        nT = sb("new_T", [P, 2, KT, P])
        qbd = sb("q_diag", [P, KT, 32])
        kT = sb("kT", [P, 2, KT, P])
        sc = sb("scores", [P, 2, NKEY])
        pr = sb("probs", [P, 2, NKEY])
        pT = sb("probs_T", [P, CT + 1, 2, P])
        obd = sb("o_diag", [P, 2, P])
        oo = sb("o_out", [16, D])
        mx, nmx, ds, coef = sb("max", [P, 2]), sb("neg_max", [P, 2]), sb("sum", [P, 2]), sb("coef", [P, 2])
        KB = [ps(f"kb{x}", [P, 4, P]) for x in range(2)]
        SB = [ps(f"sb{x}", [P, 2, 2, P]) for x in range(2)]
        PB = [ps(f"pb{x}", [P, 2, 2, P]) for x in range(2)]
        OB = [ps(f"ob{x}", [P, P]) for x in range(2)]
        s_new, s_nt, s_ne, s_qb, s_ktr, s_qk, s_sm, s_mx, s_nm, s_e, s_cf, s_ptr, s_pv, s_oe, s_sel, s_st = (
            sem(x) for x in ("new", "nt", "ne", "qb", "ktr", "qk", "sm", "mx", "nm", "exp", "cf", "ptr", "pv", "oe",
                             "sel", "st"))
        s_kd, s_vd = [sem(f"kd{x}") for x in range(KR)], [sem(f"vd{x}") for x in range(VR)]
        s_ke, s_se, s_pe = ([sem(f"{n}{x}") for x in range(2)] for n in ("ke", "se", "pe"))
        s_oo = sem("oo")
        if fox:
            lf = sb("logf", [P, CT, P])
            lfn, lbd = sb("logf_new", [P, 16]), sb("logf_diag", [P, P])
            ca = sb("cum", [P, NKEY])
            zero = sb("zeros", [P, PAST])
            cn = sb("cum_new", [P, NQ])
            cb = sb("key_bias", [16, NB, NKEY])
            hs = sb("head_rows", [16, 2, P])
            s_lf, s_ct, s_cv, s_cd = sem("lf"), sem("ct"), sem("cv"), sem("cd")
        block = ctx.enter_context(nc.Block())
        W0 = C_WIN[1] if fox else C_WIN[0]
        SU, PU = (3, 2), (4, 3)

        @block.sync
        def _(sp):
            sp.dma_start(nr[:, 0, :], q_rows).then_inc(s_new, 16)
            sp.dma_start(nr[:, 1, :], k_new).then_inc(s_new, 16)
            if fox:
                sp.dma_start(lfn[:], logf_new).then_inc(s_lf, 16)
                sp.dma_start(hs[:].rearrange("a g p -> a (g p)"), core.hsel[:, 2048:NHSEL]).then_inc(s_lf, 16)
                for b in range(NB):
                    sp.dma_start(lf[:, :, b * 16:(b + 1) * 16],
                                 logf_cache[b].rearrange("(t p) h -> p t h", p=P)).then_inc(s_lf, 16)
                sp.wait_ge(s_cv, 8)
                sp.dma_start(cum, ca[:]).then_inc(s_cd, 16)
                sp.wait_ge(s_cd, 16)
                sp.dma_start(cb[:], cum.rearrange("(b h) k -> h b k", h=16)).then_inc(s_cd, 16)

            def load_k(b, t):
                sp.wait_ge(s_ktr, b * 16 + 2 * t + 2)
                sp.dma_start(kr[:, t % KR, :], k_cache[bass.ds(b * CT + t, 1)].rearrange("a p n -> (a p) n"))\
                    .then_inc(s_kd[t % KR], 16)

            def load_v(b, t):
                sp.wait_ge(s_pv, b * (CT + 1) + (t + 2 if t >= VR else t + 1))
                sp.dma_start(vr[:, t % VR, :], v_cache[bass.ds(b * CT + t, 1)].rearrange("a p n -> (a p) n"))\
                    .then_inc(s_vd[t % VR], 16)

            for t in range(CT):
                load_k(0, t)
            with sp.Fori(1, NB) as b:
                for t in range(CT):
                    load_k(b, t)
                    load_v(b - 1, t)
            for t in range(CT):
                load_v(NB - 1, t)
            sp.wait_ge(s_st, 16 * NB + 16)

        @block.gpsimd
        def _(pool):
            pool.memset(qbd[:], 0.0).then_inc(s_qb, 1)
            pool.wait_ge(s_qb, 1)
            pool.wait_ge(s_ne, 4)
            with pool.Fori(0, NB) as b:
                pool.wait_ge(s_sm, b + 1)
                for m in range(2):
                    rows = slice(64 * m, 64 * m + 64)
                    pool.tensor_copy(qbd[rows, :, 16 * m:16 * m + 16], nT[rows, 0, :, bass.ts(b, NQ)]).then_inc(s_qb, 1)

        @block.tensor
        def _(pe):
            for s, n in ((s_ktr, 2 * KR), (s_qk, 2), (s_pv, VR + 1), (s_sm, 1), (s_e, 1),
                         (s_sel, 1), (s_ptr, 1), (s_cf, 1), (s_ke[0], 1), (s_ke[1], 1), (s_se[0], 1),
                         (s_se[1], 1), (s_pe[0], 1), (s_pe[1], 1), (s_oe, 1), (s_oo, 1)):
                pe.sem_inc(s, n)
            pe.wait_ge(s_new, 32)
            for x in range(2):
                for g in range(2):
                    if x:
                        pe.wait_ge(s_ne, g + 1)
                    for c_ in range(4):
                        ins = pe.transpose(KB[g][:, c_, :], nr[:, x, (4 * g + c_) * P:(4 * g + c_ + 1) * P], core.ident)
                    ins.then_inc(s_nt, 1)
            if fox:
                pe.wait_ge(s_lf, 160)
                for t in range(CT):
                    ins = pe.transpose(SB[t // 4][:].rearrange("p a b c -> p (a b c)")[:, (t % 4) * P:(t % 4 + 1) * P],
                                       lf[:, t, :], core.ident)
                ins.then_inc(s_ct, 1)
                pe.wait_ge(s_cv, 2)
                pe.matmul(OB[0][:, 0:NQ], lbd[:], core.const[:, C_FRAME:C_FRAME + NQ],
                          start=True, stop=True).then_inc(s_ct, 1)
                pe.wait_ge(s_cd, 32)
                pe.wait_ge(s_cv, 8)
            pe.wait_ge(s_ne, 4)

            def keys(b, t):
                pe.wait_ge(s_kd[t % KR], b * 32 + 16 * (t // KR + 1))
                for g in range(2):
                    pe.wait_ge(s_ke[g], b * CT + t + 1)
                    for c_ in range(4):
                        ins = pe.transpose(KB[g][:, c_, :], kr[:, t % KR, (4 * g + c_) * P:(4 * g + c_ + 1) * P],
                                           core.ident)
                    ins.then_inc(s_ktr, 1)

            def scores(b, t):
                pair = t // 2
                bank, use = pair % 2, pair // 2
                if t % 2 == 0:
                    pe.wait_ge(s_se[bank], b * SU[bank] + use + 1)
                if t == 0:
                    pe.wait_ge(s_qb, b * 2 + 3)
                if t < CT:
                    for g in range(2):
                        pe.wait_ge(s_ke[g], b * CT + t + 2)
                for g in range(2):
                    out = SB[bank][:, t % 2, g, :]
                    for j in range(4):
                        k = kT[:, t % 2, 4 * g + j, :] if t < CT else nT[:, 1, 4 * g + j, :]
                        ins = pe.matmul(out[32 * j:32 * j + 32, :], qbd[:, 4 * g + j, :], k,
                                        start=True, stop=not fox and t < CT, skip_group_check=True)
                    if t == CT:
                        ins = pe.matmul(out, core.ident, core.const[:, bass.ds(b * -16 + (W0 + 112), P)],
                                        start=False, stop=not fox, skip_group_check=True)
                    if fox:
                        ins = pe.matmul(out, hs[:, g, :], cb[:, bass.ds(b, 1), t * P:(t + 1) * P].rearrange(
                            "h a k -> h (a k)"), start=False, stop=True, skip_group_check=True)
                ins.then_inc(s_qk if t < CT else s_sm, 1)

            def probs(b, pair):
                bank, use = pair % 2, pair // 2
                pe.wait_ge(s_pe[bank], b * PU[bank] + use + 1)
                if pair == 0:
                    pe.wait_ge(s_e, b * 2 + 3)
                for t in range(2 * pair, min(2 * pair + 2, CT + 1)):
                    for g in range(2):
                        ins = pe.transpose(PB[bank][:, t % 2, g, :], pr[:, g, t * P:(t + 1) * P], core.ident)
                ins.then_inc(s_ptr, 1)

            def values(b, t):
                pair = t // 2
                if t == 0:
                    pe.wait_ge(s_oe, b + 1)
                    pe.wait_ge(s_st, 16)
                if t % 2 == 0:
                    pe.wait_ge(s_pe[pair % 2], b * PU[pair % 2] + pair // 2 + 2)
                if t < CT:
                    pe.wait_ge(s_vd[t % VR], b * 32 + 16 * (t // VR + 1))
                for g in range(2):
                    for j in range(4):
                        cols = slice((4 * g + j) * P, (4 * g + j + 1) * P)
                        v = vr[:, t % VR, cols] if t < CT else vn[:, cols]
                        ins = pe.matmul(OB[g][32 * j:32 * j + 32, :], pT[:, t, g, 32 * j:32 * j + 32], v,
                                        start=t == 0, stop=t == CT)
                ins.then_inc(s_pv, 1)

            def select(b):
                pe.wait_ge(s_oe, b + 2)
                for g in range(2):
                    out = PB[g][:].rearrange("p a b c -> p (a b c)")
                    pe.wait_ge(s_pe[g], b * PU[g] + PU[g])
                    for j in range(4):
                        if fox:
                            for s in range(2):
                                c0 = C_SELB + (j * 2 + s) * 16
                                ins = pe.matmul(out[0:16, j * P + 64 * s:j * P + 64 * s + 64],
                                                core.const[:, c0:c0 + 16], obd[:, g, 64 * s:64 * s + 64],
                                                start=True, stop=True)
                        else:
                            c0 = C_SELA + j * 16
                            ins = pe.matmul(out[0:16, j * P:(j + 1) * P], core.const[:, c0:c0 + 16], obd[:, g, :],
                                            start=True, stop=True)
                    ins.then_inc(s_sel, 1)

            def stream(bs, bv):
                if bs is not None:
                    keys(bs, 0)
                if bv is not None:
                    probs(bv, 0)
                for t in range(CT + 1):
                    if bs is not None:
                        if t + 1 < CT:
                            keys(bs, t + 1)
                        scores(bs, t)
                    if bv is not None:
                        if t % 2 == 1:
                            probs(bv, t // 2 + 1)
                        values(bv, t)
                if bv is not None:
                    select(bv)

            stream(0, None)
            with pe.Fori(1, NB) as b:
                stream(b, b - 1)
            stream(None, NB - 1)

        def evacuation(eng, copy, half):
            other = 1 - half

            def keys(b, t):
                eng.wait_ge(s_ktr, b * 16 + (2 * t + half + 1 + 2 * KR))
                eng.wait_ge(s_qk, b * CT + t + 1)
                copy(kT[:, t % 2, 4 * half:4 * half + 4, :], KB[half][:]).then_inc(s_ke[half], 1)

            def scores(b, pair):
                if pair % 2 != half:
                    return
                n = 2 if pair < CT // 2 else 1
                if n == 2:
                    eng.wait_ge(s_qk, b * CT + 2 * pair + 2 + 2)
                else:
                    eng.wait_ge(s_sm, b + 2)
                if pair < 2:
                    eng.wait_ge(s_e, b * 2 + 1)
                dst = sc[:, :, 2 * pair * P:(2 * pair + n) * P].rearrange("p g (t k) -> p t g k", t=n)
                for x in range(n):
                    ins = copy(dst[:, x], SB[half][:, x])
                ins.then_inc(s_se[half], 1)

            def probs(b, pair):
                if pair % 2 != other:
                    return
                n = 2 if pair < CT // 2 else 1
                eng.wait_ge(s_ptr, b * 5 + pair + 2)
                if pair < 2:
                    eng.wait_ge(s_pv, b * (CT + 1) + VR + 1)
                copy(pT[:, 2 * pair:2 * pair + n], PB[other][:, 0:n]).then_inc(s_pe[other], 1)

            def selected(b):
                eng.wait_ge(s_sel, b * 2 + other + 2)
                eng.wait_ge(s_st, b * 16 + 16)
                copy(oo[:, other * HALF:(other + 1) * HALF],
                     PB[other][:].rearrange("p a b c -> p (a b c)")[0:16, :]).then_inc(s_pe[other], 1)

            def stream(bs, bv, outputs):
                if bs is not None:
                    keys(bs, 0)
                if bv is not None:
                    probs(bv, 0)
                for t in range(CT + 1):
                    if bs is not None:
                        if t + 1 < CT:
                            keys(bs, t + 1)
                        if t % 2 == 1 or t == CT:
                            scores(bs, t // 2)
                    if bv is not None and t % 2 == 1:
                        probs(bv, t // 2 + 1)
                if bv is not None:
                    outputs(bv)
                    selected(bv)

            return stream

        @block.scalar
        def _(act):
            def copy(o, x):
                return act.activation(o, x, ACT.Copy)

            def outputs(b):
                act.wait_ge(s_pv, b * (CT + 1) + (CT + 2 + VR))
                act.wait_ge(s_cf, b * 2 + 3)
                act.wait_ge(s_sel, b * 2 + 1)
                for g in range(2):
                    ins = act.activation(obd[:, g, :], OB[g][:], ACT.Copy, scale=coef[:, g:g + 1])
                ins.then_inc(s_oe, 1)

            def exps(b):
                for g in range(2):
                    act.wait_ge(s_nm, b * 2 + g + 1)
                    act.wait_ge(s_ptr, b * 5 + 1)
                    act.wait_ge(s_cf, b * 2 + 1)
                    act.activation(pr[:, g, :], sc[:, g, :], ACT.Exp, bias=nmx[:, g:g + 1], scale=QS,
                                   accum_out=ds[:, g:g + 1]).then_inc(s_e, 1)

            act.dma_start(vn[:], v_new).then_inc(s_st, 16)
            for x in range(2):
                act.wait_ge(s_nt, 2 * x + 1)
                copy(nT[:, x, 0:4, :], KB[0][:]).then_inc(s_ne, 1)
                act.wait_ge(s_nt, 2 * x + 2)
                copy(nT[:, x, 4:8, :], KB[1][:]).then_inc(s_ne, 1)
            stream = evacuation(act, copy, 0)

            def store(b):
                for g in range(2):
                    act.wait_ge(s_pe[g], b * PU[g] + PU[g] + 1)
                act.dma_start(o_rows[bass.ds(b * NQ + SEQ, NQ), :], oo[:]).then_inc(s_st, 16)

            stream(0, None, outputs)
            exps(0)
            with act.Fori(1, NB) as b:
                stream(b, b - 1, outputs)
                store(b - 1)
                exps(b)
            stream(None, NB - 1, outputs)
            store(NB - 1)

        @block.vector
        def _(dve):
            if fox:
                dve.memset(zero[:], 0.0).then_inc(s_cv, 1)
                dve.wait_ge(s_lf, 160)
                dve.tensor_tensor(lbd[:].rearrange("p (b h) -> p b h", h=16),
                                  lfn[:].unsqueeze(1).to_broadcast([P, NB, 16]),
                                  core.const[:, C_STREAM:C_STREAM + NB].unsqueeze(2).to_broadcast([P, NB, 16]),
                                  ALU.mult).then_inc(s_cv, 1)
                dve.wait_ge(s_ct, 1)
                for x in range(2):
                    dve.wait_ge(s_cv, 2 + x)
                    src = SB[x][:].rearrange("p a b c -> p (a b c)")
                    dve.tensor_tensor_scan(ca[:, x * HALF:(x + 1) * HALF], src, zero[:, 0:HALF],
                                           ca[:, HALF - 1:HALF] if x else 0.0, ALU.add, ALU.add).then_inc(s_cv, 1)
                dve.wait_ge(s_ct, 2)
                dve.wait_ge(s_cv, 4)
                dve.tensor_tensor_scan(cn[:], OB[0][:, 0:NQ], zero[:, 0:NQ], 0.0, ALU.add, ALU.add).then_inc(s_cv, 1)
                dve.wait_ge(s_cv, 5)
                dve.tensor_copy(mx[:, 0:1], ca[:, PAST - 1:PAST]).then_inc(s_cv, 1)
                dve.wait_ge(s_cv, 6)
                dve.tensor_scalar(ca[:, 0:PAST], ca[:, 0:PAST], mx[:, 0:1], -1.0 / QS, ALU.subtract,
                                  ALU.mult).then_inc(s_cv, 1)
                dve.wait_ge(s_cv, 7)
                dve.scalar_tensor_tensor(ca[:, PAST:NKEY].rearrange("p (b q) -> p b q", q=NQ),
                                         cn[:].unsqueeze(1).to_broadcast([P, NB, NQ]), -1.0 / QS,
                                         core.const[:, C_STREAM:C_STREAM + NB].unsqueeze(2).to_broadcast([P, NB, NQ]),
                                         ALU.mult, ALU.mult).then_inc(s_cv, 1)

            def maxima(b):
                for x in range(2):
                    dve.wait_ge(s_se[x], b * SU[x] + SU[x] + 1)
                for g in range(2):
                    dve.tensor_reduce(mx[:, g:g + 1], sc[:, g, :], AX, ALU.max).then_inc(s_mx, 1)
                for g in range(2):
                    dve.wait_ge(s_mx, b * 2 + g + 1)
                    dve.tensor_scalar(nmx[:, g:g + 1], mx[:, g:g + 1], -QS, None, ALU.mult).then_inc(s_nm, 1)

            def coefficients(b):
                dve.wait_ge(s_e, b * 2 + 3)
                dve.wait_ge(s_oe, b + 1)
                dve.reciprocal(coef[:], ds[:]).then_inc(s_cf, 2 if fox else 1)
                if not fox:
                    dve.wait_ge(s_cf, b * 2 + 2)
                    dve.tensor_scalar(coef[:], coef[:], core.lamcol[:, 0:1], None, ALU.mult).then_inc(s_cf, 1)

            stream = evacuation(dve, dve.tensor_copy, 1)
            stream(0, None, lambda b: None)
            maxima(0)
            coefficients(0)
            with dve.Fori(1, NB) as b:
                stream(b, b - 1, lambda b: None)
                maxima(b)
                coefficients(b)
            stream(None, NB - 1, lambda b: None)




def final_phase(nc, core, gain, y_prompt, y_sample):
    with ExitStack() as ctx:
        sb, ps, sem = scope(core, ctx, "fin")
        g, sq, y = sb("gain", [P, D]), sb("sq", [P, 2, D]), sb("y", [P, 2, D])
        ss, rs = sb("ss", [P, RT]), sb("rs", [P, RT])
        s_g, s_ss, s_v, s_y, s_rt = sem("g"), sem("ss"), sem("v"), sem("y"), sem("rt")
        s_o = [sem("o0"), sem("o1")]
        block = ctx.enter_context(nc.Block())

        @block.sync
        def _(sp):
            sp.dma_start(g[:], gain.partition_broadcast(P)).then_inc(s_g, 16)
            for r in range(RT):
                sp.wait_ge(s_y, r + 1)
                sp.dma_start(rows_of(y_prompt, y_sample, r), y[:, r % 2, :]).then_inc(s_o[r % 2], 16)
            for k in range(2):
                sp.wait_ge(s_o[k], 16 * ((RT - k + 1) // 2))

        @block.scalar
        def _(act):
            for r in range(RT):
                if r >= 2:
                    act.wait_ge(s_ss, r - 1)
                act.activation(sq[:, r % 2, :], core.h[:, r, :], ACT.Square,
                               accum_out=ss[:, r:r + 1]).then_inc(s_ss, 1)
                act.wait_ge(s_v, 2 * r + 2)
                act.activation(rs[:, r:r + 1], rs[:, r:r + 1], ACT.Sqrt).then_inc(s_rt, 1)

        @block.vector
        def _(dve):
            dve.wait_ge(s_g, 16)
            for r in range(RT):
                dve.wait_ge(s_ss, r + 1)
                dve.tensor_scalar(rs[:, r:r + 1], ss[:, r:r + 1], 1.0 / D, EPS, ALU.mult, ALU.add).then_inc(s_v, 1)
                dve.wait_ge(s_v, 2 * r + 1)
                dve.reciprocal(rs[:, r:r + 1], rs[:, r:r + 1]).then_inc(s_v, 1)
                dve.wait_ge(s_rt, r + 1)
                if r >= 2:
                    dve.wait_ge(s_o[r % 2], 16 * (r // 2))
                dve.scalar_tensor_tensor(y[:, r % 2, :], core.h[:, r, :], rs[:, r:r + 1], g[:], ALU.mult,
                                         ALU.mult).then_inc(s_y, 1)


def stream_step(nc, a, o, stop=99):
    xp = a["x_prompt"].rearrange("a s d -> (a s) d")
    xs = a["x_sample"].rearrange("b s d -> (b s) d")
    yp = o["y_prompt"].rearrange("a s d -> (a s) d")
    ys = o["y_sample"].rearrange("b s d -> (b s) d")
    kv = {}
    for n in ("ak_p", "av_p", "ak_s", "av_s"):
        kv[n] = o[n].rearrange("n b s h e -> (n b s) (h e)")
    for n in ("bk_p", "bv_p", "bk_s", "bv_s"):
        kv[n] = o[n].rearrange("b s h e -> (b s) (h e)")
    fp, fs = (o[n].rearrange("b s h -> (b s) h") for n in ("bf_p", "bf_s"))
    cak = a["cache_a_k"].rearrange("n b (t p) h e -> (n b t) p (h e)", p=P)
    cav = a["cache_a_v"].rearrange("n b (t p) h e -> (n b t) p (h e)", p=P)
    cbk = a["cache_b_k"].rearrange("b (t p) h e -> (b t) p (h e)", p=P)
    cbv = a["cache_b_v"].rearrange("b (t p) h e -> (b t) p (h e)", p=P)
    q = nc.dram_tensor("q_scratch", [ROWS, D], F32).ap()
    ao = nc.dram_tensor("o_scratch", [ROWS, D], F32).ap()
    cum = nc.dram_tensor("cum_scratch", [P, NKEY], F32).ap()
    cum_parts = nc.dram_tensor("cum_parts_scratch", [16, 4, SEQ], F32).ap()
    qd = (q[0:SEQ, :], q[SEQ:ROWS, :])
    with ExitStack() as ctx:
        core = Core(nc, ctx, a["head_sel"])
        start_phase(nc, core, xp, xs, a["const"],
                    [a[n] for n in ("lambda_q1", "lambda_k1", "lambda_q2", "lambda_k2")])
        wa = a["w_qkv_a"].rearrange("n d e -> (n d) e")
        dense_phase(nc, core, "qkv", "rms", a["norm_attn"][0, :], None,
                    [(wa, c, "rope", (*qd, c)) for c in (0, HALF)]
                    + [(wa, D + c, "rope", (kv["ak_p"], kv["ak_s"], c)) for c in (0, HALF)]
                    + [(wa, 2 * D + c, "store", (kv["av_p"], kv["av_s"], c)) for c in (0, HALF)])
        if stop <= 1:
            return
        prompt_attention(nc, core, "pa", False, q, kv["ak_p"], kv["av_p"], None, None, ao)
        if stop <= 2:
            return
        decode_attention(nc, core, "da", False, q[SEQ:ROWS, :], kv["ak_s"], kv["av_s"], cak, cav, None, None, None, ao)
        if stop <= 3:
            return
        dense_phase(nc, core, "oa", "head", a["subln_a"][0, :], ao,
                    [(a["w_o_a"].rearrange("n d e -> (n d) e"), c, "add", c) for c in (0, HALF)])
        mlp_phase(nc, core, "m0", a["norm_mlp"][0, :], a["w_up"][0], a["w_down"][0])
        if stop <= 4:
            return
        core.clear_semaphores()
        w = a["w_kvf"]
        dense_phase(nc, core, "kv", "rms", a["norm_kv"], None,
                    [(w, c, "store", (kv["bk_p"], kv["bk_s"], c)) for c in (0, HALF)]
                    + [(w, D + c, "store", (kv["bv_p"], kv["bv_s"], c)) for c in (0, HALF)],
                    forget=(w[:, 2 * D:2 * D + 16], a["b_f"], fp, fs))
        dense_phase(nc, core, "qb", "rms", a["norm_attn"][1, :], None,
                    [(a["w_q_b"].rearrange("n d e -> (n d) e"), c, "store", (*qd, c)) for c in (0, HALF)])
        if stop <= 5:
            return
        prompt_attention(nc, core, "pb", True, q, kv["bk_p"], kv["bv_p"], fp, cum_parts, ao)
        decode_attention(nc, core, "db", True, q[SEQ:ROWS, :], kv["bk_s"], kv["bv_s"], cbk, cbv, fs,
                         a["cache_b_logf"], cum, ao)
        if stop <= 6:
            return
        dense_phase(nc, core, "ob", "plain", None, ao,
                    [(a["w_o_b"].rearrange("n d e -> (n d) e"), c, "add", c) for c in (0, HALF)])
        mlp_phase(nc, core, "m1", a["norm_mlp"][1, :], a["w_up"][1], a["w_down"][1])
        final_phase(nc, core, a["norm_final"], yp, ys)
        core.clear_semaphores()


_INS = ["x_prompt", "x_sample", "cache_a_k", "cache_a_v", "cache_b_k", "cache_b_v", "cache_b_logf", "norm_attn",
        "norm_mlp", "w_qkv_a", "lambda_q1", "lambda_k1", "lambda_q2", "lambda_k2", "subln_a", "w_o_a", "norm_kv",
        "w_kvf", "b_f", "w_q_b", "w_o_b", "w_up", "w_down", "norm_final"]
_OUTS = {"y_prompt": (1, SEQ, D), "y_sample": (NB, NQ, D), "ak_p": (1, 1, SEQ, 16, 64), "av_p": (1, 1, SEQ, 8, 128),
         "bk_p": (1, SEQ, 16, 64), "bv_p": (1, SEQ, 16, 64), "bf_p": (1, SEQ, 16),
         "ak_s": (1, NB, NQ, 16, 64), "av_s": (1, NB, NQ, 8, 128),
         "bk_s": (NB, NQ, 16, 64), "bv_s": (NB, NQ, 16, 64), "bf_s": (NB, NQ, 16)}


def kernel(**inputs):
    import numpy as _np
    import concourse.bacc as _bacc
    from concourse import mybir as _mybir
    from concourse.bass_utils import run_bass_kernel_spmd as _run

    nc = _bacc.Bacc("TRN2", target_bir_lowering=False, num_devices=1)
    table, head_sel = constant_tables()
    arrays, a, o = {}, {}, {}
    for name, x in [(n, inputs[n]) for n in _INS] + [("const", table), ("head_sel", head_sel)]:
        x = _np.ascontiguousarray(x)
        arrays[f"in_{name}"] = x
        a[name] = nc.dram_tensor(f"in_{name}", x.shape, _mybir.dt.from_np(x.dtype), kind="ExternalInput").ap()
    for name, shape in _OUTS.items():
        o[name] = nc.dram_tensor(f"out_{name}", shape, F32, kind="ExternalOutput").ap()
    stream_step(nc, a, o)
    r = _run(nc, [arrays], core_ids=[0])
    return tuple(r.results[0][f"out_{name}"] for name in _OUTS)
```

```python
from contextlib import ExitStack

import numpy as np

import concourse.bass as bass
from concourse import mybir

F32 = mybir.dt.float32
F32R = mybir.dt.float32r
ALU = mybir.AluOpType
ACT = mybir.ActivationFunctionType
AX = mybir.AxisListType.X

P = 128
D = 1024
KT = D // P
SEQ = 1024
RT = SEQ // P + 1
ROWS = RT * P
NB, NQ = 8, 16
PAST = 1024
CT = PAST // P
NKEY = PAST + P
DFF = 4096
FC = 256
EPS = 1e-6
NEG = -1e30
QS = 64.0 ** -0.5
HALF = 512

C_IDENT, C_BLK, C_TRI = 0, 128, 256
C_WIN = (384, 384 + 240)
C_SELA = 864
C_SELB = C_SELA + 64
C_STREAM = C_SELB + 128
C_FRAME = C_STREAM + 8
C_LAM = C_FRAME + 16
C_ROPE = C_LAM + 2
C_AUX = C_ROPE + RT * 64
NCONST = C_AUX + 2
NHSEL = 16 * 128 + 2 * 128


def constant_tables():
    p = np.arange(P)
    t = np.zeros((P, NCONST), np.float32)
    t[:, C_IDENT:C_IDENT + P] = np.eye(P)
    t[:, C_BLK:C_BLK + P] = np.where(p[None] // 64 <= p[:, None] // 64, 0, NEG)
    t[:, C_TRI:C_TRI + P] = np.where(p[None] <= p[:, None], 0, NEG)
    j, m, q = p // 32, p // 16 % 2, p % 16
    c = np.arange(240)[None] - 112
    t[:, C_WIN[0]:C_WIN[0] + 240] = np.where((c >= 0) & (c < NQ), 0, NEG)
    t[:, C_WIN[1]:C_WIN[1] + 240] = np.where((c >= 0) & (c <= q[:, None]), 0, NEG)
    for a in range(4):
        for f in range(NQ):
            t[:, C_SELA + a * 16 + f] = (j == a) & (q == f)
            for s in range(2):
                t[:, C_SELB + (a * 2 + s) * 16 + f] = (j == a) & (q == f) & (m == s)
    for b in range(8):
        t[:, C_STREAM + b] = p // 16 == b
    for f in range(NQ):
        t[:, C_FRAME + f] = q == f
    t[:, C_LAM] = m == 0
    t[:, C_LAM + 1] = -(m == 1).astype(np.float32)
    t[66:68, C_AUX] = 1
    t[64:66, C_AUX + 1] = 1
    inv = np.power(np.float32(10000.0), -np.arange(32, dtype=np.float32) / np.float32(32))
    for r in range(RT):
        pos = (r * P + p if r < RT - 1 else PAST + q).astype(np.float32)
        ang = (pos[:, None] * inv[None]).astype(np.float32)
        t[:, C_ROPE + r * 64:C_ROPE + r * 64 + 32] = np.cos(ang)
        t[:, C_ROPE + r * 64 + 32:C_ROPE + r * 64 + 64] = np.sin(ang)
    h = np.zeros((16, NHSEL), np.float32)
    for a in range(16):
        h[a, a * 128:(a + 1) * 128] = 1
        for g in range(2):
            h[a, 2048 + g * 128:2048 + (g + 1) * 128] = 2 * (4 * g + j) + m == a
    return t, h


class Core:

    def __init__(self, nc, ctx, hsel):
        self.nc, self.hsel, self.sems = nc, hsel, []
        self.h = ctx.enter_context(nc.sbuf_tensor("h_rows", [P, RT, D], F32))
        self.const = ctx.enter_context(nc.sbuf_tensor("const_sb", [P, NCONST], F32))
        self.ident = self.const[:, C_IDENT:C_IDENT + P]
        self.neglam = ctx.enter_context(nc.sbuf_tensor("neglam", [P, 1], F32))
        self.lamcol = ctx.enter_context(nc.sbuf_tensor("lamcol", [P, 1], F32))

    def normed_rows(self, ctx, tag):
        self.xt_hi, self.xt_lo = (ctx.enter_context(self.nc.sbuf_tensor(f"{tag}_xt_{x}", [P, KT, ROWS], F32R))
                                  for x in ("hi", "lo"))

    def clear_semaphores(self):
        self.nc.clear_and_free_semaphores(self.sems)
        self.nc.all_engine_barrier()
        self.sems = []

    def cos_sin(self, r):
        v = self.const[:, C_ROPE + r * 64:C_ROPE + (r + 1) * 64]
        return v[:, 0:32], v[:, 32:64]


def rows_of(prompt, sample, r):
    return prompt[r * P:(r + 1) * P, :] if r < RT - 1 else sample


def scope(core, ctx, tag):
    nc = core.nc

    def sb(name, shape, dt=F32):
        return ctx.enter_context(nc.sbuf_tensor(f"{tag}_{name}", shape, dt))

    def ps(name, shape):
        return ctx.enter_context(nc.psum_tensor(f"{tag}_{name}", shape, F32))

    def sem(name):
        s = nc.alloc_semaphore(name=f"{tag}_{name}")
        core.sems.append(s)
        return s

    return sb, ps, sem




def start_phase(nc, core, x_prompt, x_sample, table, lams):
    with ExitStack() as ctx:
        sb, ps, sem = scope(core, ctx, "st")
        lv = sb("lam_vectors", [P, 4, 64])
        prod = sb("lam_products", [P, 64])
        dots = sb("lam_dots", [P, 2])
        ex = sb("lam_exps", [P, 2])
        s_load, s_dot, s_exp, s_v = sem("load"), sem("dot"), sem("exp"), sem("v")
        block = ctx.enter_context(nc.Block())

        @block.sync
        def _(sp):
            for i, v in enumerate(lams):
                sp.dma_start(lv[:, i, :], v.rearrange("a d -> (a d)").partition_broadcast(P)).then_inc(s_load, 16)
            sp.dma_start(core.const[:], table).then_inc(s_load, 16)
            for r in range(RT):
                sp.dma_start(core.h[:, r, :], rows_of(x_prompt, x_sample, r)).then_inc(s_load, 16)
            sp.wait_ge(s_load, 16 * (5 + RT))

        @block.scalar
        def _(act):
            act.wait_ge(s_dot, 2)
            act.activation(ex[:], dots[:], ACT.Exp).then_inc(s_exp, 1)

        @block.vector
        def _(dve):
            dve.wait_ge(s_load, 16 * (5 + RT))
            for i in range(2):
                if i:
                    dve.wait_ge(s_dot, 1)
                dve.tensor_tensor_reduce(prod[:], lv[:, 2 * i, :], lv[:, 2 * i + 1, :], 1.0, 0.0,
                                         ALU.mult, ALU.add, dots[:, i:i + 1]).then_inc(s_dot, 1)
            dve.wait_ge(s_exp, 1)
            dve.tensor_tensor(core.neglam[:], ex[:, 1:2], ex[:, 0:1], ALU.subtract).then_inc(s_v, 1)
            dve.wait_ge(s_v, 1)
            dve.tensor_scalar(core.neglam[:], core.neglam[:], -0.2, None, ALU.add).then_inc(s_v, 1)
            dve.wait_ge(s_v, 2)
            dve.tensor_scalar(core.lamcol[:], core.const[:, C_LAM + 1:C_LAM + 2], core.neglam[:, 0:1], -1.0,
                              ALU.mult, ALU.mult).then_inc(s_v, 1)
            dve.wait_ge(s_v, 3)
            dve.tensor_tensor(core.lamcol[:], core.lamcol[:], core.const[:, C_LAM:C_LAM + 1],
                              ALU.add).then_inc(s_v, 1)




class Norm:

    def __init__(self, core, sb, ps, sem, tag, kind, gain, src=None, buffers=2):
        self.core, self.kind, self.gain_src, self.src = core, kind, gain, src
        self.xn, self.buffers = sb(f"{tag}xn", [P, buffers, D]), buffers
        self.own_rows = kind in ("rms", "final")
        self.w, self.width = (1, D) if self.own_rows else (8, P)
        self.stat, self.rstd = sb(f"{tag}stat", [P, RT, self.w]), sb(f"{tag}rstd", [P, RT, self.w])
        if kind != "plain":
            self.gain = sb(f"{tag}gain", [P, self.width])
        if kind == "head":
            self.sqh = sb(f"{tag}sqh", [P, D])
        if kind != "final":
            self.bank = [ps(f"{tag}nt{i}", [P, 4, P]) for i in range(2)]
        self.s_pre, self.s_root, self.s_gain, self.s_sq, self.s_rs, self.s_xn, self.s_tp, self.s_hi, self.s_lo = (
            sem(tag + x) for x in ("pre", "root", "gain", "sumsq", "rstd", "xn", "xT", "xhi", "xlo"))
        self.s_x = [sem(f"{tag}x{x}") for x in range(2)]
        self.steps = 0

    def sync(self, sp):
        if self.kind != "plain":
            sp.dma_start(self.gain[:], self.gain_src.partition_broadcast(P)).then_inc(self.s_gain, 16)

    def store(self, sp):
        for r in range(RT):
            sp.wait_ge(self.s_xn, r + 1)
            sp.dma_start(self.src(r), self.buffer(r)).then_inc(self.s_x[r % 2], 16)
        for k in range(2):
            sp.wait_ge(self.s_x[k], 16 * ((RT - k + 1) // 2))

    def buffer(self, r):
        return self.xn[:, r % self.buffers, :]

    def buffer_free(self, eng, r):
        if r >= self.buffers and self.kind == "final":
            eng.wait_ge(self.s_x[r % 2], 16 * (r // 2))
        elif r >= self.buffers:
            eng.wait_ge(self.s_tp, 2 * (r - self.buffers) + 2)

    def scalar(self, act, r):
        def load(x):
            self.buffer_free(act, x)
            act.dma_start(self.buffer(x), self.src[x * P:(x + 1) * P, :]).then_inc(self.s_x[x % 2], 16)

        if r == 0 and not self.own_rows:
            load(0)
            load(1)
        if self.own_rows:
            self.buffer_free(act, r)
            act.activation(self.buffer(r), self.core.h[:, r, :], ACT.Square,
                           accum_out=self.stat[:, r, 0:1]).then_inc(self.s_sq, 1)
        elif self.kind == "head":
            act.wait_ge(self.s_x[r % 2], 16 * (r // 2 + 1))
            if r:
                act.wait_ge(self.s_pre, r)
            act.activation(self.sqh[:], self.buffer(r), ACT.Square).then_inc(self.s_sq, 1)
        if self.kind != "plain":
            act.wait_ge(self.s_pre, r + 1)
            act.activation(self.rstd[:, r, 0:self.w], self.rstd[:, r, 0:self.w], ACT.Sqrt).then_inc(self.s_root, 1)
        if r:
            self.high(act, r - 1)
            if not self.own_rows and r + 1 < RT:
                load(r + 1)

    def high(self, act, r):
        if self.kind == "final":
            return
        for g in range(2):
            act.wait_ge(self.s_tp, 2 * r + g + 1)
            act.activation(self.core.xt_hi[:, 4 * g:4 * g + 4, r * P:(r + 1) * P], self.bank[g][:],
                           ACT.Copy).then_inc(self.s_hi, 1)

    def vector(self, dve, r):
        k = self.kind
        x = self.buffer(r)
        xh = x.rearrange("p (h e) -> p h e", e=P)

        def own(ins):
            self.steps += 1
            ins.then_inc(self.s_rs, 1)
            dve.wait_ge(self.s_rs, self.steps)

        if k != "plain":
            if r == 0:
                dve.wait_ge(self.s_gain, 16)
                if k == "head":
                    own(dve.tensor_scalar(self.gain[:], self.gain[:], 0.8, None, ALU.mult))
            dve.wait_ge(self.s_sq, r + 1)
            if k == "head":
                own(dve.tensor_reduce(self.stat[:, r, :], self.sqh[:].rearrange("p (h e) -> p h e", e=P), AX, ALU.add))
            own(dve.tensor_scalar(self.stat[:, r, 0:self.w], self.stat[:, r, 0:self.w], 1.0 / self.width, EPS,
                                  ALU.mult, ALU.add))
            dve.reciprocal(self.rstd[:, r, 0:self.w], self.stat[:, r, 0:self.w]).then_inc(self.s_pre, 1)
        if r:
            self.low(dve, r - 1)
        if k == "plain":
            return
        dve.wait_ge(self.s_root, r + 1)
        if self.own_rows:
            dve.scalar_tensor_tensor(x, self.core.h[:, r, :], self.rstd[:, r, 0:1], self.gain[:], ALU.mult,
                                     ALU.mult).then_inc(self.s_xn, 1)
        else:
            own(dve.tensor_tensor(xh, xh, self.rstd[:, r, :].unsqueeze(2).to_broadcast([P, 8, P]), ALU.mult))
            dve.tensor_tensor(xh, xh, self.gain[:].unsqueeze(1).to_broadcast([P, 8, P]),
                              ALU.mult).then_inc(self.s_xn, 1)

    def low(self, dve, r):
        if self.kind == "final":
            return
        for g in range(2):
            dve.wait_ge(self.s_hi, 2 * r + g + 1)
            hi = self.core.xt_hi[:, 4 * g:4 * g + 4, r * P:(r + 1) * P]
            dve.tensor_tensor(self.core.xt_lo[:, 4 * g:4 * g + 4, r * P:(r + 1) * P], self.bank[g][:],
                              hi.bitcast(F32), ALU.subtract).then_inc(self.s_lo, 1)

    def tensor(self, pe, r):
        if self.kind == "final":
            return
        if self.kind == "plain":
            pe.wait_ge(self.s_x[r % 2], 16 * (r // 2 + 1))
        else:
            pe.wait_ge(self.s_xn, r + 1)
        for g in range(2):
            if r:
                pe.wait_ge(self.s_lo, 2 * r + g - 1)
            for c in range(4):
                ins = pe.transpose(self.bank[g][:, c, :], self.buffer(r)[:, (4 * g + c) * P:(4 * g + c + 1) * P],
                                   self.core.ident)
            ins.then_inc(self.s_tp, 1)

    def ready(self, pe, r):
        pe.wait_ge(self.s_lo, 2 * r + 2)


def product(pe, out, lhs, rhs, start, stop):
    (lh, ll), (rh, rl) = lhs, rhs
    pe.matmul(out, lh, rh, start=start, stop=False)
    pe.matmul(out, lh, rl, start=False, stop=False)
    return pe.matmul(out, ll, rh, start=False, stop=stop)




def dense_phase(nc, core, tag, kind, gain, src, pieces, forget=None, following=None):
    with ExitStack() as ctx:
        sb, ps, sem = scope(core, ctx, tag)
        norm = Norm(core, sb, ps, sem, "", kind, gain, src) if kind else None
        nxt = None
        if following is not None:
            nxt = Norm(core, sb, ps, sem, "next_", "rms", following, buffers=1 if norm else 2)
        PARTS = 4
        KP = KT // PARTS
        raw = sb("w_raw", [P, 2, KP, HALF])
        whi = sb("w_hi", [P, 2, KT, HALF], F32R)
        wlo = sb("w_lo", [P, 2, KT, HALF], F32R)
        stores = any(do != "add" for _, _, do, _ in pieces)
        passes = [[i] for i in range(len(pieces))] if stores else [list(range(len(pieces)))]
        last = len(passes) - 1
        behind = 0 if norm else 1
        if stores:
            ob = sb("out_rows", [P, 2, HALF])
        if any(do == "rope" for _, _, do, _ in pieces):
            tc, tsn = sb("times_cos", [P, HALF]), sb("times_sin", [P, HALF])
        NPS = 3 if forget or (norm and nxt) else 4
        acc = [ps(f"acc{i}", [P, HALF]) for i in range(NPS)]
        s_whi, s_wlo, s_mm, s_ev = sem("whi"), sem("wlo"), sem("mm"), sem("ev")
        s_raw = [sem("raw0"), sem("raw1")]
        s_rot = sem("rot")
        s_st = [sem("store0"), sem("store1")]
        if forget:
            w_f, b_f, f_prompt, f_sample = forget
            fraw = sb("f_raw", [P, KT, 16])
            fhi, flo = sb("f_hi", [P, KT, 16], F32R), sb("f_lo", [P, KT, 16], F32R)
            fb = sb("f_bias", [P, 16])
            z, e, u, t, m = (sb(f"f_{x}", [P, RT, 16]) for x in "zeutm")
            facc = ps("f_acc", [P, RT, 16])
            s_fl, s_fw, s_fm, s_fv, s_fa, s_fo = sem("fl"), sem("fw"), sem("fm"), sem("fv"), sem("fa"), sem("fo")
        block = ctx.enter_context(nc.Block())
        NT = len(pieces) * RT

        def row_steps(i, first, body, end):
            ahead = NPS - 1 if stores else 2
            if i or not norm:
                for r in range(RT):
                    body(r)
                return
            for r in range(RT + ahead):
                if r < RT:
                    first(r)
                elif r == RT:
                    end()
                if r >= ahead:
                    body(r - ahead)

        @block.sync
        def _(sp):
            def load(n):
                w, c0, _, _ = pieces[n // PARTS]
                k = n % PARTS * KP
                if n >= 2:
                    sp.wait_ge(s_wlo, n - 1)
                sp.dma_start(raw[:, n % 2], w[:, c0:c0 + HALF].rearrange("(k p) n -> p k n", p=P)[
                    :, k:k + KP, :]).then_inc(s_raw[n % 2], 16)

            if norm:
                norm.sync(sp)
            load(0)
            load(1)
            if forget:
                sp.dma_start(fraw[:], w_f.rearrange("(k p) n -> p k n", p=P)).then_inc(s_fl, 16)
                sp.dma_start(fb[:], b_f.partition_broadcast(P)).then_inc(s_fl, 16)
            if nxt:
                nxt.sync(sp)
            for n in range(2, PARTS * len(pieces)):
                load(n)

        @block.gpsimd
        def _(pool):
            if forget:
                pool.wait_ge(s_fl, 32)
                pool.tensor_copy(fhi[:], fraw[:]).then_inc(s_fw, 1)
                pool.wait_ge(s_fw, 1)
                pool.tensor_tensor(flo[:], fraw[:], fhi[:].bitcast(F32), ALU.subtract).then_inc(s_fw, 1)
            for n in range(PARTS * len(pieces)):
                k, slot = n % PARTS * KP, n // PARTS % 2
                pool.wait_ge(s_whi, n + 1)
                pool.tensor_tensor(wlo[:, slot, k:k + KP, :], raw[:, n % 2], whi[:, slot, k:k + KP, :].bitcast(F32),
                                   ALU.subtract).then_inc(s_wlo, 1)

        @block.tensor
        def _(pe):
            def forget_products(r):
                if r == 0:
                    pe.wait_ge(s_fw, 2)
                for k in range(KT):
                    x = [v[:, k, r * P:(r + 1) * P] for v in (core.xt_hi, core.xt_lo)]
                    ins = product(pe, facc[:, r, :], x, (fhi[:, k, :], flo[:, k, :]), k == 0, k == KT - 1)
                if r == RT - 1:
                    ins.then_inc(s_fm, 1)

            if norm:
                norm.tensor(pe, 0)
            n = 0
            for i, group in enumerate(passes):
                for r in range(RT):
                    if norm and i == 0:
                        if r + 1 < RT:
                            norm.tensor(pe, r + 1)
                        norm.ready(pe, r)
                    if forget and i == 0:
                        forget_products(r)
                    for piece in group:
                        if r == 0:
                            pe.wait_ge(s_wlo, PARTS * (piece + 1))
                        if n >= NPS:
                            pe.wait_ge(s_ev, n - NPS + 1)
                        for k in range(KT):
                            x = [v[:, k, r * P:(r + 1) * P] for v in (core.xt_hi, core.xt_lo)]
                            ins = product(pe, acc[n % NPS][:], x, (whi[:, piece % 2, k, :], wlo[:, piece % 2, k, :]),
                                          k == 0, k == KT - 1)
                        ins.then_inc(s_mm, 1)
                        n += 1
                    if nxt and i == last and r > behind:
                        nxt.tensor(pe, r - behind - 1)
            if nxt:
                for r in range(RT - behind - 1, RT):
                    nxt.tensor(pe, r)

        @block.vector
        def _(dve):
            rotations = [0]

            def forget_values():
                dve.wait_ge(s_fm, 1)
                dve.tensor_tensor(z[:], facc[:], fb[:].unsqueeze(1).to_broadcast([P, RT, 16]),
                                  ALU.add).then_inc(s_fv, 1)
                dve.wait_ge(s_fv, 1)
                dve.tensor_scalar(u[:], z[:], -1.0, None, ALU.mult).then_inc(s_fv, 1)
                dve.wait_ge(s_fv, 2)
                dve.tensor_tensor(t[:], z[:], u[:], ALU.min).then_inc(s_fv, 1)
                dve.wait_ge(s_fa, 1)
                dve.tensor_scalar(u[:], e[:], 1.0, None, ALU.add).then_inc(s_fv, 1)
                dve.wait_ge(s_fa, 2)
                dve.tensor_scalar(m[:], u[:], 1.0, None, ALU.is_equal).then_inc(s_fv, 1)
                dve.tensor_scalar(u[:], u[:], -1.0, None, ALU.add).then_inc(s_fv, 1)
                dve.wait_ge(s_fv, 6)
                dve.tensor_tensor(u[:], u[:], m[:], ALU.add).then_inc(s_fv, 1)
                dve.tensor_tensor(t[:], t[:], m[:], ALU.add).then_inc(s_fv, 1)
                dve.wait_ge(s_fv, 8)
                dve.tensor_tensor(t[:], t[:], e[:], ALU.mult).then_inc(s_fv, 1)
                dve.reciprocal(m[:], u[:]).then_inc(s_fv, 1)
                dve.wait_ge(s_fv, 10)
                dve.tensor_tensor(t[:], t[:], m[:], ALU.mult).then_inc(s_fv, 1)
                dve.tensor_scalar(z[:], z[:], 0.0, None, ALU.min).then_inc(s_fv, 1)
                dve.wait_ge(s_fv, 12)
                dve.tensor_tensor(z[:], z[:], t[:], ALU.subtract).then_inc(s_fv, 1)

            def out_rows(n, r, do, dst):
                dve.wait_ge(s_mm, n + 1)
                src_ = acc[n % NPS][:]
                if do == "add":
                    hc = core.h[:, r, dst:dst + HALF]
                    dve.tensor_tensor(hc, hc, src_, ALU.add).then_inc(s_ev, 1)
                    return
                if n >= 2:
                    dve.wait_ge(s_st[n % 2], 16 * (n // 2))
                o = ob[:, n % 2, :]
                if do == "store":
                    dve.tensor_copy(o, src_).then_inc(s_ev, 1)
                    return
                v = src_.rearrange("p (h s e) -> p h s e", s=2, e=32)
                cos, sin = (x.unsqueeze(1).unsqueeze(1).to_broadcast([P, 8, 2, 32]) for x in core.cos_sin(r))
                if rotations[0]:
                    dve.wait_ge(s_ev, n)
                tcv = tc[:].rearrange("p (h s e) -> p h s e", s=2, e=32)
                tsv = tsn[:].rearrange("p (h s e) -> p h s e", s=2, e=32)
                dve.tensor_tensor(tcv, v, cos, ALU.mult).then_inc(s_rot, 1)
                dve.tensor_tensor(tsv, v, sin, ALU.mult).then_inc(s_rot, 1)
                rotations[0] += 2
                dve.wait_ge(s_rot, rotations[0])
                ov = o.rearrange("p (h s e) -> p h s e", s=2, e=32)
                dve.tensor_tensor(ov[:, :, 0, :], tcv[:, :, 0, :], tsv[:, :, 1, :], ALU.subtract).then_inc(s_rot, 1)
                rotations[0] += 1
                dve.wait_ge(s_rot, rotations[0])
                dve.tensor_tensor(ov[:, :, 1, :], tcv[:, :, 1, :], tsv[:, :, 0, :], ALU.add).then_inc(s_ev, 1)

            for i, group in enumerate(passes):
                def body(r):
                    for x, piece in enumerate(group):
                        out_rows((i * RT + r) * len(group) + x, r, *pieces[piece][2:])
                    if nxt and i == last and r >= behind:
                        nxt.vector(dve, r - behind)

                row_steps(i, lambda r: norm.vector(dve, r), body, lambda: norm.low(dve, RT - 1))
                if forget and i == 0:
                    forget_values()
            if nxt:
                for r in range(RT - behind, RT):
                    nxt.vector(dve, r)
                nxt.low(dve, RT - 1)

        @block.scalar
        def _(act):
            def weight_highs(piece):
                if piece >= 2:
                    act.wait_ge(s_mm, RT * (piece - 1))
                for n in range(PARTS * piece, PARTS * (piece + 1)):
                    k = n % PARTS * KP
                    act.wait_ge(s_raw[n % 2], 16 * (n // 2 + 1))
                    act.activation(whi[:, piece % 2, k:k + KP, :], raw[:, n % 2], ACT.Copy).then_inc(s_whi, 1)

            def forget_values():
                act.wait_ge(s_fv, 3)
                act.activation(e[:], t[:], ACT.Exp).then_inc(s_fa, 1)
                act.wait_ge(s_fv, 4)
                act.activation(t[:], u[:], ACT.Ln).then_inc(s_fa, 1)
                act.wait_ge(s_fv, 13)
                act.dma_start(f_prompt.rearrange("(r p) h -> p r h", p=P), z[:, 0:RT - 1, :]).then_inc(s_fo, 16)
                act.dma_start(f_sample, z[:, RT - 1, :]).then_inc(s_fo, 16)

            weight_highs(0)
            for i, group in enumerate(passes):
                def body(r):
                    n = (i * RT + r) * len(group)
                    if r == 0 and i + 1 < len(pieces) and not (norm and i == 0):
                        weight_highs(i + 1)
                    if stores:
                        prompt, sample, d0 = pieces[i][3]
                        act.wait_ge(s_ev, n + 1)
                        act.dma_start(rows_of(prompt, sample, r)[:, d0:d0 + HALF],
                                      ob[:, n % 2, :]).then_inc(s_st[n % 2], 16)
                    if nxt and i == last:
                        if not stores:
                            act.wait_ge(s_ev, n + len(group))
                        nxt.scalar(act, r)

                def first(r):
                    norm.scalar(act, r)
                    if r == 1 and len(pieces) > 1:
                        weight_highs(1)

                row_steps(i, first, body, lambda: norm.high(act, RT - 1))
                if forget and i == 0:
                    forget_values()
            if nxt:
                nxt.high(act, RT - 1)
            if stores:
                for k in range(2):
                    act.wait_ge(s_st[k], 16 * ((NT - k + 1) // 2))
            if forget:
                act.wait_ge(s_fo, 32)




def mlp_phase(nc, core, tag, w_up, w_down, following, y_rows=None):
    with ExitStack() as ctx:
        sb, ps, sem = scope(core, ctx, tag)
        nxt = Norm(core, sb, ps, sem, "next_", "final" if y_rows else "rms", following, y_rows)
        NF, RG = FC // P, 3
        GW = ROWS // RG
        up_raw, dn_raw = sb("up_raw", [P, KT, FC]), sb("dn_raw", [P, NF, D])
        up_hi, up_lo = sb("up_hi", [P, KT, FC], F32R), sb("up_lo", [P, KT, FC], F32R)
        dn_hi, dn_lo = sb("dn_hi", [P, NF, D], F32R), sb("dn_lo", [P, NF, D], F32R)
        hid_hi, hid_lo = sb("hid_hi", [P, NF, ROWS], F32R), sb("hid_lo", [P, NF, ROWS], F32R)
        rl, sq = sb("relu", [P, 2, GW]), sb("relu2", [P, 2, GW])
        ups = [ps(f"up{i}", [P, HALF]) for i in range(3)]
        dns = [ps(f"dn{i}", [P, HALF]) for i in range(3)]
        s_ur, s_dr, s_uh, s_ul, s_dh, s_dl = (sem(x) for x in ("ur", "dr", "uh", "ul", "dh", "dl"))
        s_um, s_ue, s_sq, s_hh, s_hl, s_dm, s_de = (sem(x) for x in ("um", "ue", "sq", "hh", "hl", "dm", "de"))
        block = ctx.enter_context(nc.Block())
        NU, ND = NF * RG, RT * 2
        STEPS = DFF // FC

        @block.sync
        def _(sp):
            nxt.sync(sp)
            with sp.Fori(0, STEPS) as i:
                sp.wait_ge(s_ul, i + 1)
                sp.dma_start(up_raw[:], w_up[:, bass.ts(i, FC)].rearrange("(k p) n -> p k n", p=P)).then_inc(s_ur, 16)
                sp.wait_ge(s_dl, i + 1)
                sp.dma_start(dn_raw[:], w_down[bass.ts(i, FC), :].rearrange("(k p) n -> p k n", p=P)).then_inc(s_dr, 16)
            if y_rows:
                nxt.store(sp)

        @block.gpsimd
        def _(pool):
            pool.sem_inc(s_ul, 1)
            pool.sem_inc(s_dl, 1)
            with pool.Fori(0, STEPS) as i:
                pool.wait_ge(s_uh, i + 1)
                pool.tensor_tensor(up_lo[:], up_raw[:], up_hi[:].bitcast(F32), ALU.subtract).then_inc(s_ul, 1)
                pool.wait_ge(s_dh, i + 1)
                pool.tensor_tensor(dn_lo[:], dn_raw[:], dn_hi[:].bitcast(F32), ALU.subtract).then_inc(s_dl, 1)

        @block.tensor
        def _(pe):
            pe.sem_inc(s_hl, 3)
            pe.sem_inc(s_de, 3)
            pe.sem_inc(s_um, 1)
            pe.sem_inc(s_dm, 1)

            def step(i, last=False):
                pe.wait_ge(s_ul, i + 2)
                for g in range(RG):
                    for f in range(NF):
                        n = g * NF + f
                        pe.wait_ge(s_hl, i * NU + n + 1)
                        for k in range(KT):
                            w = [v[:, k, f * P:(f + 1) * P] for v in (up_hi, up_lo)]
                            x = [v[:, k, g * GW:(g + 1) * GW] for v in (core.xt_hi, core.xt_lo)]
                            ins = product(pe, ups[n % 3][:, 0:GW], w, x, k == 0, k == KT - 1)
                        ins.then_inc(s_um, 1)
                pe.wait_ge(s_dl, i + 2)
                for r in range(RT):
                    if r % 3 == 0:
                        pe.wait_ge(s_hl, i * NU + NF * (r // 3 + 1) + 3)
                    for c in range(2):
                        n = 2 * r + c
                        pe.wait_ge(s_de, i * ND + n + 1)
                        for f in range(NF):
                            x = [v[:, f, r * P:(r + 1) * P] for v in (hid_hi, hid_lo)]
                            w = [v[:, f, c * HALF:(c + 1) * HALF] for v in (dn_hi, dn_lo)]
                            ins = product(pe, dns[n % 3][:], x, w, f == 0, f == NF - 1)
                        ins.then_inc(s_dm, 1)
                    if last and r >= 2:
                        nxt.tensor(pe, r - 2)

            with pe.Fori(0, STEPS - 1) as i:
                step(i)
            step(STEPS - 1, last=True)
            nxt.tensor(pe, RT - 2)
            nxt.tensor(pe, RT - 1)

        @block.scalar
        def _(act):
            act.sem_inc(s_sq, 2)

            def up_high(i):
                act.wait_ge(s_ur, i * 16 + 16)
                act.wait_ge(s_um, i * NU + 1)
                act.activation(up_hi[:], up_raw[:], ACT.Copy).then_inc(s_uh, 1)

            def step(i):
                act.wait_ge(s_dr, i * 16 + 16)
                act.wait_ge(s_dm, i * ND + 1)
                act.activation(dn_hi[:], dn_raw[:], ACT.Copy).then_inc(s_dh, 1)
                for n in range(NU):
                    g, f = n // NF, n % NF
                    act.wait_ge(s_um, i * NU + n + 2)
                    act.wait_ge(s_sq, i * NU + n + 1)
                    act.activation(rl[:, n % 2, :], ups[n % 3][:, 0:GW], ACT.Relu).then_inc(s_ue, 1)
                    act.wait_ge(s_sq, i * NU + n + 3)
                    act.activation(hid_hi[:, f, g * GW:(g + 1) * GW], sq[:, n % 2, :], ACT.Copy).then_inc(s_hh, 1)

            up_high(0)
            with act.Fori(0, STEPS - 1) as i:
                step(i)
                up_high(i + 1)
            step(STEPS - 1)
            for r in range(RT):
                act.wait_ge(s_de, (STEPS - 1) * ND + 2 * r + 5)
                nxt.scalar(act, r)
            nxt.high(act, RT - 1)

        @block.vector
        def _(dve):
            def step(i, last=False):
                def square(n):
                    dve.wait_ge(s_ue, i * NU + n + 1)
                    dve.tensor_tensor(sq[:, n % 2, :], rl[:, n % 2, :], rl[:, n % 2, :], ALU.mult).then_inc(s_sq, 1)

                def low(n):
                    g, f = n // NF, n % NF
                    dve.wait_ge(s_hh, i * NU + n + 1)
                    hi = hid_hi[:, f, g * GW:(g + 1) * GW].bitcast(F32)
                    dve.tensor_tensor(hid_lo[:, f, g * GW:(g + 1) * GW], sq[:, n % 2, :], hi,
                                      ALU.subtract).then_inc(s_hl, 1)

                for n in range(NU):
                    square(n)
                    low(n)
                for n in range(ND):
                    r, c = n // 2, n % 2
                    hc = core.h[:, r, c * HALF:(c + 1) * HALF]
                    dve.wait_ge(s_dm, i * ND + n + 2)
                    dve.tensor_tensor(hc, hc, dns[n % 3][:], ALU.add).then_inc(s_de, 1)
                    if last and c and r:
                        nxt.vector(dve, r - 1)

            with dve.Fori(0, STEPS - 1) as i:
                step(i)
            step(STEPS - 1, last=True)
            nxt.vector(dve, RT - 1)
            nxt.low(dve, RT - 1)




def prompt_attention(nc, core, tag, fox, q_rows, k_rows, v_rows, logf, cum, o_rows):
    with ExitStack() as ctx:
        sb, ps, sem = scope(core, ctx, tag)
        QT, PAIRS, TURNS = SEQ // P, 8, 4
        NM = 2 if fox else 1
        kd, qd = sb("k_dup", [P, QT, 2, 2, 64]), sb("q_dup", [P, QT, 2, 2, 64])
        vr = sb("v_rows", [P, 2, QT, P])
        khi, klo = sb("kT_hi", [P, 2, 2, SEQ], F32R), sb("kT_lo", [P, 2, 2, SEQ], F32R)
        q2 = sb("qT", [P, 2, 2, SEQ], F32R)
        pr = sb("probs", [P, 2, 2, SEQ])
        wT = sb("wT", [P, 2, NM, SEQ])
        ost = sb("o_rows", [P, 2, QT, P])
        nmx, dsum, rinv, fac = (sb(n, [P, 2 * QT]) for n in ("neg_max", "row_sum", "inv_sum", "factor"))
        ident_r, mask_r = sb("ident_r", [P, P], F32R), sb("mask_r", [P, P], F32R)
        S = [ps(f"s{m}", [P, 2, HALF]) for m in range(2)]
        T = [ps(f"t{b}", [P, HALF]) for b in range(2)]
        K = ps("kq", [P, HALF])
        FIRST = [K, T[0]]
        O = ps("o", [P, P])
        s_kt, s_ke = sem("kt"), sem("ke")
        s_kd, s_qd, s_t, s_kh, s_s, s_nm, s_e, s_f, s_w, s_pv, s_oe, s_of, s_c = (
            sem(x) for x in ("kd", "qd", "t", "kh", "s", "nm", "exp", "fac", "w", "pv", "oe", "of", "c"))
        s_vd, s_te, s_od = ([sem(f"{n}{b}") for b in range(2)] for n in ("vd", "te", "od"))
        if fox:
            q2b = sb("qT_aux", [P, 2, 2, SEQ], F32R)
            lf, c = sb("logf", [P, QT, 16]), sb("cum", [16, SEQ])
            cp = sb("cum_parts", [16, 4, SEQ], F32R)
            s_lf, s_cv, s_cd, s_qb = sem("lf"), sem("cv"), sem("cd"), sem("qb")
            s_ax = [sem("ax0"), sem("ax1")]
        block = ctx.enter_context(nc.Block())

        tiles = [QT - 1 - s % QT for s in range(2 * QT)]
        groups = [[(k, min(4, t + 1 - k)) for k in range(0, t + 1, 4)] for t in tiles]

        kq_steps = [[8 * (s // QT) + j for j in ((6, 7) if s % QT == 6 else (s % QT,) if s % QT < 6 else ())]
                    for s in range(2 * QT)]

        w_units, NU = {}, 0
        for s in range(2 * QT):
            for m in range(NM):
                w_units[s, m] = NU
                NU += len(groups[s])

        class Turn:

            def __init__(self, it, last=False):
                self.it, self.last = it, last
                self.w = w_units

            def units(self, n):
                return self.it * NU + n

            def fills(self, n):
                return self.it * (NU // 2) + n // 2

            def kq_of(self, s, m):
                units = [] if self.last and s >= QT else kq_steps[s]
                return units[-1:] if m else units[:-1]

            def has_next(self, s):
                return not (self.last and s == 2 * QT - 1)

        def kq_parts(j):
            j %= 8
            return j < 4, j % 4 // 2, 4 * (j % 2)

        @block.sync
        def _(sp):
            def load_k(p):
                v = k_rows[0:SEQ, bass.ts(p, P)].rearrange("(t p) e -> p t e", p=P)
                for m in range(2):
                    for dup in range(2):
                        sp.dma_start(kd[:, :, m, dup, :], v[:, :, m * 64:m * 64 + 64]).then_inc(s_kd, 16)

            def load_q(p):
                v = q_rows[0:SEQ, bass.ts(p, P)].rearrange("(t p) e -> p t e", p=P)
                for m in range(2):
                    for dup in range(2):
                        sp.dma_start(qd[:, :, m, dup, :], v[:, :, m * 64:m * 64 + 64]).then_inc(s_qd, 16)

            def load_v(p, par):
                sp.dma_start(vr[:, par], v_rows[0:SEQ, bass.ts(p, P)].rearrange(
                    "(t p) e -> p t e", p=P)).then_inc(s_vd[par], 16)

            def load_c(p, par):
                v = cum[bass.ds(p * 2, 2)]
                sp.dma_start(klo[64:66, par].bitcast(F32), v[:, 0:2, :].rearrange("m r k -> r m k")).then_inc(s_ax[par], 16)
                sp.dma_start(q2b[66:68, par].bitcast(F32), v[:, 2:4, :].rearrange("m r k -> r m k")).then_inc(s_ax[par], 16)

            if fox:
                sp.dma_start(lf[:], logf.rearrange("(r p) h -> p r h", p=P)).then_inc(s_lf, 16)
            load_k(0)
            load_q(0)
            load_v(0, 0)
            load_v(1, 1)
            if fox:
                sp.wait_ge(s_cv, 11)
                sp.dma_start(cum[:], cp[:].bitcast(F32)).then_inc(s_cd, 16)
                sp.wait_ge(s_cd, 16)
                load_c(0, 0)
                load_c(1, 1)
            sp.wait_ge(s_kt, 4)
            load_k(1)
            sp.wait_ge(s_kt, 8)
            load_q(1)
            with sp.Fori(0, TURNS - 1) as it:
                for par in range(2):
                    p = it * 2 + (2 + par)
                    sp.wait_ge(s_kt, it * 16 + (8 * par + 12))
                    load_k(p)
                    sp.wait_ge(s_kt, it * 16 + (8 * par + 16))
                    load_q(p)
                    if fox:
                        sp.wait_ge(s_s, it * 32 + 16 * (par + 1))
                        load_c(p, par)
                    sp.wait_ge(s_pv, it * (2 * QT * NM) + QT * NM * (par + 1))
                    load_v(p, par)

        @block.gpsimd
        def _(pool):
            pool.tensor_copy(ident_r[:], core.ident).then_inc(s_c, 1)
            m0 = C_TRI if fox else C_BLK
            pool.tensor_copy(mask_r[:], core.const[:, m0:m0 + P]).then_inc(s_c, 1)

            def store(it, par):
                pool.wait_ge(s_oe, it * (2 * QT) + (QT * (par + 1) + 1))
                pool.dma_start(o_rows[0:SEQ, bass.ts(it * 2 + par, P)].rearrange("(t p) e -> p t e", p=P),
                               ost[:, par]).then_inc(s_od[par], 16)
                pool.wait_ge(s_od[par], it * 16 + 16)
                pool.sem_inc(s_of, 1)

            with pool.Fori(0, TURNS - 1) as it:
                store(it, 0)
                store(it, 1)
            store(TURNS - 1, 0)
            store(TURNS - 1, 1)

        @block.tensor
        def _(pe):
            for s, n in ((s_te[0], 1), (s_te[1], 1), (s_ke, 1), (s_e, 2), (s_oe, 1), (s_of, 2)):
                pe.sem_inc(s, n)
            if fox:
                pe.wait_ge(s_lf, 16)
                for t in range(QT):
                    ins = pe.transpose(S[0][0:16, t // 4, (t % 4) * P:(t % 4 + 1) * P], lf[:, t, :], core.ident)
                ins.then_inc(s_cv, 1)

            def kq_unit(j, read, loaded, bank):
                keys, m, t0 = kq_parts(j)
                src = kd if keys else qd
                if j % 4 == 0:
                    pe.wait_ge(s_kd if keys else s_qd, loaded)
                pe.wait_ge(s_ke, read + 1)
                for x in range(4):
                    ins = pe.transpose(bank[:, x * P:(x + 1) * P], src[:, t0 + x, m].rearrange("p a e -> p (a e)"),
                                       core.ident)
                ins.then_inc(s_kt, 1)

            def scores(turn, s, m):
                t, par = tiles[s % (2 * QT)], s // QT % 2
                it = turn.it
                if s % QT == 0 and m == 0:
                    pe.wait_ge(s_ke, it * 16 + (s // QT * 8 + 9))
                    if fox:
                        pe.wait_ge(s_qb, it * 8 + 4 * (s // QT + 1))
                        pe.wait_ge(s_ax[par], it * 32 + (64 if s == 2 * QT else 32))
                n = (t + 1) * P
                pe.wait_ge(s_e, it * 32 + (2 * s + m + 1))
                for k0 in range(0, n, HALF):
                    w = min(HALF, n - k0)
                    last = k0 + w == n
                    out = S[m][:, k0 // HALF, 0:w]
                    pe.matmul(out, q2[:, par, m, t * P:(t + 1) * P], khi[:, par, m, k0:k0 + w],
                              start=True, stop=False)
                    ins = pe.matmul(out, (q2b if fox else q2)[:, par, m, t * P:(t + 1) * P],
                                    klo[:, par, m, k0:k0 + w], start=False, stop=True)
                    if last:
                        ins = pe.matmul(out[:, w - P:w], ident_r[:], mask_r[:], start=False, stop=True,
                                        skip_group_check=True)
                ins.then_inc(s_s, 1)

            def weights(turn, s, m):
                n0, it = turn.w[s, m], turn.it
                if fox:
                    pe.wait_ge(s_e, it * 32 + (2 * s + m + 3))
                else:
                    pe.wait_ge(s_w, it * (2 * QT) + (s + 1))
                for x, (k0, cnt) in enumerate(groups[s]):
                    b = (n0 + x) % 2
                    pe.wait_ge(s_te[b], turn.fills(n0 + x) + 1)
                    for y in range(cnt):
                        ins = pe.transpose(T[b][:, y * P:(y + 1) * P], pr[:, s % 2, m, (k0 + y) * P:(k0 + y + 1) * P],
                                           core.ident)
                    ins.then_inc(s_t, 1)

            def values(turn, s, m):
                t, par, it = tiles[s], s // QT, turn.it
                if m == 0:
                    pe.wait_ge(s_oe, it * (2 * QT) + (s + 1))
                if s % QT == 0 and m == 0:
                    pe.wait_ge(s_vd[par], it * 16 + 16)
                n0 = turn.w[s, m]
                out = O[:, 64 * m:64 * m + 64] if fox else O[:]
                for x, (k0, cnt) in enumerate(groups[s]):
                    pe.wait_ge(s_te[(n0 + x) % 2], turn.fills(n0 + x) + 2)
                    for k in range(k0, k0 + cnt):
                        v = vr[:, par, k, 64 * m:64 * m + 64] if fox else vr[:, par, k, :]
                        ins = pe.matmul(out, wT[:, s % 2, m, k * P:(k + 1) * P], v, start=k == 0, stop=k == t)
                ins.then_inc(s_pv, 1)

            def run(turn):
                for s in range(2 * QT):
                    for m in range(2):
                        if turn.has_next(s):
                            scores(turn, s + 1, m)
                        for j in turn.kq_of(s, m):
                            kq_unit(j, turn.it * 16 + (8 + j), turn.it * 128 + (128 if j < 8 else 192), K)
                        if fox or m:
                            if s:
                                values(turn, s - 1, m if fox else 0)
                            weights(turn, s, m if fox else 0)
                for m in range(NM):
                    values(turn, 2 * QT - 1, m)

            for j in range(8):
                kq_unit(j, max(j - 1, 0), 64, FIRST[j % 2])
            pe.wait_ge(s_c, 2)
            if fox:
                pe.wait_ge(s_cv, 11)
                pe.wait_ge(s_qb, 4)
                pe.wait_ge(s_ax[0], 32)
            scores(Turn(0), 0, 0)
            scores(Turn(0), 0, 1)
            with pe.Fori(0, TURNS - 1) as it:
                run(Turn(it))
            run(Turn(TURNS - 1, last=True))

        def kq_high(eng, j, done, par, bank=K):
            keys, m, t0 = kq_parts(j)
            eng.wait_ge(s_kt, done + 1)
            if fox and not keys:
                eng.activation(q2b[0:64, par, m, t0 * P:t0 * P + HALF], bank[0:64, :], ACT.Copy,
                               scale=QS).then_inc(s_qb, 1)
            eng.activation((khi if keys else q2)[:, par, m, t0 * P:t0 * P + HALF], bank[:], ACT.Copy,
                           scale=1.0 if keys else QS).then_inc(s_kh, 1)

        def kq_low(eng, j, done, par, bank=K):
            keys, m, t0 = kq_parts(j)
            cols = slice(t0 * P, t0 * P + HALF)
            eng.wait_ge(s_kh, done + 1)
            if keys:
                rows = slice(0, 64) if fox else slice(0, P)
                ins = eng.tensor_tensor(klo[rows, par, m, cols], bank[rows, :], khi[rows, par, m, cols].bitcast(F32),
                                        ALU.subtract)
            else:
                q = q2[64:P, par, m, cols]
                ins = eng.scalar_tensor_tensor(q, bank[64:P, :], QS, q.bitcast(F32), ALU.mult, ALU.subtract)
            ins.then_inc(s_ke, 1)

        def weights_out(eng, copy, turn, s, m, mine):
            for x, (k0, cnt) in enumerate(groups[s]):
                n = turn.w[s, m] + x
                if mine(n):
                    eng.wait_ge(s_t, turn.units(n) + 1)
                    copy(wT[:, s % 2, m, k0 * P:(k0 + cnt) * P], T[n % 2][:, 0:cnt * P]).then_inc(s_te[n % 2], 1)

        @block.scalar
        def _(act):
            def exp(turn, s, m):
                n, col = (tiles[s % (2 * QT)] + 1) * P, 2 * (s % QT) + m
                act.wait_ge(s_nm, turn.it * 32 + (2 * s + m + 1))
                act.activation(pr[:, s % 2, m, 0:n], S[m][:].rearrange("p a b -> p (a b)")[:, 0:n], ACT.Exp,
                               bias=nmx[:, col:col + 1], accum_out=dsum[:, col:col + 1]).then_inc(s_e, 1)

            def copy(o, x):
                return act.activation(o, x, ACT.Copy)

            def run(turn):
                for s in range(2 * QT):
                    for m in range(2):
                        for j in turn.kq_of(s, m):
                            kq_high(act, j, turn.it * 16 + (8 + j), (j // 8 + 1) % 2)
                        if turn.has_next(s):
                            exp(turn, s + 1, m)
                        if fox or m:
                            weights_out(act, copy, turn, s, m if fox else 0, lambda n: not fox or n % 2 == 0)

            for j in range(8):
                kq_high(act, j, j, 0, FIRST[j % 2])
            exp(Turn(0), 0, 0)
            exp(Turn(0), 0, 1)
            with act.Fori(0, TURNS - 1) as it:
                run(Turn(it))
            run(Turn(TURNS - 1, last=True))

        @block.vector
        def _(dve):
            if fox:
                k_one, q_one = (core.const[64:P, C_AUX + x:C_AUX + x + 1].to_broadcast([64, 4 * SEQ]) for x in range(2))
                dve.tensor_copy(klo[64:P].rearrange("p a b c -> p (a b c)"), k_one).then_inc(s_c, 1)
                dve.tensor_copy(q2b[64:P].rearrange("p a b c -> p (a b c)"), q_one).then_inc(s_c, 1)

            def cumulate():
                zero = pr[0:16, 0, 0, :]
                dve.memset(zero, 0.0).then_inc(s_cv, 1)
                dve.wait_ge(s_cv, 2)
                dve.tensor_copy(c[:], S[0][0:16, :, :].rearrange("p a b -> p (a b)")).then_inc(s_cv, 1)
                dve.wait_ge(s_cv, 3)
                dve.tensor_tensor_scan(c[:], c[:], zero, 0.0, ALU.add, ALU.add).then_inc(s_cv, 1)
                dve.wait_ge(s_cv, 4)
                dve.tensor_copy(cp[:, 2, :], c[:]).then_inc(s_cv, 1)
                dve.wait_ge(s_cv, 5)
                dve.tensor_tensor(cp[:, 3, :], c[:], cp[:, 2, :].bitcast(F32), ALU.subtract).then_inc(s_cv, 1)
                dve.wait_ge(s_cv, 6)
                dve.tensor_scalar(cp[:, 0, :], cp[:, 2, :].bitcast(F32), -1.0, None, ALU.mult).then_inc(s_cv, 1)
                dve.tensor_scalar(cp[:, 1, :], cp[:, 3, :].bitcast(F32), -1.0, None, ALU.mult).then_inc(s_cv, 1)
                dve.wait_ge(s_cv, 8)
                dve.wait_ge(s_c, 4)
                dve.memset(zero, 0.0).then_inc(s_cv, 3)

            def maximum(turn, s, m):
                n, col = (tiles[s % (2 * QT)] + 1) * P, 2 * (s % QT) + m
                dve.wait_ge(s_s, turn.it * 32 + (2 * s + m + 1))
                dve.tensor_reduce(nmx[:, col:col + 1], S[m][:].rearrange("p a b -> p (a b)")[:, 0:n],
                                  AX, ALU.max, negate=True).then_inc(s_nm, 1)

            def combine(turn, s):
                d = s % QT
                dve.wait_ge(s_e, turn.it * 32 + (2 * s + 4))
                dve.reciprocal(rinv[:, 2 * d:2 * d + 2], dsum[:, 2 * d:2 * d + 2]).then_inc(s_f, 1)
                if fox:
                    return
                n = (tiles[s] + 1) * P
                dve.wait_ge(s_f, turn.it * (4 * QT) + (2 * s + 1))
                dve.tensor_scalar(fac[:, d:d + 1], dsum[:, 2 * d:2 * d + 1], rinv[:, 2 * d + 1:2 * d + 2],
                                  core.neglam[:, 0:1], ALU.mult, ALU.mult).then_inc(s_f, 1)
                dve.wait_ge(s_f, turn.it * (4 * QT) + (2 * s + 2))
                dve.scalar_tensor_tensor(pr[:, s % 2, 0, 0:n], pr[:, s % 2, 1, 0:n], fac[:, d:d + 1],
                                         pr[:, s % 2, 0, 0:n], ALU.mult, ALU.add).then_inc(s_w, 1)

            def outputs(turn, s):
                t, d, par, it = tiles[s], s % QT, s // QT, turn.it
                dve.wait_ge(s_pv, it * (2 * QT * NM) + (s + 1) * NM)
                if d == 0:
                    dve.wait_ge(s_of, it * 2 + (par + 1))
                if fox:
                    dve.wait_ge(s_f, it * (2 * QT) + (s + 1))
                    dve.tensor_tensor(ost[:, par, t, :].rearrange("p (s e) -> p s e", s=2),
                                      O[:].rearrange("p (s e) -> p s e", s=2),
                                      rinv[:, 2 * d:2 * d + 2].unsqueeze(2).to_broadcast([P, 2, 64]),
                                      ALU.mult).then_inc(s_oe, 1)
                else:
                    dve.tensor_scalar(ost[:, par, t, :], O[:], rinv[:, 2 * d:2 * d + 1], None,
                                      ALU.mult).then_inc(s_oe, 1)

            def run(turn):
                for s in range(2 * QT):
                    for m in range(2):
                        if turn.has_next(s):
                            maximum(turn, s + 1, m)
                        for j in turn.kq_of(s, m):
                            kq_low(dve, j, turn.it * 16 + (8 + j), (j // 8 + 1) % 2)
                        if fox:
                            weights_out(dve, dve.tensor_copy, turn, s, m, lambda n: n % 2 == 1)
                        if not m:
                            combine(turn, s)
                    if s:
                        outputs(turn, s - 1)
                outputs(turn, 2 * QT - 1)

            if fox:
                cumulate()
            for j in range(8):
                kq_low(dve, j, j, 0, FIRST[j % 2])
            maximum(Turn(0), 0, 0)
            maximum(Turn(0), 0, 1)
            with dve.Fori(0, TURNS - 1) as it:
                run(Turn(it))
            run(Turn(TURNS - 1, last=True))




def decode_attention(nc, core, tag, fox, q_rows, k_new, v_new, k_cache, v_cache, logf_new, logf_cache, cum, o_rows):
    with ExitStack() as ctx:
        sb, ps, sem = scope(core, ctx, tag)
        KR = VR = 4
        kr, vr = sb("k_tiles", [P, KR, D]), sb("v_tiles", [P, VR, D])
        nr, vn = sb("new_rows", [P, 2, D]), sb("v_new", [P, D])
        nT = sb("new_T", [P, 2, KT, P])
        qbd = sb("q_diag", [P, KT, 32])
        kT = sb("kT", [P, 2, KT, P])
        sc = sb("scores", [P, 2, NKEY])
        pr = sb("probs", [P, 2, NKEY])
        pT = sb("probs_T", [P, CT + 1, 2, P])
        obd = sb("o_diag", [P, 2, P])
        oo = sb("o_out", [16, D])
        mx, nmx, ds, coef = sb("max", [P, 2]), sb("neg_max", [P, 2]), sb("sum", [P, 2]), sb("coef", [P, 2])
        KB = [ps(f"kb{x}", [P, 4, P]) for x in range(2)]
        SB = [ps(f"sb{x}", [P, 2, 2, P]) for x in range(2)]
        PB = [ps(f"pb{x}", [P, 2, 2, P]) for x in range(2)]
        OB = [ps(f"ob{x}", [P, P]) for x in range(2)]
        s_new, s_nt, s_ne, s_qb, s_ktr, s_qk, s_sm, s_mx, s_nm, s_e, s_cf, s_ptr, s_pv, s_oe, s_sel, s_st = (
            sem(x) for x in ("new", "nt", "ne", "qb", "ktr", "qk", "sm", "mx", "nm", "exp", "cf", "ptr", "pv", "oe",
                             "sel", "st"))
        s_kd, s_vd = [sem(f"kd{x}") for x in range(KR)], [sem(f"vd{x}") for x in range(VR)]
        s_ke, s_se, s_pe = ([sem(f"{n}{x}") for x in range(2)] for n in ("ke", "se", "pe"))
        s_oo = sem("oo")
        if fox:
            lf = sb("logf", [P, CT, P])
            lfn, lbd = sb("logf_new", [P, 16]), sb("logf_diag", [P, P])
            ca = sb("cum", [P, NKEY])
            zero = sb("zeros", [P, PAST])
            cn = sb("cum_new", [P, NQ])
            cb = sb("key_bias", [16, NB, NKEY])
            hs = sb("head_rows", [16, 2, P])
            s_lf, s_ct, s_cv, s_cd = sem("lf"), sem("ct"), sem("cv"), sem("cd")
        block = ctx.enter_context(nc.Block())
        W0 = C_WIN[1] if fox else C_WIN[0]
        SU, PU = (3, 2), (4, 3)

        @block.sync
        def _(sp):
            sp.dma_start(nr[:, 0, :], q_rows).then_inc(s_new, 16)
            sp.dma_start(nr[:, 1, :], k_new).then_inc(s_new, 16)
            if fox:
                sp.dma_start(lfn[:], logf_new).then_inc(s_lf, 16)
                sp.dma_start(hs[:].rearrange("a g p -> a (g p)"), core.hsel[:, 2048:NHSEL]).then_inc(s_lf, 16)
                for b in range(NB):
                    sp.dma_start(lf[:, :, b * 16:(b + 1) * 16],
                                 logf_cache[b].rearrange("(t p) h -> p t h", p=P)).then_inc(s_lf, 16)
                sp.wait_ge(s_cv, 8)
                sp.dma_start(cum, ca[:]).then_inc(s_cd, 16)
                sp.wait_ge(s_cd, 16)
                sp.dma_start(cb[:], cum.rearrange("(b h) k -> h b k", h=16)).then_inc(s_cd, 16)

            def load_k(b, t):
                sp.wait_ge(s_ktr, b * 16 + 2 * t + 2)
                sp.dma_start(kr[:, t % KR, :], k_cache[bass.ds(b * CT + t, 1)].rearrange("a p n -> (a p) n"))\
                    .then_inc(s_kd[t % KR], 16)

            def load_v(b, t):
                sp.wait_ge(s_pv, b * (CT + 1) + (t + 2 if t >= VR else t + 1))
                sp.dma_start(vr[:, t % VR, :], v_cache[bass.ds(b * CT + t, 1)].rearrange("a p n -> (a p) n"))\
                    .then_inc(s_vd[t % VR], 16)

            for t in range(CT):
                load_k(0, t)
            with sp.Fori(1, NB) as b:
                for t in range(CT):
                    load_k(b, t)
                    load_v(b - 1, t)
            for t in range(CT):
                load_v(NB - 1, t)
            sp.wait_ge(s_st, 16 * NB + 16)

        @block.gpsimd
        def _(pool):
            pool.memset(qbd[:], 0.0).then_inc(s_qb, 1)
            pool.wait_ge(s_qb, 1)
            pool.wait_ge(s_ne, 4)
            with pool.Fori(0, NB) as b:
                pool.wait_ge(s_sm, b + 1)
                for m in range(2):
                    rows = slice(64 * m, 64 * m + 64)
                    pool.tensor_copy(qbd[rows, :, 16 * m:16 * m + 16], nT[rows, 0, :, bass.ts(b, NQ)]).then_inc(s_qb, 1)

        @block.tensor
        def _(pe):
            for s, n in ((s_ktr, 2 * KR), (s_qk, 2), (s_pv, VR + 1), (s_sm, 1), (s_e, 1),
                         (s_sel, 1), (s_ptr, 1), (s_cf, 1), (s_ke[0], 1), (s_ke[1], 1), (s_se[0], 1),
                         (s_se[1], 1), (s_pe[0], 1), (s_pe[1], 1), (s_oe, 1), (s_oo, 1)):
                pe.sem_inc(s, n)
            pe.wait_ge(s_new, 32)
            for x in range(2):
                for g in range(2):
                    if x:
                        pe.wait_ge(s_ne, g + 1)
                    for c_ in range(4):
                        ins = pe.transpose(KB[g][:, c_, :], nr[:, x, (4 * g + c_) * P:(4 * g + c_ + 1) * P], core.ident)
                    ins.then_inc(s_nt, 1)
            if fox:
                pe.wait_ge(s_lf, 160)
                for t in range(CT):
                    ins = pe.transpose(SB[t // 4][:].rearrange("p a b c -> p (a b c)")[:, (t % 4) * P:(t % 4 + 1) * P],
                                       lf[:, t, :], core.ident)
                ins.then_inc(s_ct, 1)
                pe.wait_ge(s_cv, 2)
                pe.matmul(OB[0][:, 0:NQ], lbd[:], core.const[:, C_FRAME:C_FRAME + NQ],
                          start=True, stop=True).then_inc(s_ct, 1)
                pe.wait_ge(s_cd, 32)
                pe.wait_ge(s_cv, 8)
            pe.wait_ge(s_ne, 4)

            def keys(b, t):
                pe.wait_ge(s_kd[t % KR], b * 32 + 16 * (t // KR + 1))
                for g in range(2):
                    pe.wait_ge(s_ke[g], b * CT + t + 1)
                    for c_ in range(4):
                        ins = pe.transpose(KB[g][:, c_, :], kr[:, t % KR, (4 * g + c_) * P:(4 * g + c_ + 1) * P],
                                           core.ident)
                    ins.then_inc(s_ktr, 1)

            def scores(b, t):
                pair = t // 2
                bank, use = pair % 2, pair // 2
                if t % 2 == 0:
                    pe.wait_ge(s_se[bank], b * SU[bank] + use + 1)
                if t == 0:
                    pe.wait_ge(s_qb, b * 2 + 3)
                if t < CT:
                    for g in range(2):
                        pe.wait_ge(s_ke[g], b * CT + t + 2)
                for g in range(2):
                    out = SB[bank][:, t % 2, g, :]
                    for j in range(4):
                        k = kT[:, t % 2, 4 * g + j, :] if t < CT else nT[:, 1, 4 * g + j, :]
                        ins = pe.matmul(out[32 * j:32 * j + 32, :], qbd[:, 4 * g + j, :], k,
                                        start=True, stop=not fox and t < CT, skip_group_check=True)
                    if t == CT:
                        ins = pe.matmul(out, core.ident, core.const[:, bass.ds(b * -16 + (W0 + 112), P)],
                                        start=False, stop=not fox, skip_group_check=True)
                    if fox:
                        ins = pe.matmul(out, hs[:, g, :], cb[:, bass.ds(b, 1), t * P:(t + 1) * P].rearrange(
                            "h a k -> h (a k)"), start=False, stop=True, skip_group_check=True)
                ins.then_inc(s_qk if t < CT else s_sm, 1)

            def probs(b, pair):
                bank, use = pair % 2, pair // 2
                pe.wait_ge(s_pe[bank], b * PU[bank] + use + 1)
                if pair == 0:
                    pe.wait_ge(s_e, b * 2 + 3)
                for t in range(2 * pair, min(2 * pair + 2, CT + 1)):
                    for g in range(2):
                        ins = pe.transpose(PB[bank][:, t % 2, g, :], pr[:, g, t * P:(t + 1) * P], core.ident)
                ins.then_inc(s_ptr, 1)

            def values(b, t):
                pair = t // 2
                if t == 0:
                    pe.wait_ge(s_oe, b + 1)
                    pe.wait_ge(s_st, 16)
                if t % 2 == 0:
                    pe.wait_ge(s_pe[pair % 2], b * PU[pair % 2] + pair // 2 + 2)
                if t < CT:
                    pe.wait_ge(s_vd[t % VR], b * 32 + 16 * (t // VR + 1))
                for g in range(2):
                    for j in range(4):
                        cols = slice((4 * g + j) * P, (4 * g + j + 1) * P)
                        v = vr[:, t % VR, cols] if t < CT else vn[:, cols]
                        ins = pe.matmul(OB[g][32 * j:32 * j + 32, :], pT[:, t, g, 32 * j:32 * j + 32], v,
                                        start=t == 0, stop=t == CT)
                ins.then_inc(s_pv, 1)

            def select(b):
                pe.wait_ge(s_oe, b + 2)
                for g in range(2):
                    out = PB[g][:].rearrange("p a b c -> p (a b c)")
                    pe.wait_ge(s_pe[g], b * PU[g] + PU[g])
                    for j in range(4):
                        if fox:
                            for s in range(2):
                                c0 = C_SELB + (j * 2 + s) * 16
                                ins = pe.matmul(out[0:16, j * P + 64 * s:j * P + 64 * s + 64],
                                                core.const[:, c0:c0 + 16], obd[:, g, 64 * s:64 * s + 64],
                                                start=True, stop=True)
                        else:
                            c0 = C_SELA + j * 16
                            ins = pe.matmul(out[0:16, j * P:(j + 1) * P], core.const[:, c0:c0 + 16], obd[:, g, :],
                                            start=True, stop=True)
                    ins.then_inc(s_sel, 1)

            def stream(bs, bv):
                if bs is not None:
                    keys(bs, 0)
                if bv is not None:
                    probs(bv, 0)
                for t in range(CT + 1):
                    if bs is not None:
                        if t + 1 < CT:
                            keys(bs, t + 1)
                        scores(bs, t)
                    if bv is not None:
                        if t % 2 == 1:
                            probs(bv, t // 2 + 1)
                        values(bv, t)
                if bv is not None:
                    select(bv)

            stream(0, None)
            with pe.Fori(1, NB) as b:
                stream(b, b - 1)
            stream(None, NB - 1)

        def evacuation(eng, copy, half):
            other = 1 - half

            def keys(b, t):
                eng.wait_ge(s_ktr, b * 16 + (2 * t + half + 1 + 2 * KR))
                eng.wait_ge(s_qk, b * CT + t + 1)
                copy(kT[:, t % 2, 4 * half:4 * half + 4, :], KB[half][:]).then_inc(s_ke[half], 1)

            def scores(b, pair):
                if pair % 2 != half:
                    return
                n = 2 if pair < CT // 2 else 1
                if n == 2:
                    eng.wait_ge(s_qk, b * CT + 2 * pair + 2 + 2)
                else:
                    eng.wait_ge(s_sm, b + 2)
                if pair < 2:
                    eng.wait_ge(s_e, b * 2 + 1)
                dst = sc[:, :, 2 * pair * P:(2 * pair + n) * P].rearrange("p g (t k) -> p t g k", t=n)
                for x in range(n):
                    ins = copy(dst[:, x], SB[half][:, x])
                ins.then_inc(s_se[half], 1)

            def probs(b, pair):
                if pair % 2 != other:
                    return
                n = 2 if pair < CT // 2 else 1
                eng.wait_ge(s_ptr, b * 5 + pair + 2)
                if pair < 2:
                    eng.wait_ge(s_pv, b * (CT + 1) + VR + 1)
                copy(pT[:, 2 * pair:2 * pair + n], PB[other][:, 0:n]).then_inc(s_pe[other], 1)

            def selected(b):
                eng.wait_ge(s_sel, b * 2 + other + 2)
                eng.wait_ge(s_st, b * 16 + 16)
                copy(oo[:, other * HALF:(other + 1) * HALF],
                     PB[other][:].rearrange("p a b c -> p (a b c)")[0:16, :]).then_inc(s_pe[other], 1)

            def stream(bs, bv, outputs):
                if bs is not None:
                    keys(bs, 0)
                if bv is not None:
                    probs(bv, 0)
                for t in range(CT + 1):
                    if bs is not None:
                        if t + 1 < CT:
                            keys(bs, t + 1)
                        if t % 2 == 1 or t == CT:
                            scores(bs, t // 2)
                    if bv is not None and t % 2 == 1:
                        probs(bv, t // 2 + 1)
                if bv is not None:
                    outputs(bv)
                    selected(bv)

            return stream

        @block.scalar
        def _(act):
            def copy(o, x):
                return act.activation(o, x, ACT.Copy)

            def outputs(b):
                act.wait_ge(s_pv, b * (CT + 1) + (CT + 2 + VR))
                act.wait_ge(s_cf, b * 2 + 3)
                act.wait_ge(s_sel, b * 2 + 1)
                for g in range(2):
                    ins = act.activation(obd[:, g, :], OB[g][:], ACT.Copy, scale=coef[:, g:g + 1])
                ins.then_inc(s_oe, 1)

            def exps(b):
                for g in range(2):
                    act.wait_ge(s_nm, b * 2 + g + 1)
                    act.wait_ge(s_ptr, b * 5 + 1)
                    act.wait_ge(s_cf, b * 2 + 1)
                    act.activation(pr[:, g, :], sc[:, g, :], ACT.Exp, bias=nmx[:, g:g + 1], scale=QS,
                                   accum_out=ds[:, g:g + 1]).then_inc(s_e, 1)

            act.dma_start(vn[:], v_new).then_inc(s_st, 16)
            for x in range(2):
                act.wait_ge(s_nt, 2 * x + 1)
                copy(nT[:, x, 0:4, :], KB[0][:]).then_inc(s_ne, 1)
                act.wait_ge(s_nt, 2 * x + 2)
                copy(nT[:, x, 4:8, :], KB[1][:]).then_inc(s_ne, 1)
            stream = evacuation(act, copy, 0)

            def store(b):
                for g in range(2):
                    act.wait_ge(s_pe[g], b * PU[g] + PU[g] + 1)
                act.dma_start(o_rows[bass.ds(b * NQ + SEQ, NQ), :], oo[:]).then_inc(s_st, 16)

            stream(0, None, outputs)
            exps(0)
            with act.Fori(1, NB) as b:
                stream(b, b - 1, outputs)
                store(b - 1)
                exps(b)
            stream(None, NB - 1, outputs)
            store(NB - 1)

        @block.vector
        def _(dve):
            if fox:
                dve.memset(zero[:], 0.0).then_inc(s_cv, 1)
                dve.wait_ge(s_lf, 160)
                dve.tensor_tensor(lbd[:].rearrange("p (b h) -> p b h", h=16),
                                  lfn[:].unsqueeze(1).to_broadcast([P, NB, 16]),
                                  core.const[:, C_STREAM:C_STREAM + NB].unsqueeze(2).to_broadcast([P, NB, 16]),
                                  ALU.mult).then_inc(s_cv, 1)
                dve.wait_ge(s_ct, 1)
                for x in range(2):
                    dve.wait_ge(s_cv, 2 + x)
                    src = SB[x][:].rearrange("p a b c -> p (a b c)")
                    dve.tensor_tensor_scan(ca[:, x * HALF:(x + 1) * HALF], src, zero[:, 0:HALF],
                                           ca[:, HALF - 1:HALF] if x else 0.0, ALU.add, ALU.add).then_inc(s_cv, 1)
                dve.wait_ge(s_ct, 2)
                dve.wait_ge(s_cv, 4)
                dve.tensor_tensor_scan(cn[:], OB[0][:, 0:NQ], zero[:, 0:NQ], 0.0, ALU.add, ALU.add).then_inc(s_cv, 1)
                dve.wait_ge(s_cv, 5)
                dve.tensor_copy(mx[:, 0:1], ca[:, PAST - 1:PAST]).then_inc(s_cv, 1)
                dve.wait_ge(s_cv, 6)
                dve.tensor_scalar(ca[:, 0:PAST], ca[:, 0:PAST], mx[:, 0:1], -1.0 / QS, ALU.subtract,
                                  ALU.mult).then_inc(s_cv, 1)
                dve.wait_ge(s_cv, 7)
                dve.scalar_tensor_tensor(ca[:, PAST:NKEY].rearrange("p (b q) -> p b q", q=NQ),
                                         cn[:].unsqueeze(1).to_broadcast([P, NB, NQ]), -1.0 / QS,
                                         core.const[:, C_STREAM:C_STREAM + NB].unsqueeze(2).to_broadcast([P, NB, NQ]),
                                         ALU.mult, ALU.mult).then_inc(s_cv, 1)

            def maxima(b):
                for x in range(2):
                    dve.wait_ge(s_se[x], b * SU[x] + SU[x] + 1)
                for g in range(2):
                    dve.tensor_reduce(mx[:, g:g + 1], sc[:, g, :], AX, ALU.max).then_inc(s_mx, 1)
                for g in range(2):
                    dve.wait_ge(s_mx, b * 2 + g + 1)
                    dve.tensor_scalar(nmx[:, g:g + 1], mx[:, g:g + 1], -QS, None, ALU.mult).then_inc(s_nm, 1)

            def coefficients(b):
                dve.wait_ge(s_e, b * 2 + 3)
                dve.wait_ge(s_oe, b + 1)
                dve.reciprocal(coef[:], ds[:]).then_inc(s_cf, 2 if fox else 1)
                if not fox:
                    dve.wait_ge(s_cf, b * 2 + 2)
                    dve.tensor_scalar(coef[:], coef[:], core.lamcol[:, 0:1], None, ALU.mult).then_inc(s_cf, 1)

            stream = evacuation(dve, dve.tensor_copy, 1)
            stream(0, None, lambda b: None)
            maxima(0)
            coefficients(0)
            with dve.Fori(1, NB) as b:
                stream(b, b - 1, lambda b: None)
                maxima(b)
                coefficients(b)
            stream(None, NB - 1, lambda b: None)




def stream_step(nc, a, o, stop=99):
    xp = a["x_prompt"].rearrange("a s d -> (a s) d")
    xs = a["x_sample"].rearrange("b s d -> (b s) d")
    yp = o["y_prompt"].rearrange("a s d -> (a s) d")
    ys = o["y_sample"].rearrange("b s d -> (b s) d")
    kv = {}
    for n in ("ak_p", "av_p", "ak_s", "av_s"):
        kv[n] = o[n].rearrange("n b s h e -> (n b s) (h e)")
    for n in ("bk_p", "bv_p", "bk_s", "bv_s"):
        kv[n] = o[n].rearrange("b s h e -> (b s) (h e)")
    fp, fs = (o[n].rearrange("b s h -> (b s) h") for n in ("bf_p", "bf_s"))
    cak = a["cache_a_k"].rearrange("n b (t p) h e -> (n b t) p (h e)", p=P)
    cav = a["cache_a_v"].rearrange("n b (t p) h e -> (n b t) p (h e)", p=P)
    cbk = a["cache_b_k"].rearrange("b (t p) h e -> (b t) p (h e)", p=P)
    cbv = a["cache_b_v"].rearrange("b (t p) h e -> (b t) p (h e)", p=P)
    q = nc.dram_tensor("q_scratch", [ROWS, D], F32).ap()
    ao = nc.dram_tensor("o_scratch", [ROWS, D], F32).ap()
    cum = nc.dram_tensor("cum_scratch", [P, NKEY], F32).ap()
    cum_parts = nc.dram_tensor("cum_parts_scratch", [16, 4, SEQ], F32).ap()
    qd = (q[0:SEQ, :], q[SEQ:ROWS, :])
    with ExitStack() as ctx:
        core = Core(nc, ctx, a["head_sel"])
        start_phase(nc, core, xp, xs, a["const"],
                    [a[n] for n in ("lambda_q1", "lambda_k1", "lambda_q2", "lambda_k2")])
        wa = a["w_qkv_a"].rearrange("n d e -> (n d) e")
        with ExitStack() as rows:
            core.normed_rows(rows, "a")
            dense_phase(nc, core, "qkv", "rms", a["norm_attn"][0, :], None,
                        [(wa, c, "rope", (*qd, c)) for c in (0, HALF)]
                        + [(wa, D + c, "rope", (kv["ak_p"], kv["ak_s"], c)) for c in (0, HALF)]
                        + [(wa, 2 * D + c, "store", (kv["av_p"], kv["av_s"], c)) for c in (0, HALF)])
        if stop <= 1:
            return
        prompt_attention(nc, core, "pa", False, q, kv["ak_p"], kv["av_p"], None, None, ao)
        if stop <= 2:
            return
        decode_attention(nc, core, "da", False, q[SEQ:ROWS, :], kv["ak_s"], kv["av_s"], cak, cav, None, None, None, ao)
        if stop <= 3:
            return
        with ExitStack() as rows:
            core.normed_rows(rows, "b")
            dense_phase(nc, core, "oa", "head", a["subln_a"][0, :], ao,
                        [(a["w_o_a"].rearrange("n d e -> (n d) e"), c, "add", c) for c in (0, HALF)],
                        following=a["norm_mlp"][0, :])
            mlp_phase(nc, core, "m0", a["w_up"][0], a["w_down"][0], a["norm_kv"])
            if stop <= 4:
                return
            core.clear_semaphores()
            w = a["w_kvf"]
            dense_phase(nc, core, "kv", None, None, None,
                        [(w, c, "store", (kv["bk_p"], kv["bk_s"], c)) for c in (0, HALF)]
                        + [(w, D + c, "store", (kv["bv_p"], kv["bv_s"], c)) for c in (0, HALF)],
                        forget=(w[:, 2 * D:2 * D + 16], a["b_f"], fp, fs), following=a["norm_attn"][1, :])
            dense_phase(nc, core, "qb", None, None, None,
                        [(a["w_q_b"].rearrange("n d e -> (n d) e"), c, "store", (*qd, c)) for c in (0, HALF)])
        if stop <= 5:
            return
        prompt_attention(nc, core, "pb", True, q, kv["bk_p"], kv["bv_p"], fp, cum_parts, ao)
        decode_attention(nc, core, "db", True, q[SEQ:ROWS, :], kv["bk_s"], kv["bv_s"], cbk, cbv, fs,
                         a["cache_b_logf"], cum, ao)
        if stop <= 6:
            return
        with ExitStack() as rows:
            core.normed_rows(rows, "c")
            dense_phase(nc, core, "ob", "plain", None, ao,
                        [(a["w_o_b"].rearrange("n d e -> (n d) e"), c, "add", c) for c in (0, HALF)],
                        following=a["norm_mlp"][1, :])
            mlp_phase(nc, core, "m1", a["w_up"][1], a["w_down"][1], a["norm_final"],
                      lambda r: rows_of(yp, ys, r))
        core.clear_semaphores()


_INS = ["x_prompt", "x_sample", "cache_a_k", "cache_a_v", "cache_b_k", "cache_b_v", "cache_b_logf", "norm_attn",
        "norm_mlp", "w_qkv_a", "lambda_q1", "lambda_k1", "lambda_q2", "lambda_k2", "subln_a", "w_o_a", "norm_kv",
        "w_kvf", "b_f", "w_q_b", "w_o_b", "w_up", "w_down", "norm_final"]
_OUTS = {"y_prompt": (1, SEQ, D), "y_sample": (NB, NQ, D), "ak_p": (1, 1, SEQ, 16, 64), "av_p": (1, 1, SEQ, 8, 128),
         "bk_p": (1, SEQ, 16, 64), "bv_p": (1, SEQ, 16, 64), "bf_p": (1, SEQ, 16),
         "ak_s": (1, NB, NQ, 16, 64), "av_s": (1, NB, NQ, 8, 128),
         "bk_s": (NB, NQ, 16, 64), "bv_s": (NB, NQ, 16, 64), "bf_s": (NB, NQ, 16)}


def kernel(**inputs):
    import numpy as _np
    import concourse.bacc as _bacc
    from concourse import mybir as _mybir
    from concourse.bass_utils import run_bass_kernel_spmd as _run

    nc = _bacc.Bacc("TRN2", target_bir_lowering=False, num_devices=1)
    table, head_sel = constant_tables()
    arrays, a, o = {}, {}, {}
    for name, x in [(n, inputs[n]) for n in _INS] + [("const", table), ("head_sel", head_sel)]:
        x = _np.ascontiguousarray(x)
        arrays[f"in_{name}"] = x
        a[name] = nc.dram_tensor(f"in_{name}", x.shape, _mybir.dt.from_np(x.dtype), kind="ExternalInput").ap()
    for name, shape in _OUTS.items():
        o[name] = nc.dram_tensor(f"out_{name}", shape, F32, kind="ExternalOutput").ap()
    stream_step(nc, a, o)
    r = _run(nc, [arrays], core_ids=[0])
    return tuple(r.results[0][f"out_{name}"] for name in _OUTS)
```

```python
from contextlib import ExitStack

import numpy as np

import concourse.bass as bass
from concourse import mybir

F32 = mybir.dt.float32
F32R = mybir.dt.float32r
ALU = mybir.AluOpType
ACT = mybir.ActivationFunctionType
AX = mybir.AxisListType.X

P = 128
D = 1024
KT = D // P
SEQ = 1024
RT = SEQ // P + 1
ROWS = RT * P
NB, NQ = 8, 16
PAST = 1024
CT = PAST // P
NKEY = PAST + P
DFF = 4096
FC = 256
EPS = 1e-6
NEG = -1e30
QS = 64.0 ** -0.5
HALF = 512

C_IDENT, C_BLK, C_TRI = 0, 128, 256
C_WIN = (384, 384 + 240)
C_SELA = 864
C_SELB = C_SELA + 64
C_STREAM = C_SELB + 128
C_FRAME = C_STREAM + 8
C_LAM = C_FRAME + 16
C_ROPE = C_LAM + 2
C_AUX = C_ROPE + RT * 64
NCONST = C_AUX + 2
NHSEL = 2 * 128


def constant_tables():
    p = np.arange(P)
    t = np.zeros((P, NCONST), np.float32)
    t[:, C_IDENT:C_IDENT + P] = np.eye(P)
    t[:, C_BLK:C_BLK + P] = np.where(p[None] // 64 <= p[:, None] // 64, 0, NEG)
    t[:, C_TRI:C_TRI + P] = np.where(p[None] <= p[:, None], 0, NEG)
    j, m, q = p // 32, p // 16 % 2, p % 16
    c = np.arange(240)[None] - 112
    t[:, C_WIN[0]:C_WIN[0] + 240] = np.where((c >= 0) & (c < NQ), 0, NEG)
    t[:, C_WIN[1]:C_WIN[1] + 240] = np.where((c >= 0) & (c <= q[:, None]), 0, NEG)
    for a in range(4):
        for f in range(NQ):
            t[:, C_SELA + a * 16 + f] = (j == a) & (q == f)
            for s in range(2):
                t[:, C_SELB + (a * 2 + s) * 16 + f] = (j == a) & (q == f) & (m == s)
    for b in range(8):
        t[:, C_STREAM + b] = p // 16 == b
    for f in range(NQ):
        t[:, C_FRAME + f] = q == f
    t[:, C_LAM] = m == 0
    t[:, C_LAM + 1] = -(m == 1).astype(np.float32)
    t[66:68, C_AUX] = 1
    t[64:66, C_AUX + 1] = 1
    inv = np.power(np.float32(10000.0), -np.arange(32, dtype=np.float32) / np.float32(32))
    for r in range(RT):
        pos = (r * P + p if r < RT - 1 else PAST + q).astype(np.float32)
        ang = (pos[:, None] * inv[None]).astype(np.float32)
        t[:, C_ROPE + r * 64:C_ROPE + r * 64 + 32] = np.cos(ang)
        t[:, C_ROPE + r * 64 + 32:C_ROPE + r * 64 + 64] = np.sin(ang)
    h = np.zeros((16, NHSEL), np.float32)
    for a in range(16):
        for g in range(2):
            h[a, g * 128:(g + 1) * 128] = 2 * (4 * g + j) + m == a
    return t, h


class Core:

    def __init__(self, nc, ctx, hsel, x_prompt, x_sample):
        self.nc, self.hsel, self.sems = nc, hsel, []
        self.x = x_prompt, x_sample
        self.s_row = [nc.alloc_semaphore(name=f"row{r}") for r in range(RT)]
        self.sems += self.s_row
        self.h = ctx.enter_context(nc.sbuf_tensor("h_rows", [P, RT, D], F32))
        self.const = ctx.enter_context(nc.sbuf_tensor("const_sb", [P, NCONST], F32))
        self.ident = self.const[:, C_IDENT:C_IDENT + P]
        self.neglam = ctx.enter_context(nc.sbuf_tensor("neglam", [P, 1], F32))
        self.lamcol = ctx.enter_context(nc.sbuf_tensor("lamcol", [P, 1], F32))

    def load_row(self, sp, r):
        sp.dma_start(self.h[:, r, :], rows_of(*self.x, r)).then_inc(self.s_row[r], 16)

    def normed_rows(self, ctx, tag):
        self.xt_hi, self.xt_lo = (ctx.enter_context(self.nc.sbuf_tensor(f"{tag}_xt_{x}", [P, KT, ROWS], F32R))
                                  for x in ("hi", "lo"))

    def clear_semaphores(self):
        self.nc.clear_and_free_semaphores(self.sems)
        self.nc.all_engine_barrier()
        self.sems = []

    def cos_sin(self, r):
        v = self.const[:, C_ROPE + r * 64:C_ROPE + (r + 1) * 64]
        return v[:, 0:32], v[:, 32:64]


def rows_of(prompt, sample, r):
    return prompt[r * P:(r + 1) * P, :] if r < RT - 1 else sample


def scope(core, ctx, tag):
    nc = core.nc

    def sb(name, shape, dt=F32):
        return ctx.enter_context(nc.sbuf_tensor(f"{tag}_{name}", shape, dt))

    def ps(name, shape):
        return ctx.enter_context(nc.psum_tensor(f"{tag}_{name}", shape, F32))

    def sem(name):
        s = nc.alloc_semaphore(name=f"{tag}_{name}")
        core.sems.append(s)
        return s

    return sb, ps, sem




FIRST_ROWS = 3


def start_phase(nc, core, table, lams):
    with ExitStack() as ctx:
        sb, ps, sem = scope(core, ctx, "st")
        lv = sb("lam_vectors", [P, 4, 64])
        prod = sb("lam_products", [P, 64])
        dots = sb("lam_dots", [P, 2])
        ex = sb("lam_exps", [P, 2])
        s_load, s_dot, s_exp, s_v = sem("load"), sem("dot"), sem("exp"), sem("v")
        block = ctx.enter_context(nc.Block())

        @block.sync
        def _(sp):
            for i, v in enumerate(lams):
                sp.dma_start(lv[:, i, :], v.rearrange("a d -> (a d)").partition_broadcast(P)).then_inc(s_load, 16)
            sp.dma_start(core.const[:], table).then_inc(s_load, 16)
            for r in range(FIRST_ROWS):
                core.load_row(sp, r)

        @block.scalar
        def _(act):
            act.wait_ge(s_dot, 2)
            act.activation(ex[:], dots[:], ACT.Exp).then_inc(s_exp, 1)

        @block.vector
        def _(dve):
            dve.wait_ge(s_load, 80)
            for i in range(2):
                if i:
                    dve.wait_ge(s_dot, 1)
                dve.tensor_tensor_reduce(prod[:], lv[:, 2 * i, :], lv[:, 2 * i + 1, :], 1.0, 0.0,
                                         ALU.mult, ALU.add, dots[:, i:i + 1]).then_inc(s_dot, 1)
            dve.wait_ge(s_exp, 1)
            dve.tensor_tensor(core.neglam[:], ex[:, 1:2], ex[:, 0:1], ALU.subtract).then_inc(s_v, 1)
            dve.wait_ge(s_v, 1)
            dve.tensor_scalar(core.neglam[:], core.neglam[:], -0.2, None, ALU.add).then_inc(s_v, 1)
            dve.wait_ge(s_v, 2)
            dve.tensor_scalar(core.lamcol[:], core.const[:, C_LAM + 1:C_LAM + 2], core.neglam[:, 0:1], -1.0,
                              ALU.mult, ALU.mult).then_inc(s_v, 1)
            dve.wait_ge(s_v, 3)
            dve.tensor_tensor(core.lamcol[:], core.lamcol[:], core.const[:, C_LAM:C_LAM + 1],
                              ALU.add).then_inc(s_v, 1)




class Norm:

    def __init__(self, core, sb, ps, sem, tag, kind, gain, src=None, buffers=2):
        self.core, self.kind, self.gain_src, self.src = core, kind, gain, src
        self.xn, self.buffers = sb(f"{tag}xn", [P, buffers, D]), buffers
        self.own_rows = kind in ("rms", "final")
        self.w, self.width = (1, D) if self.own_rows else (8, P)
        self.stat, self.rstd = sb(f"{tag}stat", [P, RT, self.w]), sb(f"{tag}rstd", [P, RT, self.w])
        if kind != "plain":
            self.gain = sb(f"{tag}gain", [P, self.width])
        if kind == "head":
            self.sqh = sb(f"{tag}sqh", [P, D])
        if kind != "final":
            self.bank = [ps(f"{tag}nt{i}", [P, 4, P]) for i in range(2)]
        self.s_pre, self.s_root, self.s_gain, self.s_sq, self.s_rs, self.s_xn, self.s_tp, self.s_hi, self.s_lo = (
            sem(tag + x) for x in ("pre", "root", "gain", "sumsq", "rstd", "xn", "xT", "xhi", "xlo"))
        self.s_x = [sem(f"{tag}x{x}") for x in range(2)]
        self.steps, self.first = 0, False

    def sync(self, sp):
        if self.kind != "plain":
            sp.dma_start(self.gain[:], self.gain_src.partition_broadcast(P)).then_inc(self.s_gain, 16)

    def store(self, sp):
        for r in range(RT):
            sp.wait_ge(self.s_xn, r + 1)
            sp.dma_start(self.src(r), self.buffer(r)).then_inc(self.s_x[r % 2], 16)
        for k in range(2):
            sp.wait_ge(self.s_x[k], 16 * ((RT - k + 1) // 2))

    def buffer(self, r):
        return self.xn[:, r % self.buffers, :]

    def buffer_free(self, eng, r):
        if r >= self.buffers and self.kind == "final":
            eng.wait_ge(self.s_x[r % 2], 16 * (r // 2))
        elif r >= self.buffers:
            eng.wait_ge(self.s_tp, 2 * (r - self.buffers) + 2)

    def load(self, act, r):
        if self.own_rows or r >= RT:
            return
        self.buffer_free(act, r)
        act.dma_start(self.buffer(r), self.src[r * P:(r + 1) * P, :]).then_inc(self.s_x[r % 2], 16)

    def scalar(self, act, r):
        if self.first:
            act.wait_ge(self.core.s_row[r], 16)
        if self.own_rows:
            self.buffer_free(act, r)
            act.activation(self.buffer(r), self.core.h[:, r, :], ACT.Square,
                           accum_out=self.stat[:, r, 0:1]).then_inc(self.s_sq, 1)
        elif self.kind == "head":
            act.wait_ge(self.s_x[r % 2], 16 * (r // 2 + 1))
            if r:
                act.wait_ge(self.s_pre, r)
            act.activation(self.sqh[:], self.buffer(r), ACT.Square).then_inc(self.s_sq, 1)
        if self.kind != "plain":
            act.wait_ge(self.s_pre, r + 1)
            act.activation(self.rstd[:, r, 0:self.w], self.rstd[:, r, 0:self.w], ACT.Sqrt).then_inc(self.s_root, 1)
        if r:
            self.high(act, r - 1)
            self.load(act, r + 1)

    def high(self, act, r):
        if self.kind == "final":
            return
        for g in range(2):
            act.wait_ge(self.s_tp, 2 * r + g + 1)
            act.activation(self.core.xt_hi[:, 4 * g:4 * g + 4, r * P:(r + 1) * P], self.bank[g][:],
                           ACT.Copy).then_inc(self.s_hi, 1)

    def vector(self, dve, r):
        k = self.kind
        x = self.buffer(r)
        xh = x.rearrange("p (h e) -> p h e", e=P)

        def own(ins):
            self.steps += 1
            ins.then_inc(self.s_rs, 1)
            dve.wait_ge(self.s_rs, self.steps)

        if k != "plain":
            if r == 0:
                dve.wait_ge(self.s_gain, 16)
                if k == "head":
                    own(dve.tensor_scalar(self.gain[:], self.gain[:], 0.8, None, ALU.mult))
            dve.wait_ge(self.s_sq, r + 1)
            if k == "head":
                own(dve.tensor_reduce(self.stat[:, r, :], self.sqh[:].rearrange("p (h e) -> p h e", e=P), AX, ALU.add))
            own(dve.tensor_scalar(self.stat[:, r, 0:self.w], self.stat[:, r, 0:self.w], 1.0 / self.width, EPS,
                                  ALU.mult, ALU.add))
            dve.reciprocal(self.rstd[:, r, 0:self.w], self.stat[:, r, 0:self.w]).then_inc(self.s_pre, 1)
        if r:
            self.low(dve, r - 1)
        if k == "plain":
            return
        dve.wait_ge(self.s_root, r + 1)
        if self.own_rows:
            dve.scalar_tensor_tensor(x, self.core.h[:, r, :], self.rstd[:, r, 0:1], self.gain[:], ALU.mult,
                                     ALU.mult).then_inc(self.s_xn, 1)
        else:
            own(dve.tensor_tensor(xh, xh, self.rstd[:, r, :].unsqueeze(2).to_broadcast([P, 8, P]), ALU.mult))
            dve.tensor_tensor(xh, xh, self.gain[:].unsqueeze(1).to_broadcast([P, 8, P]),
                              ALU.mult).then_inc(self.s_xn, 1)

    def low(self, dve, r):
        if self.kind == "final":
            return
        for g in range(2):
            dve.wait_ge(self.s_hi, 2 * r + g + 1)
            hi = self.core.xt_hi[:, 4 * g:4 * g + 4, r * P:(r + 1) * P]
            dve.tensor_tensor(self.core.xt_lo[:, 4 * g:4 * g + 4, r * P:(r + 1) * P], self.bank[g][:],
                              hi.bitcast(F32), ALU.subtract).then_inc(self.s_lo, 1)

    def tensor(self, pe, r):
        if self.kind == "final":
            return
        if self.kind == "plain":
            pe.wait_ge(self.s_x[r % 2], 16 * (r // 2 + 1))
        else:
            pe.wait_ge(self.s_xn, r + 1)
        for g in range(2):
            if r:
                pe.wait_ge(self.s_lo, 2 * r + g - 1)
            for c in range(4):
                ins = pe.transpose(self.bank[g][:, c, :], self.buffer(r)[:, (4 * g + c) * P:(4 * g + c + 1) * P],
                                   self.core.ident)
            ins.then_inc(self.s_tp, 1)

    def ready(self, pe, r):
        pe.wait_ge(self.s_lo, 2 * r + 2)


def product(pe, out, lhs, rhs, start, stop):
    (lh, ll), (rh, rl) = lhs, rhs
    pe.matmul(out, lh, rh, start=start, stop=False)
    pe.matmul(out, lh, rl, start=False, stop=False)
    return pe.matmul(out, ll, rh, start=False, stop=stop)




def dense_phase(nc, core, tag, kind, gain, src, pieces, forget=None, following=None, swap=None):
    with ExitStack() as ctx:
        sb, ps, sem = scope(core, ctx, tag)
        norm = Norm(core, sb, ps, sem, "", kind, gain, src) if kind else None
        if kind == "rms":
            norm.first = True
        nxt = None
        if following is not None:
            nxt = Norm(core, sb, ps, sem, "next_", "rms", following, buffers=1 if norm else 2)
        PARTS = 4
        KP = KT // PARTS
        raw = sb("w_raw", [P, 2, KP, HALF])
        whi = sb("w_hi", [P, 2, KT, HALF], F32R)
        wlo = sb("w_lo", [P, 2, KT, HALF], F32R)
        stores = any(do != "add" for _, _, do, _ in pieces)
        passes = [[i] for i in range(len(pieces))] if stores else [list(range(len(pieces)))]
        swap = len(passes) - 1 if swap is None else swap
        behind = 0 if norm else 1
        if stores:
            ob = sb("out_rows", [P, 2, HALF])
        if any(do == "rope" for _, _, do, _ in pieces):
            tc, tsn = sb("times_cos", [P, HALF]), sb("times_sin", [P, HALF])
        NPS = 3 if forget or (norm and nxt) else 4
        acc = [ps(f"acc{i}", [P, HALF]) for i in range(NPS)]
        s_whi, s_wlo, s_mm, s_ev = sem("whi"), sem("wlo"), sem("mm"), sem("ev")
        s_raw = [sem("raw0"), sem("raw1")]
        s_rot = sem("rot")
        s_st = [sem("store0"), sem("store1")]
        if forget:
            w_f, b_f, f_prompt, f_sample = forget
            fraw = sb("f_raw", [P, KT, 16])
            fhi, flo = sb("f_hi", [P, KT, 16], F32R), sb("f_lo", [P, KT, 16], F32R)
            fb = sb("f_bias", [P, 16])
            z, e, u, t, m = (sb(f"f_{x}", [P, RT, 16]) for x in "zeutm")
            facc = ps("f_acc", [P, RT, 16])
            s_fl, s_fw, s_fm, s_fv, s_fa, s_fo = sem("fl"), sem("fw"), sem("fm"), sem("fv"), sem("fa"), sem("fo")
        block = ctx.enter_context(nc.Block())
        NT = len(pieces) * RT

        def row_steps(i, first, body, end):
            ahead = NPS - 1 if stores else 2
            if i or not norm:
                for r in range(RT):
                    body(r)
                return
            for r in range(RT + ahead):
                if r < RT:
                    first(r)
                elif r == RT:
                    end()
                if r >= ahead:
                    body(r - ahead)

        @block.sync
        def _(sp):
            def load(n):
                w, c0, _, _ = pieces[n // PARTS]
                k = n % PARTS * KP
                if n >= 2:
                    sp.wait_ge(s_wlo, n - 1)
                sp.dma_start(raw[:, n % 2], w[:, c0:c0 + HALF].rearrange("(k p) n -> p k n", p=P)[
                    :, k:k + KP, :]).then_inc(s_raw[n % 2], 16)

            if norm:
                norm.sync(sp)
            load(0)
            load(1)
            if kind == "rms":
                core.load_row(sp, FIRST_ROWS)
                core.load_row(sp, FIRST_ROWS + 1)
            if forget:
                sp.dma_start(fraw[:], w_f.rearrange("(k p) n -> p k n", p=P)).then_inc(s_fl, 16)
                sp.dma_start(fb[:], b_f.partition_broadcast(P)).then_inc(s_fl, 16)
            if nxt:
                nxt.sync(sp)
            for n in range(2, PARTS * len(pieces)):
                load(n)
                if kind == "rms" and n + FIRST_ROWS < RT:
                    core.load_row(sp, n + FIRST_ROWS)

        @block.gpsimd
        def _(pool):
            if forget:
                pool.wait_ge(s_fl, 32)
                pool.tensor_copy(fhi[:], fraw[:]).then_inc(s_fw, 1)
                pool.wait_ge(s_fw, 1)
                pool.tensor_tensor(flo[:], fraw[:], fhi[:].bitcast(F32), ALU.subtract).then_inc(s_fw, 1)
            for n in range(PARTS * len(pieces)):
                k, slot = n % PARTS * KP, n // PARTS % 2
                pool.wait_ge(s_whi, n + 1)
                pool.tensor_tensor(wlo[:, slot, k:k + KP, :], raw[:, n % 2], whi[:, slot, k:k + KP, :].bitcast(F32),
                                   ALU.subtract).then_inc(s_wlo, 1)

        @block.tensor
        def _(pe):
            def forget_products(r):
                if r == 0:
                    pe.wait_ge(s_fw, 2)
                for k in range(KT):
                    x = [v[:, k, r * P:(r + 1) * P] for v in (core.xt_hi, core.xt_lo)]
                    ins = product(pe, facc[:, r, :], x, (fhi[:, k, :], flo[:, k, :]), k == 0, k == KT - 1)
                if r == RT - 1:
                    ins.then_inc(s_fm, 1)

            if norm:
                norm.tensor(pe, 0)
            n = 0
            for i, group in enumerate(passes):
                for r in range(RT):
                    if norm and i == 0:
                        if r + 1 < RT:
                            norm.tensor(pe, r + 1)
                        norm.ready(pe, r)
                    if i == swap + 1:
                        nxt.ready(pe, r)
                    if forget and i == 0:
                        forget_products(r)
                    for piece in group:
                        if r == 0:
                            pe.wait_ge(s_wlo, PARTS * (piece + 1))
                        if n >= NPS:
                            pe.wait_ge(s_ev, n - NPS + 1)
                        for k in range(KT):
                            x = [v[:, k, r * P:(r + 1) * P] for v in (core.xt_hi, core.xt_lo)]
                            ins = product(pe, acc[n % NPS][:], x, (whi[:, piece % 2, k, :], wlo[:, piece % 2, k, :]),
                                          k == 0, k == KT - 1)
                        ins.then_inc(s_mm, 1)
                        n += 1
                    if nxt and i == swap and r > behind:
                        nxt.tensor(pe, r - behind - 1)
                if nxt and i == swap:
                    for r in range(RT - behind - 1, RT):
                        nxt.tensor(pe, r)

        @block.vector
        def _(dve):
            rotations = [0]

            def forget_values():
                dve.wait_ge(s_fm, 1)
                dve.tensor_tensor(z[:], facc[:], fb[:].unsqueeze(1).to_broadcast([P, RT, 16]),
                                  ALU.add).then_inc(s_fv, 1)
                dve.wait_ge(s_fv, 1)
                dve.tensor_scalar(u[:], z[:], -1.0, None, ALU.mult).then_inc(s_fv, 1)
                dve.wait_ge(s_fv, 2)
                dve.tensor_tensor(t[:], z[:], u[:], ALU.min).then_inc(s_fv, 1)
                dve.wait_ge(s_fa, 1)
                dve.tensor_scalar(u[:], e[:], 1.0, None, ALU.add).then_inc(s_fv, 1)
                dve.wait_ge(s_fa, 2)
                dve.tensor_scalar(m[:], u[:], 1.0, None, ALU.is_equal).then_inc(s_fv, 1)
                dve.tensor_scalar(u[:], u[:], -1.0, None, ALU.add).then_inc(s_fv, 1)
                dve.wait_ge(s_fv, 6)
                dve.tensor_tensor(u[:], u[:], m[:], ALU.add).then_inc(s_fv, 1)
                dve.tensor_tensor(t[:], t[:], m[:], ALU.add).then_inc(s_fv, 1)
                dve.wait_ge(s_fv, 8)
                dve.tensor_tensor(t[:], t[:], e[:], ALU.mult).then_inc(s_fv, 1)
                dve.reciprocal(m[:], u[:]).then_inc(s_fv, 1)
                dve.wait_ge(s_fv, 10)
                dve.tensor_tensor(t[:], t[:], m[:], ALU.mult).then_inc(s_fv, 1)
                dve.tensor_scalar(z[:], z[:], 0.0, None, ALU.min).then_inc(s_fv, 1)
                dve.wait_ge(s_fv, 12)
                dve.tensor_tensor(z[:], z[:], t[:], ALU.subtract).then_inc(s_fv, 1)

            def out_rows(n, r, do, dst):
                dve.wait_ge(s_mm, n + 1)
                src_ = acc[n % NPS][:]
                if do == "add":
                    hc = core.h[:, r, dst:dst + HALF]
                    dve.tensor_tensor(hc, hc, src_, ALU.add).then_inc(s_ev, 1)
                    return
                if n >= 2:
                    dve.wait_ge(s_st[n % 2], 16 * (n // 2))
                o = ob[:, n % 2, :]
                if do == "store":
                    dve.tensor_copy(o, src_).then_inc(s_ev, 1)
                    return
                v = src_.rearrange("p (h s e) -> p h s e", s=2, e=32)
                cos, sin = (x.unsqueeze(1).unsqueeze(1).to_broadcast([P, 8, 2, 32]) for x in core.cos_sin(r))
                if rotations[0]:
                    dve.wait_ge(s_ev, n)
                tcv = tc[:].rearrange("p (h s e) -> p h s e", s=2, e=32)
                tsv = tsn[:].rearrange("p (h s e) -> p h s e", s=2, e=32)
                dve.tensor_tensor(tcv, v, cos, ALU.mult).then_inc(s_rot, 1)
                dve.tensor_tensor(tsv, v, sin, ALU.mult).then_inc(s_rot, 1)
                rotations[0] += 2
                dve.wait_ge(s_rot, rotations[0])
                ov = o.rearrange("p (h s e) -> p h s e", s=2, e=32)
                dve.tensor_tensor(ov[:, :, 0, :], tcv[:, :, 0, :], tsv[:, :, 1, :], ALU.subtract).then_inc(s_rot, 1)
                rotations[0] += 1
                dve.wait_ge(s_rot, rotations[0])
                dve.tensor_tensor(ov[:, :, 1, :], tcv[:, :, 1, :], tsv[:, :, 0, :], ALU.add).then_inc(s_ev, 1)

            for i, group in enumerate(passes):
                def body(r):
                    for x, piece in enumerate(group):
                        out_rows((i * RT + r) * len(group) + x, r, *pieces[piece][2:])
                    if nxt and i == swap and r >= behind:
                        nxt.vector(dve, r - behind)

                row_steps(i, lambda r: norm.vector(dve, r), body, lambda: norm.low(dve, RT - 1))
                if forget and i == 0:
                    forget_values()
                if nxt and i == swap:
                    for r in range(RT - behind, RT):
                        nxt.vector(dve, r)
                    nxt.low(dve, RT - 1)

        @block.scalar
        def _(act):
            def weight_high(n):
                piece, k = n // PARTS, n % PARTS * KP
                act.wait_ge(s_raw[n % 2], 16 * (n // 2 + 1))
                act.activation(whi[:, piece % 2, k:k + KP, :], raw[:, n % 2], ACT.Copy).then_inc(s_whi, 1)

            def weight_highs(piece):
                if piece >= 2:
                    act.wait_ge(s_mm, RT * (piece - 1))
                for n in range(PARTS * piece, PARTS * (piece + 1)):
                    weight_high(n)

            def forget_values():
                act.wait_ge(s_fv, 3)
                act.activation(e[:], t[:], ACT.Exp).then_inc(s_fa, 1)
                act.wait_ge(s_fv, 4)
                act.activation(t[:], u[:], ACT.Ln).then_inc(s_fa, 1)
                act.wait_ge(s_fv, 13)
                act.dma_start(f_prompt.rearrange("(r p) h -> p r h", p=P), z[:, 0:RT - 1, :]).then_inc(s_fo, 16)
                act.dma_start(f_sample, z[:, RT - 1, :]).then_inc(s_fo, 16)

            if norm:
                norm.load(act, 0)
                norm.load(act, 1)
                weight_high(0)
                weight_high(1)
            else:
                weight_highs(0)
            for i, group in enumerate(passes):
                def body(r):
                    n = (i * RT + r) * len(group)
                    if r == 0 and i + 1 < len(pieces) and not (norm and i == 0):
                        weight_highs(i + 1)
                    if stores:
                        prompt, sample, d0 = pieces[i][3]
                        act.wait_ge(s_ev, n + 1)
                        act.dma_start(rows_of(prompt, sample, r)[:, d0:d0 + HALF],
                                      ob[:, n % 2, :]).then_inc(s_st[n % 2], 16)
                    if nxt and i == swap:
                        if not stores:
                            act.wait_ge(s_ev, n + len(group))
                        nxt.scalar(act, r)

                def first(r):
                    norm.scalar(act, r)
                    if r < 3:
                        weight_high(2 * r + 2)
                        weight_high(2 * r + 3)

                row_steps(i, first, body, lambda: norm.high(act, RT - 1))
                if forget and i == 0:
                    forget_values()
                if nxt and i == swap:
                    nxt.high(act, RT - 1)
            if stores:
                for k in range(2):
                    act.wait_ge(s_st[k], 16 * ((NT - k + 1) // 2))
            if forget:
                act.wait_ge(s_fo, 32)




def mlp_phase(nc, core, tag, w_up, w_down, following, y_rows=None):
    with ExitStack() as ctx:
        sb, ps, sem = scope(core, ctx, tag)
        nxt = Norm(core, sb, ps, sem, "next_", "final" if y_rows else "rms", following, y_rows)
        NF, RG = FC // P, 3
        GW = ROWS // RG
        up_raw, dn_raw = sb("up_raw", [P, KT, FC]), sb("dn_raw", [P, NF, D])
        up_hi, up_lo = sb("up_hi", [P, KT, FC], F32R), sb("up_lo", [P, KT, FC], F32R)
        dn_hi, dn_lo = sb("dn_hi", [P, NF, D], F32R), sb("dn_lo", [P, NF, D], F32R)
        hid_hi, hid_lo = sb("hid_hi", [P, NF, ROWS], F32R), sb("hid_lo", [P, NF, ROWS], F32R)
        rl, sq = sb("relu", [P, 2, GW]), sb("relu2", [P, 2, GW])
        ups = [ps(f"up{i}", [P, HALF]) for i in range(3)]
        dns = [ps(f"dn{i}", [P, HALF]) for i in range(3)]
        s_ur, s_dr, s_uh, s_ul, s_dh, s_dl = (sem(x) for x in ("ur", "dr", "uh", "ul", "dh", "dl"))
        s_um, s_ue, s_sq, s_hh, s_hl, s_dm, s_de = (sem(x) for x in ("um", "ue", "sq", "hh", "hl", "dm", "de"))
        block = ctx.enter_context(nc.Block())
        NU, ND = NF * RG, RT * 2
        STEPS = DFF // FC

        @block.sync
        def _(sp):
            nxt.sync(sp)
            with sp.Fori(0, STEPS) as i:
                sp.wait_ge(s_ul, i + 1)
                sp.dma_start(up_raw[:], w_up[:, bass.ts(i, FC)].rearrange("(k p) n -> p k n", p=P)).then_inc(s_ur, 16)
                sp.wait_ge(s_dl, i + 1)
                sp.dma_start(dn_raw[:], w_down[bass.ts(i, FC), :].rearrange("(k p) n -> p k n", p=P)).then_inc(s_dr, 16)
            if y_rows:
                nxt.store(sp)

        @block.gpsimd
        def _(pool):
            pool.sem_inc(s_ul, 1)
            pool.sem_inc(s_dl, 1)
            with pool.Fori(0, STEPS) as i:
                pool.wait_ge(s_uh, i + 1)
                pool.tensor_tensor(up_lo[:], up_raw[:], up_hi[:].bitcast(F32), ALU.subtract).then_inc(s_ul, 1)
                pool.wait_ge(s_dh, i + 1)
                pool.tensor_tensor(dn_lo[:], dn_raw[:], dn_hi[:].bitcast(F32), ALU.subtract).then_inc(s_dl, 1)

        @block.tensor
        def _(pe):
            pe.sem_inc(s_hl, 3)
            pe.sem_inc(s_de, 3)
            pe.sem_inc(s_um, 1)
            pe.sem_inc(s_dm, 1)

            def step(i, last=False):
                pe.wait_ge(s_ul, i + 2)
                for g in range(RG):
                    for f in range(NF):
                        n = g * NF + f
                        pe.wait_ge(s_hl, i * NU + n + 1)
                        for k in range(KT):
                            w = [v[:, k, f * P:(f + 1) * P] for v in (up_hi, up_lo)]
                            x = [v[:, k, g * GW:(g + 1) * GW] for v in (core.xt_hi, core.xt_lo)]
                            ins = product(pe, ups[n % 3][:, 0:GW], w, x, k == 0, k == KT - 1)
                        ins.then_inc(s_um, 1)
                pe.wait_ge(s_dl, i + 2)
                for r in range(RT):
                    if r % 3 == 0:
                        pe.wait_ge(s_hl, i * NU + NF * (r // 3 + 1) + 3)
                    for c in range(2):
                        n = 2 * r + c
                        pe.wait_ge(s_de, i * ND + n + 1)
                        for f in range(NF):
                            x = [v[:, f, r * P:(r + 1) * P] for v in (hid_hi, hid_lo)]
                            w = [v[:, f, c * HALF:(c + 1) * HALF] for v in (dn_hi, dn_lo)]
                            ins = product(pe, dns[n % 3][:], x, w, f == 0, f == NF - 1)
                        ins.then_inc(s_dm, 1)
                    if last and r >= 2:
                        nxt.tensor(pe, r - 2)

            with pe.Fori(0, STEPS - 1) as i:
                step(i)
            step(STEPS - 1, last=True)
            nxt.tensor(pe, RT - 2)
            nxt.tensor(pe, RT - 1)

        @block.scalar
        def _(act):
            act.sem_inc(s_sq, 2)

            def up_high(i):
                act.wait_ge(s_ur, i * 16 + 16)
                act.wait_ge(s_um, i * NU + 1)
                act.activation(up_hi[:], up_raw[:], ACT.Copy).then_inc(s_uh, 1)

            def step(i):
                act.wait_ge(s_dr, i * 16 + 16)
                act.wait_ge(s_dm, i * ND + 1)
                act.activation(dn_hi[:], dn_raw[:], ACT.Copy).then_inc(s_dh, 1)
                for n in range(NU):
                    g, f = n // NF, n % NF
                    act.wait_ge(s_um, i * NU + n + 2)
                    act.wait_ge(s_sq, i * NU + n + 1)
                    act.activation(rl[:, n % 2, :], ups[n % 3][:, 0:GW], ACT.Relu).then_inc(s_ue, 1)
                    act.wait_ge(s_sq, i * NU + n + 3)
                    act.activation(hid_hi[:, f, g * GW:(g + 1) * GW], sq[:, n % 2, :], ACT.Copy).then_inc(s_hh, 1)

            up_high(0)
            with act.Fori(0, STEPS - 1) as i:
                step(i)
                up_high(i + 1)
            step(STEPS - 1)
            for r in range(RT):
                act.wait_ge(s_de, (STEPS - 1) * ND + 2 * r + 5)
                nxt.scalar(act, r)
            nxt.high(act, RT - 1)

        @block.vector
        def _(dve):
            def step(i, last=False):
                def square(n):
                    dve.wait_ge(s_ue, i * NU + n + 1)
                    dve.tensor_tensor(sq[:, n % 2, :], rl[:, n % 2, :], rl[:, n % 2, :], ALU.mult).then_inc(s_sq, 1)

                def low(n):
                    g, f = n // NF, n % NF
                    dve.wait_ge(s_hh, i * NU + n + 1)
                    hi = hid_hi[:, f, g * GW:(g + 1) * GW].bitcast(F32)
                    dve.tensor_tensor(hid_lo[:, f, g * GW:(g + 1) * GW], sq[:, n % 2, :], hi,
                                      ALU.subtract).then_inc(s_hl, 1)

                for n in range(NU):
                    square(n)
                    low(n)
                for n in range(ND):
                    r, c = n // 2, n % 2
                    hc = core.h[:, r, c * HALF:(c + 1) * HALF]
                    dve.wait_ge(s_dm, i * ND + n + 2)
                    dve.tensor_tensor(hc, hc, dns[n % 3][:], ALU.add).then_inc(s_de, 1)
                    if last and c and r:
                        nxt.vector(dve, r - 1)

            with dve.Fori(0, STEPS - 1) as i:
                step(i)
            step(STEPS - 1, last=True)
            nxt.vector(dve, RT - 1)
            nxt.low(dve, RT - 1)




def prompt_attention(nc, core, tag, fox, q_rows, k_rows, v_rows, logf, cum, o_rows):
    with ExitStack() as ctx:
        sb, ps, sem = scope(core, ctx, tag)
        QT, TURNS = SEQ // P, 4
        NM = 2 if fox else 1
        kd, qd = sb("k_dup", [P, QT, 2, 2, 64]), sb("q_dup", [P, QT, 2, 2, 64])
        vr = sb("v_rows", [P, 2, QT, P])
        khi, klo = sb("kT_hi", [P, 2, 2, SEQ], F32R), sb("kT_lo", [P, 2, 2, SEQ], F32R)
        q2 = sb("qT", [P, 2, 2, SEQ], F32R)
        pr = sb("probs", [P, 2, 2, SEQ])
        wT = sb("wT", [P, 2, NM, SEQ])
        ost = sb("o_rows", [P, 2, QT, P])
        nmx, dsum, rinv, fac = (sb(n, [P, 2 * QT]) for n in ("neg_max", "row_sum", "inv_sum", "factor"))
        ident_r, mask_r = sb("ident_r", [P, P], F32R), sb("mask_r", [P, P], F32R)
        S = [ps(f"s{m}", [P, 2, HALF]) for m in range(2)]
        T = [ps(f"t{b}", [P, HALF]) for b in range(2)]
        K = ps("kq", [P, HALF])
        FIRST = [K, T[0]]
        O = ps("o", [P, 2, P])
        s_kt, s_ke = sem("kt"), sem("ke")
        s_kd, s_qd, s_t, s_kh, s_s, s_nm, s_e, s_f, s_w, s_pv, s_oe, s_of, s_c = (
            sem(x) for x in ("kd", "qd", "t", "kh", "s", "nm", "exp", "fac", "w", "pv", "oe", "of", "c"))
        s_vd, s_te, s_od = ([sem(f"{n}{b}") for b in range(2)] for n in ("vd", "te", "od"))
        if fox:
            q2b = sb("qT_aux", [P, 2, 2, SEQ], F32R)
            lf, c = sb("logf", [P, QT, 16]), sb("cum", [16, SEQ])
            cp = sb("cum_parts", [16, 4, SEQ], F32R)
            s_lf, s_cv, s_cd, s_qb = sem("lf"), sem("cv"), sem("cd"), sem("qb")
            s_ax = [sem("ax0"), sem("ax1")]
            oT = sb("o_T", [P, P])
            s_ot, s_ob = sem("ot"), sem("ob")
        block = ctx.enter_context(nc.Block())

        tiles = [QT - 1 - s % QT for s in range(2 * QT)]
        groups = [[(k, min(4, t + 1 - k)) for k in range(0, t + 1, 4)] for t in tiles]

        kq_steps = [[8 * (s // QT) + j for j in ((6, 7) if s % QT == 6 else (s % QT,) if s % QT < 6 else ())]
                    for s in range(2 * QT)]

        w_units, NU = {}, 0
        for s in range(2 * QT):
            for m in range(NM):
                w_units[s, m] = NU
                NU += len(groups[s])

        class Turn:

            def __init__(self, it, last=False):
                self.it, self.last = it, last
                self.w = w_units

            def units(self, n):
                return self.it * NU + n

            def fills(self, n):
                return self.it * (NU // 2) + n // 2

            def kq_of(self, s, m):
                units = [] if self.last and s >= QT else kq_steps[s]
                return units[-1:] if m else units[:-1]

            def has_next(self, s):
                return not (self.last and s == 2 * QT - 1)

        def kq_parts(j):
            j %= 8
            return j < 4, j % 4 // 2, 4 * (j % 2)

        @block.sync
        def _(sp):
            def load_k(p):
                v = k_rows[0:SEQ, bass.ts(p, P)].rearrange("(t p) e -> p t e", p=P)
                for m in range(2):
                    for dup in range(2):
                        sp.dma_start(kd[:, :, m, dup, :], v[:, :, m * 64:m * 64 + 64]).then_inc(s_kd, 16)

            def load_q(p):
                v = q_rows[0:SEQ, bass.ts(p, P)].rearrange("(t p) e -> p t e", p=P)
                for m in range(2):
                    for dup in range(2):
                        sp.dma_start(qd[:, :, m, dup, :], v[:, :, m * 64:m * 64 + 64]).then_inc(s_qd, 16)

            def load_v(p, par):
                sp.dma_start(vr[:, par], v_rows[0:SEQ, bass.ts(p, P)].rearrange(
                    "(t p) e -> p t e", p=P)).then_inc(s_vd[par], 16)

            def load_c(p, par):
                v = cum[bass.ds(p * 2, 2)]
                sp.dma_start(klo[64:66, par].bitcast(F32), v[:, 0:2, :].rearrange("m r k -> r m k")).then_inc(s_ax[par], 16)
                sp.dma_start(q2b[66:68, par].bitcast(F32), v[:, 2:4, :].rearrange("m r k -> r m k")).then_inc(s_ax[par], 16)

            if fox:
                sp.dma_start(lf[:], logf.rearrange("(r p) h -> p r h", p=P)).then_inc(s_lf, 16)
            load_k(0)
            load_q(0)
            load_v(0, 0)
            load_v(1, 1)
            if fox:
                sp.wait_ge(s_cv, 11)
                sp.dma_start(cum[:], cp[:].bitcast(F32)).then_inc(s_cd, 16)
                sp.wait_ge(s_cd, 16)
                load_c(0, 0)
                load_c(1, 1)
            sp.wait_ge(s_kt, 4)
            load_k(1)
            sp.wait_ge(s_kt, 8)
            load_q(1)
            with sp.Fori(0, TURNS - 1) as it:
                for par in range(2):
                    p = it * 2 + (2 + par)
                    sp.wait_ge(s_kt, it * 16 + (8 * par + 12))
                    load_k(p)
                    sp.wait_ge(s_kt, it * 16 + (8 * par + 16))
                    load_q(p)
                    if fox:
                        sp.wait_ge(s_s, it * 32 + 16 * (par + 1))
                        load_c(p, par)
                    sp.wait_ge(s_pv, it * (2 * QT) + QT * (par + 1))
                    load_v(p, par)

        @block.gpsimd
        def _(pool):
            pool.tensor_copy(ident_r[:], core.ident).then_inc(s_c, 1)
            m0 = C_TRI if fox else C_BLK
            pool.tensor_copy(mask_r[:], core.const[:, m0:m0 + P]).then_inc(s_c, 1)

            def store(it, par):
                pool.wait_ge(s_oe, it * (2 * QT) + (QT * (par + 1) + 1))
                pool.dma_start(o_rows[0:SEQ, bass.ts(it * 2 + par, P)].rearrange("(t p) e -> p t e", p=P),
                               ost[:, par]).then_inc(s_od[par], 16)
                pool.wait_ge(s_od[par], it * 16 + 16)
                pool.sem_inc(s_of, 1)

            with pool.Fori(0, TURNS - 1) as it:
                store(it, 0)
                store(it, 1)
            store(TURNS - 1, 0)
            store(TURNS - 1, 1)

        @block.tensor
        def _(pe):
            for s, n in ((s_te[0], 1), (s_te[1], 1), (s_ke, 1), (s_e, 2), (s_oe, 1), (s_of, 2)):
                pe.sem_inc(s, n)
            if fox:
                pe.wait_ge(s_lf, 16)
                for t in range(QT):
                    ins = pe.transpose(S[0][0:16, t // 4, (t % 4) * P:(t % 4 + 1) * P], lf[:, t, :], core.ident)
                ins.then_inc(s_cv, 1)

            def kq_unit(j, read, loaded, bank):
                keys, m, t0 = kq_parts(j)
                src = kd if keys else qd
                if j % 4 == 0:
                    pe.wait_ge(s_kd if keys else s_qd, loaded)
                pe.wait_ge(s_ke, read + 1)
                for x in range(4):
                    ins = pe.transpose(bank[:, x * P:(x + 1) * P], src[:, t0 + x, m].rearrange("p a e -> p (a e)"),
                                       core.ident)
                ins.then_inc(s_kt, 1)

            def scores(turn, s, m):
                t, par = tiles[s % (2 * QT)], s // QT % 2
                it = turn.it
                if s % QT == 0 and m == 0:
                    pe.wait_ge(s_ke, it * 16 + (s // QT * 8 + 9))
                    if fox:
                        pe.wait_ge(s_qb, it * 8 + 4 * (s // QT + 1))
                        pe.wait_ge(s_ax[par], it * 32 + (64 if s == 2 * QT else 32))
                n = (t + 1) * P
                pe.wait_ge(s_e, it * 32 + (2 * s + m + 1))
                for k0 in range(0, n, HALF):
                    w = min(HALF, n - k0)
                    last = k0 + w == n
                    out = S[m][:, k0 // HALF, 0:w]
                    pe.matmul(out, q2[:, par, m, t * P:(t + 1) * P], khi[:, par, m, k0:k0 + w],
                              start=True, stop=False)
                    ins = pe.matmul(out, (q2b if fox else q2)[:, par, m, t * P:(t + 1) * P],
                                    klo[:, par, m, k0:k0 + w], start=False, stop=True)
                    if last:
                        ins = pe.matmul(out[:, w - P:w], ident_r[:], mask_r[:], start=False, stop=True,
                                        skip_group_check=True)
                ins.then_inc(s_s, 1)

            def weights(turn, s, m):
                n0, it = turn.w[s, m], turn.it
                if fox:
                    pe.wait_ge(s_e, it * 32 + (2 * s + m + 3))
                else:
                    pe.wait_ge(s_w, it * (2 * QT) + (s + 1))
                for x, (k0, cnt) in enumerate(groups[s]):
                    b = (n0 + x) % 2
                    pe.wait_ge(s_te[b], turn.fills(n0 + x) + 1)
                    for y in range(cnt):
                        ins = pe.transpose(T[b][:, y * P:(y + 1) * P], pr[:, s % 2, m, (k0 + y) * P:(k0 + y + 1) * P],
                                           core.ident)
                    ins.then_inc(s_t, 1)

            def values(turn, s):
                t, par, it = tiles[s], s // QT, turn.it
                pe.wait_ge(s_oe, it * (2 * QT) + (s + 1))
                if s % QT == 0:
                    pe.wait_ge(s_vd[par], it * 16 + 16)
                units = [turn.w[s, m] + x for m in range(NM) for x in range(len(groups[s]))]
                for n in units[-2:]:
                    pe.wait_ge(s_te[n % 2], turn.fills(n) + 2)
                for k in range(t + 1):
                    for m in range(NM):
                        w = wT[:, s % 2, m, k * P:(k + 1) * P]
                        if fox:
                            ins = pe.matmul(O[64 * m:64 * m + 64, 0, :], vr[:, par, k, 64 * m:64 * m + 64], w,
                                            start=k == 0, stop=k == t)
                        else:
                            ins = pe.matmul(O[:, 0, :], w, vr[:, par, k, :], start=k == 0, stop=k == t)
                ins.then_inc(s_pv, 1)

            def rows_back(turn, s):
                pe.wait_ge(s_ot, turn.it * (2 * QT) + (s + 1))
                pe.transpose(O[:, 1, :], oT[:], core.ident).then_inc(s_ob, 1)

            def run(turn):
                for s in range(2 * QT):
                    for m in range(2):
                        if turn.has_next(s):
                            scores(turn, s + 1, m)
                        for j in turn.kq_of(s, m):
                            kq_unit(j, turn.it * 16 + (8 + j), turn.it * 128 + (128 if j < 8 else 192), K)
                        if fox and m == 0 and s >= 2:
                            rows_back(turn, s - 2)
                        if m and s:
                            values(turn, s - 1)
                        if fox or m:
                            weights(turn, s, m if fox else 0)
                if fox:
                    rows_back(turn, 2 * QT - 2)
                values(turn, 2 * QT - 1)
                if fox:
                    rows_back(turn, 2 * QT - 1)

            for j in range(8):
                kq_unit(j, max(j - 1, 0), 64, FIRST[j % 2])
            pe.wait_ge(s_c, 2)
            if fox:
                pe.wait_ge(s_cv, 11)
                pe.wait_ge(s_qb, 4)
                pe.wait_ge(s_ax[0], 32)
            scores(Turn(0), 0, 0)
            scores(Turn(0), 0, 1)
            with pe.Fori(0, TURNS - 1) as it:
                run(Turn(it))
            run(Turn(TURNS - 1, last=True))

        def kq_high(eng, j, done, par, bank=K):
            keys, m, t0 = kq_parts(j)
            eng.wait_ge(s_kt, done + 1)
            if fox and not keys:
                eng.activation(q2b[0:64, par, m, t0 * P:t0 * P + HALF], bank[0:64, :], ACT.Copy,
                               scale=QS).then_inc(s_qb, 1)
            eng.activation((khi if keys else q2)[:, par, m, t0 * P:t0 * P + HALF], bank[:], ACT.Copy,
                           scale=1.0 if keys else QS).then_inc(s_kh, 1)

        def kq_low(eng, j, done, par, bank=K):
            keys, m, t0 = kq_parts(j)
            cols = slice(t0 * P, t0 * P + HALF)
            eng.wait_ge(s_kh, done + 1)
            if keys:
                rows = slice(0, 64) if fox else slice(0, P)
                ins = eng.tensor_tensor(klo[rows, par, m, cols], bank[rows, :], khi[rows, par, m, cols].bitcast(F32),
                                        ALU.subtract)
            else:
                q = q2[64:P, par, m, cols]
                ins = eng.scalar_tensor_tensor(q, bank[64:P, :], QS, q.bitcast(F32), ALU.mult, ALU.subtract)
            ins.then_inc(s_ke, 1)

        def weights_out(eng, copy, turn, s, m, mine):
            for x, (k0, cnt) in enumerate(groups[s]):
                n = turn.w[s, m] + x
                if mine(n):
                    eng.wait_ge(s_t, turn.units(n) + 1)
                    copy(wT[:, s % 2, m, k0 * P:(k0 + cnt) * P], T[n % 2][:, 0:cnt * P]).then_inc(s_te[n % 2], 1)

        @block.scalar
        def _(act):
            def exp(turn, s, m):
                n, col = (tiles[s % (2 * QT)] + 1) * P, 2 * (s % QT) + m
                act.wait_ge(s_nm, turn.it * 32 + (2 * s + m + 1))
                act.activation(pr[:, s % 2, m, 0:n], S[m][:].rearrange("p a b -> p (a b)")[:, 0:n], ACT.Exp,
                               bias=nmx[:, col:col + 1], accum_out=dsum[:, col:col + 1]).then_inc(s_e, 1)

            def copy(o, x):
                return act.activation(o, x, ACT.Copy)

            def outputs_T(turn, s):
                act.wait_ge(s_pv, turn.it * (2 * QT) + (s + 1))
                copy(oT[:], O[:, 0, :]).then_inc(s_ot, 1)

            def run(turn):
                for s in range(2 * QT):
                    for m in range(2):
                        for j in turn.kq_of(s, m):
                            kq_high(act, j, turn.it * 16 + (8 + j), (j // 8 + 1) % 2)
                        if fox and m and s:
                            outputs_T(turn, s - 1)
                        if turn.has_next(s):
                            exp(turn, s + 1, m)
                        if fox or m:
                            weights_out(act, copy, turn, s, m if fox else 0, lambda n: not fox or n % 2 == 0)
                if fox:
                    outputs_T(turn, 2 * QT - 1)

            for j in range(8):
                kq_high(act, j, j, 0, FIRST[j % 2])
            exp(Turn(0), 0, 0)
            exp(Turn(0), 0, 1)
            with act.Fori(0, TURNS - 1) as it:
                run(Turn(it))
            run(Turn(TURNS - 1, last=True))

        @block.vector
        def _(dve):
            if fox:
                k_one, q_one = (core.const[64:P, C_AUX + x:C_AUX + x + 1].to_broadcast([64, 4 * SEQ]) for x in range(2))
                dve.tensor_copy(klo[64:P].rearrange("p a b c -> p (a b c)"), k_one).then_inc(s_c, 1)
                dve.tensor_copy(q2b[64:P].rearrange("p a b c -> p (a b c)"), q_one).then_inc(s_c, 1)

            def cumulate():
                zero = pr[0:16, 0, 0, :]
                dve.memset(zero, 0.0).then_inc(s_cv, 1)
                dve.wait_ge(s_cv, 2)
                dve.tensor_copy(c[:], S[0][0:16, :, :].rearrange("p a b -> p (a b)")).then_inc(s_cv, 1)
                dve.wait_ge(s_cv, 3)
                dve.tensor_tensor_scan(c[:], c[:], zero, 0.0, ALU.add, ALU.add).then_inc(s_cv, 1)
                dve.wait_ge(s_cv, 4)
                dve.tensor_copy(cp[:, 2, :], c[:]).then_inc(s_cv, 1)
                dve.wait_ge(s_cv, 5)
                dve.tensor_tensor(cp[:, 3, :], c[:], cp[:, 2, :].bitcast(F32), ALU.subtract).then_inc(s_cv, 1)
                dve.wait_ge(s_cv, 6)
                dve.tensor_scalar(cp[:, 0, :], cp[:, 2, :].bitcast(F32), -1.0, None, ALU.mult).then_inc(s_cv, 1)
                dve.tensor_scalar(cp[:, 1, :], cp[:, 3, :].bitcast(F32), -1.0, None, ALU.mult).then_inc(s_cv, 1)
                dve.wait_ge(s_cv, 8)
                dve.wait_ge(s_c, 4)
                dve.memset(zero, 0.0).then_inc(s_cv, 3)

            def maximum(turn, s, m):
                n, col = (tiles[s % (2 * QT)] + 1) * P, 2 * (s % QT) + m
                dve.wait_ge(s_s, turn.it * 32 + (2 * s + m + 1))
                dve.tensor_reduce(nmx[:, col:col + 1], S[m][:].rearrange("p a b -> p (a b)")[:, 0:n],
                                  AX, ALU.max, negate=True).then_inc(s_nm, 1)

            def combine(turn, s):
                d = s % QT
                dve.wait_ge(s_e, turn.it * 32 + (2 * s + 4))
                dve.reciprocal(rinv[:, 2 * d:2 * d + 2], dsum[:, 2 * d:2 * d + 2]).then_inc(s_f, 1)
                if fox:
                    return
                n = (tiles[s] + 1) * P
                dve.wait_ge(s_f, turn.it * (4 * QT) + (2 * s + 1))
                dve.tensor_scalar(fac[:, d:d + 1], dsum[:, 2 * d:2 * d + 1], rinv[:, 2 * d + 1:2 * d + 2],
                                  core.neglam[:, 0:1], ALU.mult, ALU.mult).then_inc(s_f, 1)
                dve.wait_ge(s_f, turn.it * (4 * QT) + (2 * s + 2))
                dve.scalar_tensor_tensor(pr[:, s % 2, 0, 0:n], pr[:, s % 2, 1, 0:n], fac[:, d:d + 1],
                                         pr[:, s % 2, 0, 0:n], ALU.mult, ALU.add).then_inc(s_w, 1)

            def outputs(turn, s):
                t, d, par, it = tiles[s], s % QT, s // QT, turn.it
                dve.wait_ge(s_ob if fox else s_pv, it * (2 * QT) + (s + 1))
                if d == 0:
                    dve.wait_ge(s_of, it * 2 + (par + 1))
                if fox:
                    dve.wait_ge(s_f, it * (2 * QT) + (s + 1))
                    dve.tensor_tensor(ost[:, par, t, :].rearrange("p (s e) -> p s e", s=2),
                                      O[:, 1, :].rearrange("p (s e) -> p s e", s=2),
                                      rinv[:, 2 * d:2 * d + 2].unsqueeze(2).to_broadcast([P, 2, 64]),
                                      ALU.mult).then_inc(s_oe, 1)
                else:
                    dve.tensor_scalar(ost[:, par, t, :], O[:, 0, :], rinv[:, 2 * d:2 * d + 1], None,
                                      ALU.mult).then_inc(s_oe, 1)

            def run(turn):
                for s in range(2 * QT):
                    for m in range(2):
                        if turn.has_next(s):
                            maximum(turn, s + 1, m)
                        for j in turn.kq_of(s, m):
                            kq_low(dve, j, turn.it * 16 + (8 + j), (j // 8 + 1) % 2)
                        if fox:
                            weights_out(dve, dve.tensor_copy, turn, s, m, lambda n: n % 2 == 1)
                        if not m:
                            combine(turn, s)
                        if fox and not m and s >= 2:
                            outputs(turn, s - 2)
                    if not fox and s:
                        outputs(turn, s - 1)
                for s in range(2 * QT - (2 if fox else 1), 2 * QT):
                    outputs(turn, s)

            if fox:
                cumulate()
            for j in range(8):
                kq_low(dve, j, j, 0, FIRST[j % 2])
            maximum(Turn(0), 0, 0)
            maximum(Turn(0), 0, 1)
            with dve.Fori(0, TURNS - 1) as it:
                run(Turn(it))
            run(Turn(TURNS - 1, last=True))




def decode_attention(nc, core, tag, fox, q_rows, k_new, v_new, k_cache, v_cache, logf_new, logf_cache, cum, o_rows):
    with ExitStack() as ctx:
        sb, ps, sem = scope(core, ctx, tag)
        KR = VR = 4
        kr, vr = sb("k_tiles", [P, KR, D]), sb("v_tiles", [P, VR, D])
        nr, vn = sb("new_rows", [P, 2, D]), sb("v_new", [P, D])
        nT = sb("new_T", [P, 2, KT, P])
        qbd = sb("q_diag", [P, KT, 32])
        kT = sb("kT", [P, 2, KT, P])
        sc = sb("scores", [P, 2, NKEY])
        pr = sb("probs", [P, 2, NKEY])
        pT = sb("probs_T", [P, CT + 1, 2, P])
        obd = sb("o_diag", [P, 2, P])
        oo = sb("o_out", [16, D])
        mx = sb("max", [P, 2, 5])
        nmx, ds, coef = sb("neg_max", [P, 2]), sb("sum", [P, 2]), sb("coef", [P, 2])
        KB = [ps(f"kb{x}", [P, 4, P]) for x in range(2)]
        SB = [ps(f"sb{x}", [P, 2, 2, P]) for x in range(2)]
        PB = [ps(f"pb{x}", [P, 2, 2, P]) for x in range(2)]
        OB = [ps(f"ob{x}", [P, P]) for x in range(2)]
        s_new, s_nt, s_ne, s_qb, s_ktr, s_qk, s_sm, s_mx, s_nm, s_e, s_cf, s_ptr, s_pv, s_oe, s_sel, s_st = (
            sem(x) for x in ("new", "nt", "ne", "qb", "ktr", "qk", "sm", "mx", "nm", "exp", "cf", "ptr", "pv", "oe",
                             "sel", "st"))
        s_kd, s_vd = [sem(f"kd{x}") for x in range(KR)], [sem(f"vd{x}") for x in range(VR)]
        s_ke, s_se, s_pe = ([sem(f"{n}{x}") for x in range(2)] for n in ("ke", "se", "pe"))
        if fox:
            lf = sb("logf", [P, CT, P])
            lfn, lbd = sb("logf_new", [P, 16]), sb("logf_diag", [P, P])
            ca = sb("cum", [P, NKEY])
            zero = sb("zeros", [P, PAST])
            cn = sb("cum_new", [P, NQ])
            ch = sb("bias_parts", [P, 2, NKEY], F32R)
            cb = sb("key_bias", [32, NB, NKEY], F32R)
            hs, hsr = sb("head_rows", [32, 2, P]), sb("head_sel", [32, 2, P], F32R)
            s_lf, s_ct, s_cv, s_cd = sem("lf"), sem("ct"), sem("cv"), sem("cd")
        block = ctx.enter_context(nc.Block())
        W0 = C_WIN[1] if fox else C_WIN[0]
        SU, PU = (3, 2), (4, 3)
        VALUES = [[], [], [], [0], [1, 2], [3, 4], [5, 6], [7, 8], []]
        PROBS = [[], [], [0], [1], [2], [3], [4], [], []]

        @block.sync
        def _(sp):
            def load_k(b, t):
                sp.wait_ge(s_ktr, b * 16 + 2 * t + 2)
                sp.dma_start(kr[:, t % KR, :], k_cache[bass.ds(b * CT + t, 1)].rearrange("a p n -> (a p) n"))\
                    .then_inc(s_kd[t % KR], 16)

            def load_v(b, t):
                sp.wait_ge(s_pv, b * (CT + 1) + (t + 2 if t >= VR else t + 1))
                sp.dma_start(vr[:, t % VR, :], v_cache[bass.ds(b * CT + t, 1)].rearrange("a p n -> (a p) n"))\
                    .then_inc(s_vd[t % VR], 16)

            sp.dma_start(nr[:, 0, :], q_rows).then_inc(s_new, 16)
            sp.dma_start(nr[:, 1, :], k_new).then_inc(s_new, 16)
            if fox:
                sp.dma_start(lfn[:], logf_new).then_inc(s_lf, 16)
                for x in range(2):
                    sp.dma_start(hs[16 * x:16 * x + 16].rearrange("a g p -> a (g p)"),
                                 core.hsel).then_inc(s_lf, 16)
                for b in range(NB):
                    sp.dma_start(lf[:, :, b * 16:(b + 1) * 16],
                                 logf_cache[b].rearrange("(t p) h -> p t h", p=P)).then_inc(s_lf, 16)
                for t in range(KR):
                    load_k(0, t)
                sp.wait_ge(s_cv, 11)
                sp.dma_start(cum.rearrange("a p k -> p a k"), ch[:].bitcast(F32)).then_inc(s_cd, 16)
                sp.wait_ge(s_cd, 16)
                for x in range(2):
                    sp.dma_start(cb[16 * x:16 * x + 16].bitcast(F32),
                                 cum[x].rearrange("(b h) k -> h b k", h=16)).then_inc(s_cd, 16)

            for t in range(KR if fox else 0, CT):
                load_k(0, t)
            with sp.Fori(1, NB) as b:
                for t in range(CT + 2):
                    if t < CT:
                        load_k(b, t)
                    if t >= 2:
                        load_v(b - 1, t - 2)
            for t in range(CT):
                load_v(NB - 1, t)
            sp.wait_ge(s_st, 16 * NB + 16)

        @block.gpsimd
        def _(pool):
            pool.memset(qbd[:], 0.0).then_inc(s_qb, 1)
            pool.wait_ge(s_qb, 1)
            pool.wait_ge(s_ne, 4)
            with pool.Fori(0, NB) as b:
                pool.wait_ge(s_sm, b + 1)
                for m in range(2):
                    rows = slice(64 * m, 64 * m + 64)
                    pool.tensor_copy(qbd[rows, :, 16 * m:16 * m + 16], nT[rows, 0, :, bass.ts(b, NQ)]).then_inc(s_qb, 1)

        @block.tensor
        def _(pe):
            for s, n in ((s_ktr, 2 * KR), (s_qk, 2), (s_pv, VR + 1), (s_sm, 1), (s_e, 1),
                         (s_sel, 1), (s_ptr, 1), (s_cf, 1), (s_ke[0], 1), (s_ke[1], 1), (s_se[0], 1),
                         (s_se[1], 1), (s_pe[0], 1), (s_pe[1], 1), (s_oe, 1)):
                pe.sem_inc(s, n)
            pe.wait_ge(s_new, 32)
            for x in range(2):
                for g in range(2):
                    if x:
                        pe.wait_ge(s_ne, g + 1)
                    for c_ in range(4):
                        ins = pe.transpose(KB[g][:, c_, :], nr[:, x, (4 * g + c_) * P:(4 * g + c_ + 1) * P], core.ident)
                    ins.then_inc(s_nt, 1)
            if fox:
                pe.wait_ge(s_lf, 176)
                for t in range(CT):
                    ins = pe.transpose(SB[t // 4][:].rearrange("p a b c -> p (a b c)")[:, (t % 4) * P:(t % 4 + 1) * P],
                                       lf[:, t, :], core.ident)
                ins.then_inc(s_ct, 1)
                pe.wait_ge(s_cv, 2)
                pe.matmul(OB[0][:, 0:NQ], lbd[:], core.const[:, C_FRAME:C_FRAME + NQ],
                          start=True, stop=True).then_inc(s_ct, 1)
                pe.wait_ge(s_cd, 48)
                pe.wait_ge(s_cv, 11)
            pe.wait_ge(s_ne, 4)

            def keys(b, t):
                pe.wait_ge(s_kd[t % KR], b * 32 + 16 * (t // KR + 1))
                for g in range(2):
                    pe.wait_ge(s_ke[g], b * CT + t + 1)
                    for c_ in range(4):
                        ins = pe.transpose(KB[g][:, c_, :], kr[:, t % KR, (4 * g + c_) * P:(4 * g + c_ + 1) * P],
                                           core.ident)
                    ins.then_inc(s_ktr, 1)

            def scores(b, t):
                pair = t // 2
                bank, use = pair % 2, pair // 2
                if t % 2 == 0:
                    pe.wait_ge(s_se[bank], b * SU[bank] + use + 1)
                if t == 0:
                    pe.wait_ge(s_qb, b * 2 + 3)
                if t < CT:
                    for g in range(2):
                        pe.wait_ge(s_ke[g], b * CT + t + 2)
                for g in range(2):
                    out = SB[bank][:, t % 2, g, :]
                    for j in range(4):
                        k = kT[:, t % 2, 4 * g + j, :] if t < CT else nT[:, 1, 4 * g + j, :]
                        ins = pe.matmul(out[32 * j:32 * j + 32, :], qbd[:, 4 * g + j, :], k,
                                        start=True, stop=not fox and t < CT, skip_group_check=True)
                    if t == CT:
                        ins = pe.matmul(out, core.ident, core.const[:, bass.ds(b * -16 + (W0 + 112), P)],
                                        start=False, stop=not fox, skip_group_check=True)
                    if fox:
                        ins = pe.matmul(out, hsr[:, g, :], cb[:, bass.ds(b, 1), t * P:(t + 1) * P].rearrange(
                            "h a k -> h (a k)"), start=False, stop=True, skip_group_check=True)
                ins.then_inc(s_qk if t < CT else s_sm, 1)

            def probs(b, pair):
                bank, use = pair % 2, pair // 2
                pe.wait_ge(s_pe[bank], b * PU[bank] + use + 1)
                if pair == 0:
                    pe.wait_ge(s_e, b * 2 + 3)
                for t in range(2 * pair, min(2 * pair + 2, CT + 1)):
                    for g in range(2):
                        ins = pe.transpose(PB[bank][:, t % 2, g, :], pr[:, g, t * P:(t + 1) * P], core.ident)
                ins.then_inc(s_ptr, 1)

            def values(b, t):
                pair = t // 2
                if t == 0:
                    pe.wait_ge(s_oe, b + 1)
                    pe.wait_ge(s_st, 16)
                if t % 2 == 0:
                    pe.wait_ge(s_pe[pair % 2], b * PU[pair % 2] + pair // 2 + 2)
                if t < CT:
                    pe.wait_ge(s_vd[t % VR], b * 32 + 16 * (t // VR + 1))
                for g in range(2):
                    for j in range(4):
                        cols = slice((4 * g + j) * P, (4 * g + j + 1) * P)
                        v = vr[:, t % VR, cols] if t < CT else vn[:, cols]
                        ins = pe.matmul(OB[g][32 * j:32 * j + 32, :], pT[:, t, g, 32 * j:32 * j + 32], v,
                                        start=t == 0, stop=t == CT)
                ins.then_inc(s_pv, 1)

            def select(b):
                pe.wait_ge(s_oe, b + 2)
                for g in range(2):
                    out = PB[g][:].rearrange("p a b c -> p (a b c)")
                    pe.wait_ge(s_pe[g], b * PU[g] + PU[g])
                    for j in range(4):
                        if fox:
                            for s in range(2):
                                c0 = C_SELB + (j * 2 + s) * 16
                                ins = pe.matmul(out[0:16, j * P + 64 * s:j * P + 64 * s + 64],
                                                core.const[:, c0:c0 + 16], obd[:, g, 64 * s:64 * s + 64],
                                                start=True, stop=True)
                        else:
                            c0 = C_SELA + j * 16
                            ins = pe.matmul(out[0:16, j * P:(j + 1) * P], core.const[:, c0:c0 + 16], obd[:, g, :],
                                            start=True, stop=True)
                    ins.then_inc(s_sel, 1)

            def stream(bs, bv):
                if bs is not None:
                    keys(bs, 0)
                for t in range(CT + 1):
                    if bs is not None:
                        if t + 1 < CT:
                            keys(bs, t + 1)
                        scores(bs, t)
                    if bv is not None:
                        for v in VALUES[t]:
                            values(bv, v)
                        for pair in PROBS[t]:
                            probs(bv, pair)
                if bv is not None:
                    select(bv)

            stream(0, None)
            with pe.Fori(1, NB) as b:
                stream(b, b - 1)
            stream(None, NB - 1)

        def partial_maximum(b, pair):
            x, use, n = pair % 2, pair // 2, 2 if pair < CT // 2 else 1
            nc.vector.wait_ge(s_se[x], b * SU[x] + use + 2)
            nc.vector.tensor_reduce(mx[:, :, pair:pair + 1], sc[:, :, 2 * pair * P:(2 * pair + n) * P], AX,
                                    ALU.max).then_inc(s_mx, 1)

        def evacuation(eng, copy, half):
            other = 1 - half

            def keys(b, t):
                eng.wait_ge(s_ktr, b * 16 + (2 * t + half + 1 + 2 * KR))
                eng.wait_ge(s_qk, b * CT + t + 1)
                copy(kT[:, t % 2, 4 * half:4 * half + 4, :], KB[half][:]).then_inc(s_ke[half], 1)

            def scores(b, pair):
                if pair % 2 != half:
                    return
                n = 2 if pair < CT // 2 else 1
                if n == 2:
                    eng.wait_ge(s_qk, b * CT + 2 * pair + 2 + 2)
                else:
                    eng.wait_ge(s_sm, b + 2)
                if pair < 2:
                    eng.wait_ge(s_e, b * 2 + 1)
                dst = sc[:, :, 2 * pair * P:(2 * pair + n) * P].rearrange("p g (t k) -> p t g k", t=n)
                for x in range(n):
                    ins = copy(dst[:, x], SB[half][:, x])
                ins.then_inc(s_se[half], 1)

            def probs(b, pair):
                if pair % 2 != other:
                    return
                n = 2 if pair < CT // 2 else 1
                eng.wait_ge(s_ptr, b * 5 + pair + 2)
                if pair < 2:
                    eng.wait_ge(s_pv, b * (CT + 1) + VR + 1)
                copy(pT[:, 2 * pair:2 * pair + n], PB[other][:, 0:n]).then_inc(s_pe[other], 1)

            def selected(b):
                eng.wait_ge(s_sel, b * 2 + other + 2)
                eng.wait_ge(s_st, b * 16 + 16)
                copy(oo[:, other * HALF:(other + 1) * HALF],
                     PB[other][:].rearrange("p a b c -> p (a b c)")[0:16, :]).then_inc(s_pe[other], 1)

            def stream(bs, bv, softmax, outputs=None, maximum=None):
                if bs is not None:
                    keys(bs, 0)
                for t in range(CT + 1):
                    if bv is not None and t in softmax:
                        softmax[t](bv)
                    if bs is not None:
                        if t + 1 < CT:
                            keys(bs, t + 1)
                        if t % 2 == 1 or t == CT:
                            scores(bs, t // 2)
                            if half:
                                partial_maximum(bs, t // 2)
                    if bv is not None:
                        for pair in PROBS[t]:
                            probs(bv, pair)
                if bs is not None and maximum:
                    maximum(bs)
                if bv is not None:
                    if outputs:
                        outputs(bv)
                    selected(bv)

            return stream

        @block.scalar
        def _(act):
            def copy(o, x):
                return act.activation(o, x, ACT.Copy)

            def outputs(b):
                act.wait_ge(s_pv, b * (CT + 1) + (CT + 2 + VR))
                act.wait_ge(s_cf, b * 2 + 3)
                act.wait_ge(s_sel, b * 2 + 1)
                for g in range(2):
                    ins = act.activation(obd[:, g, :], OB[g][:], ACT.Copy, scale=coef[:, g:g + 1])
                ins.then_inc(s_oe, 1)

            def exp(b, g):
                if g == 0:
                    act.wait_ge(s_nm, b + 1)
                    act.wait_ge(s_ptr, b * 5 + 1)
                    act.wait_ge(s_cf, b * 2 + 1)
                act.activation(pr[:, g, :], sc[:, g, :], ACT.Exp, bias=nmx[:, g:g + 1],
                               accum_out=ds[:, g:g + 1]).then_inc(s_e, 1)

            act.dma_start(vn[:], v_new).then_inc(s_st, 16)
            for x in range(2):
                for g in range(2):
                    act.wait_ge(s_nt, 2 * x + g + 1)
                    act.activation(nT[:, x, 4 * g:4 * g + 4, :], KB[g][:], ACT.Copy,
                                   scale=1.0 if x else QS).then_inc(s_ne, 1)
            stream = evacuation(act, copy, 0)

            def store(b):
                for g in range(2):
                    act.wait_ge(s_pe[g], b * PU[g] + PU[g] + 1)
                act.dma_start(o_rows[bass.ds(b * NQ + SEQ, NQ), :], oo[:]).then_inc(s_st, 16)

            softmax = {0: lambda b: exp(b, 0), 1: lambda b: exp(b, 1)}
            stream(0, None, softmax, outputs)
            with act.Fori(1, NB) as b:
                stream(b, b - 1, softmax, outputs)
                store(b - 1)
            stream(None, NB - 1, softmax, outputs)
            store(NB - 1)

        @block.vector
        def _(dve):
            if fox:
                dve.memset(zero[:], 0.0).then_inc(s_cv, 1)
                dve.wait_ge(s_lf, 176)
                dve.tensor_tensor(lbd[:].rearrange("p (b h) -> p b h", h=16),
                                  lfn[:].unsqueeze(1).to_broadcast([P, NB, 16]),
                                  core.const[:, C_STREAM:C_STREAM + NB].unsqueeze(2).to_broadcast([P, NB, 16]),
                                  ALU.mult).then_inc(s_cv, 1)
                dve.wait_ge(s_ct, 1)
                for x in range(2):
                    dve.wait_ge(s_cv, 2 + x)
                    src = SB[x][:].rearrange("p a b c -> p (a b c)")
                    dve.tensor_tensor_scan(ca[:, x * HALF:(x + 1) * HALF], src, zero[:, 0:HALF],
                                           ca[:, HALF - 1:HALF] if x else 0.0, ALU.add, ALU.add).then_inc(s_cv, 1)
                dve.wait_ge(s_ct, 2)
                dve.wait_ge(s_cv, 4)
                dve.tensor_tensor_scan(cn[:], OB[0][:, 0:NQ], zero[:, 0:NQ], 0.0, ALU.add, ALU.add).then_inc(s_cv, 1)
                dve.wait_ge(s_cv, 5)
                dve.tensor_copy(coef[:, 0:1], ca[:, PAST - 1:PAST]).then_inc(s_cv, 1)
                dve.wait_ge(s_cv, 6)
                dve.tensor_scalar(ca[:, 0:PAST], ca[:, 0:PAST], coef[:, 0:1], -1.0, ALU.subtract,
                                  ALU.mult).then_inc(s_cv, 1)
                dve.wait_ge(s_cv, 7)
                dve.scalar_tensor_tensor(ca[:, PAST:NKEY].rearrange("p (b q) -> p b q", q=NQ),
                                         cn[:].unsqueeze(1).to_broadcast([P, NB, NQ]), -1.0,
                                         core.const[:, C_STREAM:C_STREAM + NB].unsqueeze(2).to_broadcast([P, NB, NQ]),
                                         ALU.mult, ALU.mult).then_inc(s_cv, 1)
                dve.wait_ge(s_cv, 8)
                dve.tensor_copy(ch[:, 0, :], ca[:]).then_inc(s_cv, 1)
                dve.wait_ge(s_cv, 9)
                dve.tensor_tensor(ch[:, 1, :], ca[:], ch[:, 0, :].bitcast(F32), ALU.subtract).then_inc(s_cv, 1)
                dve.tensor_copy(hsr[:], hs[:]).then_inc(s_cv, 1)

            def maximum(b):
                dve.wait_ge(s_mx, b * 5 + 5)
                dve.tensor_reduce(nmx[:], mx[:], AX, ALU.max, negate=True).then_inc(s_nm, 1)

            def coefficients(b):
                dve.wait_ge(s_e, b * 2 + 3)
                dve.wait_ge(s_oe, b + 1)
                dve.reciprocal(coef[:], ds[:]).then_inc(s_cf, 2 if fox else 1)
                if not fox:
                    dve.wait_ge(s_cf, b * 2 + 2)
                    dve.tensor_scalar(coef[:], coef[:], core.lamcol[:, 0:1], None, ALU.mult).then_inc(s_cf, 1)

            stream = evacuation(dve, dve.tensor_copy, 1)
            stream(0, None, {2: coefficients}, None, maximum)
            with dve.Fori(1, NB) as b:
                stream(b, b - 1, {2: coefficients}, None, maximum)
            stream(None, NB - 1, {2: coefficients}, None)




def stream_step(nc, a, o):
    xp = a["x_prompt"].rearrange("a s d -> (a s) d")
    xs = a["x_sample"].rearrange("b s d -> (b s) d")
    yp = o["y_prompt"].rearrange("a s d -> (a s) d")
    ys = o["y_sample"].rearrange("b s d -> (b s) d")
    kv = {}
    for n in ("ak_p", "av_p", "ak_s", "av_s"):
        kv[n] = o[n].rearrange("n b s h e -> (n b s) (h e)")
    for n in ("bk_p", "bv_p", "bk_s", "bv_s"):
        kv[n] = o[n].rearrange("b s h e -> (b s) (h e)")
    fp, fs = (o[n].rearrange("b s h -> (b s) h") for n in ("bf_p", "bf_s"))
    cak = a["cache_a_k"].rearrange("n b (t p) h e -> (n b t) p (h e)", p=P)
    cav = a["cache_a_v"].rearrange("n b (t p) h e -> (n b t) p (h e)", p=P)
    cbk = a["cache_b_k"].rearrange("b (t p) h e -> (b t) p (h e)", p=P)
    cbv = a["cache_b_v"].rearrange("b (t p) h e -> (b t) p (h e)", p=P)
    q = nc.dram_tensor("q_scratch", [ROWS, D], F32).ap()
    ao = nc.dram_tensor("o_scratch", [ROWS, D], F32).ap()
    cum = nc.dram_tensor("cum_scratch", [2, P, NKEY], F32).ap()
    cum_parts = nc.dram_tensor("cum_parts_scratch", [16, 4, SEQ], F32).ap()
    qd = (q[0:SEQ, :], q[SEQ:ROWS, :])
    with ExitStack() as ctx:
        core = Core(nc, ctx, a["head_sel"], xp, xs)
        start_phase(nc, core, a["const"],
                    [a[n] for n in ("lambda_q1", "lambda_k1", "lambda_q2", "lambda_k2")])
        wa = a["w_qkv_a"].rearrange("n d e -> (n d) e")
        with ExitStack() as rows:
            core.normed_rows(rows, "a")
            dense_phase(nc, core, "qkv", "rms", a["norm_attn"][0, :], None,
                        [(wa, c, "rope", (*qd, c)) for c in (0, HALF)]
                        + [(wa, D + c, "rope", (kv["ak_p"], kv["ak_s"], c)) for c in (0, HALF)]
                        + [(wa, 2 * D + c, "store", (kv["av_p"], kv["av_s"], c)) for c in (0, HALF)])
        prompt_attention(nc, core, "pa", False, q, kv["ak_p"], kv["av_p"], None, None, ao)
        decode_attention(nc, core, "da", False, q[SEQ:ROWS, :], kv["ak_s"], kv["av_s"], cak, cav, None, None, None, ao)
        with ExitStack() as rows:
            core.normed_rows(rows, "b")
            dense_phase(nc, core, "oa", "head", a["subln_a"][0, :], ao,
                        [(a["w_o_a"].rearrange("n d e -> (n d) e"), c, "add", c) for c in (0, HALF)],
                        following=a["norm_mlp"][0, :])
            mlp_phase(nc, core, "m0", a["w_up"][0], a["w_down"][0], a["norm_kv"])
            core.clear_semaphores()
            w = a["w_kvf"]
            dense_phase(nc, core, "kv", None, None, None,
                        [(w, c, "store", (kv["bk_p"], kv["bk_s"], c)) for c in (0, HALF)]
                        + [(w, D + c, "store", (kv["bv_p"], kv["bv_s"], c)) for c in (0, HALF)]
                        + [(a["w_q_b"].rearrange("n d e -> (n d) e"), c, "store", (*qd, c)) for c in (0, HALF)],
                        forget=(w[:, 2 * D:2 * D + 16], a["b_f"], fp, fs), following=a["norm_attn"][1, :], swap=3)
        prompt_attention(nc, core, "pb", True, q, kv["bk_p"], kv["bv_p"], fp, cum_parts, ao)
        decode_attention(nc, core, "db", True, q[SEQ:ROWS, :], kv["bk_s"], kv["bv_s"], cbk, cbv, fs,
                         a["cache_b_logf"], cum, ao)
        with ExitStack() as rows:
            core.normed_rows(rows, "c")
            dense_phase(nc, core, "ob", "plain", None, ao,
                        [(a["w_o_b"].rearrange("n d e -> (n d) e"), c, "add", c) for c in (0, HALF)],
                        following=a["norm_mlp"][1, :])
            mlp_phase(nc, core, "m1", a["w_up"][1], a["w_down"][1], a["norm_final"],
                      lambda r: rows_of(yp, ys, r))
        core.clear_semaphores()


_INS = ["x_prompt", "x_sample", "cache_a_k", "cache_a_v", "cache_b_k", "cache_b_v", "cache_b_logf", "norm_attn",
        "norm_mlp", "w_qkv_a", "lambda_q1", "lambda_k1", "lambda_q2", "lambda_k2", "subln_a", "w_o_a", "norm_kv",
        "w_kvf", "b_f", "w_q_b", "w_o_b", "w_up", "w_down", "norm_final"]
_OUTS = {"y_prompt": (1, SEQ, D), "y_sample": (NB, NQ, D), "ak_p": (1, 1, SEQ, 16, 64), "av_p": (1, 1, SEQ, 8, 128),
         "bk_p": (1, SEQ, 16, 64), "bv_p": (1, SEQ, 16, 64), "bf_p": (1, SEQ, 16),
         "ak_s": (1, NB, NQ, 16, 64), "av_s": (1, NB, NQ, 8, 128),
         "bk_s": (NB, NQ, 16, 64), "bv_s": (NB, NQ, 16, 64), "bf_s": (NB, NQ, 16)}


def kernel(**inputs):
    import numpy as _np
    import concourse.bacc as _bacc
    from concourse import mybir as _mybir
    from concourse.bass_utils import run_bass_kernel_spmd as _run

    nc = _bacc.Bacc("TRN2", target_bir_lowering=False, num_devices=1)
    table, head_sel = constant_tables()
    arrays, a, o = {}, {}, {}
    for name, x in [(n, inputs[n]) for n in _INS] + [("const", table), ("head_sel", head_sel)]:
        x = _np.ascontiguousarray(x)
        arrays[f"in_{name}"] = x
        a[name] = nc.dram_tensor(f"in_{name}", x.shape, _mybir.dt.from_np(x.dtype), kind="ExternalInput").ap()
    for name, shape in _OUTS.items():
        o[name] = nc.dram_tensor(f"out_{name}", shape, F32, kind="ExternalOutput").ap()
    stream_step(nc, a, o)
    r = _run(nc, [arrays], core_ids=[0])
    return tuple(r.results[0][f"out_{name}"] for name in _OUTS)
```
